# Optimizing a Trainium2 kernel written in Bass

```python
import math
import jax, jax.numpy as jnp
from jax import lax
import numpy as np

D_MODEL = 1024
BATCH = 1
SEQ = 1024
DEPTH = 2

GRID_W = 64
CTX_LEN = 256
EPS = 1e-6
Q_BLOCK = 128
ROPE_THETA = 10000.0
F32 = jnp.float32

POOL_WINDOWS = (2, 4, 8, 16)
POOL_GROUP = D_MODEL // 8
POOL_WIDTH = POOL_GROUP * len(POOL_WINDOWS)
DIFF_HEADS = 4
DIFF_HEAD_DIM = 64
DIFF_V_DIM = 2 * DIFF_HEAD_DIM
DIFF_QK_WIDTH = DIFF_HEADS * 2 * DIFF_HEAD_DIM
DIFF_WIDTH = DIFF_HEADS * DIFF_V_DIM
AB_IN_WIDTH = POOL_WIDTH + 2 * DIFF_QK_WIDTH + DIFF_WIDTH
AB_OUT_WIDTH = POOL_WIDTH + DIFF_WIDTH
MLA_HEADS = 16
MLA_NOPE = 64
MLA_ROPE = 32
MLA_QK = MLA_NOPE + MLA_ROPE
MLA_V = 64
MLA_Q_RANK = 384
MLA_KV_RANK = 256
FFN_HIDDEN = -(-(8 * D_MODEL) // (3 * 256)) * 256
N_AB = (DEPTH + 1) // 2
N_MLA = DEPTH // 2

kernel_name = "hybrid_pool_diffattn_mla_prefix_dit"

def rmsnorm(x, g):
    xf = x.astype(F32)
    y = xf * lax.rsqrt(jnp.mean(xf * xf, axis=-1, keepdims=True) + EPS)
    return (y * g.astype(F32)).astype(x.dtype)

def adaln(cond, w, b):
    m = jax.nn.silu(cond) @ w + b
    return jnp.split(m, 6, axis=-1)

def modulate(h, shift, scale):
    return h * (1.0 + scale) + shift

def axial_rope(rows, rot_dim):
    n_freq = rot_dim // 4
    freqs = ROPE_THETA ** (-jnp.arange(n_freq, dtype=F32) / n_freq)
    row = jnp.repeat(jnp.arange(rows, dtype=F32), GRID_W)
    col = jnp.tile(jnp.arange(GRID_W, dtype=F32), rows)
    ang = jnp.concatenate([row[:, None] * freqs, col[:, None] * freqs], axis=-1)
    return jnp.cos(ang), jnp.sin(ang)

def apply_rope(x, cos, sin):
    shp = (cos.shape[0],) + (1,) * (x.ndim - 3) + (cos.shape[1],)
    cs, sn = cos.reshape(shp), sin.reshape(shp)
    xf = x.astype(F32)
    half = x.shape[-1] // 2
    x1, x2 = xf[..., :half], xf[..., half:]
    return jnp.concatenate([x1 * cs - x2 * sn, x1 * sn + x2 * cs], axis=-1).astype(x.dtype)

def sweep_query_blocks(core, q, *kv):
    b, n = q.shape[:2]
    nb = n // Q_BLOCK
    qb = jnp.moveaxis(q.reshape((b, nb, Q_BLOCK) + q.shape[2:]), 1, 0)
    o = lax.map(lambda qi: core(qi, *kv), qb)
    return jnp.moveaxis(o, 0, 1).reshape((b, n) + o.shape[3:])

def attn_core(q, k, v, scale):
    s = jnp.einsum('bqhd,bkhd->bhqk', q.astype(F32), k.astype(F32)) * scale
    p = jax.nn.softmax(s, axis=-1)
    return jnp.einsum('bhqk,bkhe->bqhe', p, v.astype(F32)).astype(v.dtype)

def diff_attn_core(q, k, v, lam, scale):
    s = jnp.einsum('bqhjd,bkhjd->bhjqk', q.astype(F32), k.astype(F32)) * scale
    p = jax.nn.softmax(s, axis=-1)
    pd = p[:, :, 0] - lam * p[:, :, 1]
    return jnp.einsum('bhqk,bkhe->bqhe', pd, v.astype(F32)).astype(v.dtype)

def multiscale_pool(u, pool_w, pool_scale):
    b, n, _ = u.shape
    uf = u.astype(F32)
    cs = jnp.concatenate([jnp.zeros((b, 1, POOL_WIDTH), F32), jnp.cumsum(uf, axis=1)], axis=1)
    t = jnp.arange(n)
    outs = []
    for g, w in enumerate(POOL_WINDOWS):
        lo = jnp.clip(t - w // 2, 0, n)
        hi = jnp.clip(t - w // 2 + w, 0, n)
        sl = slice(g * POOL_GROUP, (g + 1) * POOL_GROUP)
        csg = cs[:, :, sl]
        mean = (csg[:, hi] - csg[:, lo]) / (hi - lo).astype(F32)[None, :, None]
        outs.append(mean - uf[:, :, sl])
    d = jnp.stack(outs, axis=2)
    y = jnp.einsum('blgc,gce->blge', d, pool_w.astype(F32)).reshape(b, n, POOL_WIDTH)
    return (y * pool_scale.astype(F32)).astype(u.dtype)

def pool_diff_mixer(a_lat, a_ctx, w_in, w_out, pool_w, pool_scale, q_g, k_g,
                    lq1, lk1, lq2, lk2, subln_g, lam_init, cos, sin, need_ctx):
    def project(a):
        b, n, _ = a.shape
        p = a @ w_in
        u, q, k, v = jnp.split(p, [POOL_WIDTH, POOL_WIDTH + DIFF_QK_WIDTH,
                                   POOL_WIDTH + 2 * DIFF_QK_WIDTH], axis=-1)
        q = rmsnorm(q.reshape(b, n, DIFF_HEADS, 2, DIFF_HEAD_DIM), q_g)
        k = rmsnorm(k.reshape(b, n, DIFF_HEADS, 2, DIFF_HEAD_DIM), k_g)
        v = v.reshape(b, n, DIFF_HEADS, DIFF_V_DIM)
        return u, q, k, v

    lam = (jnp.exp(jnp.sum(lq1.astype(F32) * lk1.astype(F32)))
           - jnp.exp(jnp.sum(lq2.astype(F32) * lk2.astype(F32))) + lam_init)
    scale = DIFF_HEAD_DIM ** -0.5

    def finish(u, o):
        b, n, _ = u.shape
        o = rmsnorm(o, subln_g) * (1.0 - lam_init)
        mixed = jnp.concatenate([multiscale_pool(u, pool_w, pool_scale),
                                 o.reshape(b, n, DIFF_WIDTH).astype(u.dtype)], axis=-1)
        return mixed @ w_out

    u_l, q_l, k_l, v_l = project(a_lat)
    u_c, q_c, k_c, v_c = project(a_ctx)
    q_l = apply_rope(q_l, cos, sin)
    k_l = apply_rope(k_l, cos, sin)
    k_all = jnp.concatenate([k_c, k_l], axis=1)
    v_all = jnp.concatenate([v_c, v_l], axis=1)
    o_l = sweep_query_blocks(lambda qi, kk, vv: diff_attn_core(qi, kk, vv, lam, scale), q_l, k_all, v_all)
    out_l = finish(u_l, o_l)
    out_c = None
    if need_ctx:
        out_c = finish(u_c, diff_attn_core(q_c, k_c, v_c, lam, scale))
    return out_l, out_c

def mla_mixer(a_lat, a_ctx, w_dq, q_lat_g, w_uq, w_dkv, kv_lat_g, w_ukv,
              q_g, k_g, w_out, cos, sin, need_ctx):
    def keys_values(a):
        b, n, _ = a.shape
        ckv = a @ w_dkv
        c_kv = rmsnorm(ckv[..., :MLA_KV_RANK], kv_lat_g)
        k_rope = ckv[..., MLA_KV_RANK:]
        kvh = (c_kv @ w_ukv).reshape(b, n, MLA_HEADS, MLA_NOPE + MLA_V)
        k = jnp.concatenate([kvh[..., :MLA_NOPE],
                             jnp.broadcast_to(k_rope[:, :, None, :], (b, n, MLA_HEADS, MLA_ROPE))], axis=-1)
        return rmsnorm(k, k_g), kvh[..., MLA_NOPE:]

    def queries(a):
        b, n, _ = a.shape
        q = (rmsnorm(a @ w_dq, q_lat_g) @ w_uq).reshape(b, n, MLA_HEADS, MLA_QK)
        return rmsnorm(q, q_g)

    def rope_tail(t):
        return jnp.concatenate([t[..., :MLA_NOPE], apply_rope(t[..., MLA_NOPE:], cos, sin)], axis=-1)

    scale = MLA_QK ** -0.5
    k_l, v_l = keys_values(a_lat)
    k_c, v_c = keys_values(a_ctx)
    q_l = rope_tail(queries(a_lat))
    k_l = rope_tail(k_l)
    k_all = jnp.concatenate([k_c, k_l], axis=1)
    v_all = jnp.concatenate([v_c, v_l], axis=1)
    b, n, _ = a_lat.shape
    o_l = sweep_query_blocks(lambda qi, kk, vv: attn_core(qi, kk, vv, scale), q_l, k_all, v_all)
    out_l = o_l.reshape(b, n, MLA_HEADS * MLA_V) @ w_out
    out_c = None
    if need_ctx:
        o_c = attn_core(queries(a_ctx), k_c, v_c, scale)
        out_c = o_c.reshape(a_ctx.shape[0], a_ctx.shape[1], MLA_HEADS * MLA_V) @ w_out
    return out_l, out_c

def swiglu(a, wg, wu, wd):
    return (jax.nn.silu(a @ wg) * (a @ wu)) @ wd

def setup_inputs(seed: int = 0) -> dict:
    key = jax.random.key(seed)
    ks = iter(jax.random.split(key, 48))

    def nrm(shape, scale):
        return jax.random.normal(next(ks), shape, F32) * scale

    def gain(shape):
        return 1.0 + 0.1 * jax.random.normal(next(ks), shape, F32)

    D = D_MODEL
    return {
        "x": nrm((BATCH, SEQ, D), 1.0),
        "c": nrm((BATCH, D), 1.0),
        "ctx": nrm((BATCH, CTX_LEN, D), 1.0),
        "c_ctx": nrm((D,), 1.0),
        "mod_w": nrm((DEPTH, D, 6 * D), 0.5 * D ** -0.5),
        "mod_b": nrm((DEPTH, 6 * D), 0.02),
        "norm_mix_g": gain((DEPTH, D)),
        "norm_ffn_g": gain((DEPTH, D)),
        "ffn_w_gate": nrm((DEPTH, D, FFN_HIDDEN), D ** -0.5),
        "ffn_w_up": nrm((DEPTH, D, FFN_HIDDEN), D ** -0.5),
        "ffn_w_down": nrm((DEPTH, FFN_HIDDEN, D), FFN_HIDDEN ** -0.5),
        "ab_w_in": nrm((N_AB, D, AB_IN_WIDTH), D ** -0.5),
        "ab_w_out": nrm((N_AB, AB_OUT_WIDTH, D), AB_OUT_WIDTH ** -0.5),
        "pool_w": nrm((N_AB, len(POOL_WINDOWS), POOL_GROUP, POOL_GROUP), POOL_GROUP ** -0.5),
        "pool_scale": gain((N_AB, POOL_WIDTH)),
        "diff_q_norm_g": gain((N_AB, DIFF_HEAD_DIM)),
        "diff_k_norm_g": gain((N_AB, DIFF_HEAD_DIM)),
        "diff_lam_q1": nrm((N_AB, DIFF_HEAD_DIM), 0.1),
        "diff_lam_k1": nrm((N_AB, DIFF_HEAD_DIM), 0.1),
        "diff_lam_q2": nrm((N_AB, DIFF_HEAD_DIM), 0.1),
        "diff_lam_k2": nrm((N_AB, DIFF_HEAD_DIM), 0.1),
        "diff_subln_g": gain((N_AB, DIFF_V_DIM)),
        "mla_w_dq": nrm((N_MLA, D, MLA_Q_RANK), D ** -0.5),
        "mla_q_lat_g": gain((N_MLA, MLA_Q_RANK)),
        "mla_w_uq": nrm((N_MLA, MLA_Q_RANK, MLA_HEADS * MLA_QK), MLA_Q_RANK ** -0.5),
        "mla_w_dkv": nrm((N_MLA, D, MLA_KV_RANK + MLA_ROPE), D ** -0.5),
        "mla_kv_lat_g": gain((N_MLA, MLA_KV_RANK)),
        "mla_w_ukv": nrm((N_MLA, MLA_KV_RANK, MLA_HEADS * (MLA_NOPE + MLA_V)), MLA_KV_RANK ** -0.5),
        "mla_q_norm_g": gain((N_MLA, MLA_QK)),
        "mla_k_norm_g": gain((N_MLA, MLA_QK)),
        "mla_w_out": nrm((N_MLA, MLA_HEADS * MLA_V, D), (MLA_HEADS * MLA_V) ** -0.5),
    }

def reference(x, c, ctx, c_ctx, mod_w, mod_b, norm_mix_g, norm_ffn_g,
              ffn_w_gate, ffn_w_up, ffn_w_down,
              ab_w_in, ab_w_out, pool_w, pool_scale, diff_q_norm_g, diff_k_norm_g,
              diff_lam_q1, diff_lam_k1, diff_lam_q2, diff_lam_k2, diff_subln_g,
              mla_w_dq, mla_q_lat_g, mla_w_uq, mla_w_dkv, mla_kv_lat_g, mla_w_ukv,
              mla_q_norm_g, mla_k_norm_g, mla_w_out):
    n_lat = x.shape[1]
    rows = n_lat // GRID_W
    cos_d, sin_d = axial_rope(rows, DIFF_HEAD_DIM)
    cos_m, sin_m = axial_rope(rows, MLA_ROPE)
    h, hc = x, ctx
    for layer in range(DEPTH):
        last = layer == DEPTH - 1
        sh1, sc1, g1, sh2, sc2, g2 = adaln(c, mod_w[layer], mod_b[layer])
        csh1, csc1, cg1, csh2, csc2, cg2 = adaln(c_ctx, mod_w[layer], mod_b[layer])
        a_lat = modulate(rmsnorm(h, norm_mix_g[layer]), sh1[:, None], sc1[:, None])
        a_ctx = modulate(rmsnorm(hc, norm_mix_g[layer]), csh1, csc1)
        if layer % 2 == 0:
            i = layer // 2
            lam_init = 0.8 - 0.6 * math.exp(-0.3 * layer)
            m_lat, m_ctx = pool_diff_mixer(
                a_lat, a_ctx, ab_w_in[i], ab_w_out[i], pool_w[i], pool_scale[i],
                diff_q_norm_g[i], diff_k_norm_g[i], diff_lam_q1[i], diff_lam_k1[i],
                diff_lam_q2[i], diff_lam_k2[i], diff_subln_g[i], lam_init,
                cos_d, sin_d, not last)
        else:
            i = layer // 2
            m_lat, m_ctx = mla_mixer(
                a_lat, a_ctx, mla_w_dq[i], mla_q_lat_g[i], mla_w_uq[i], mla_w_dkv[i],
                mla_kv_lat_g[i], mla_w_ukv[i], mla_q_norm_g[i], mla_k_norm_g[i],
                mla_w_out[i], cos_m, sin_m, not last)
        h = h + g1[:, None] * m_lat
        f_lat = modulate(rmsnorm(h, norm_ffn_g[layer]), sh2[:, None], sc2[:, None])
        h = h + g2[:, None] * swiglu(f_lat, ffn_w_gate[layer], ffn_w_up[layer], ffn_w_down[layer])
        if not last:
            hc = hc + cg1 * m_ctx
            f_ctx = modulate(rmsnorm(hc, norm_ffn_g[layer]), csh2, csc2)
            hc = hc + cg2 * swiglu(f_ctx, ffn_w_gate[layer], ffn_w_up[layer], ffn_w_down[layer])
    return h


_drawn_inputs = setup_inputs


def setup_inputs(seed=0):
    import zlib

    import numpy as np

    out = dict(_drawn_inputs(seed))
    spreads = {}
    factors = {'ctx': 3.127,
     'pool_scale': 2.993,
     'diff_q_norm_g': 8.0,
     'diff_k_norm_g': 8.0,
     'diff_lam_q1': 8.0,
     'diff_lam_k1': 8.0,
     'diff_lam_q2': 8.0,
     'diff_lam_k2': 8.0,
     'diff_subln_g': 3.046,
     'mla_w_dq': 2.669,
     'mla_q_lat_g': 8.0,
     'mla_kv_lat_g': 7.003,
     'mla_q_norm_g': 8.0,
     'mla_k_norm_g': 8.0}
    for name, (base, spread) in spreads.items():
        noise = np.random.default_rng([zlib.crc32(name.encode()), seed]).standard_normal(out[name].shape)
        drawn = base * np.exp(spread * noise) if base else spread * noise
        out[name] = __import__('jax').numpy.asarray(drawn.astype(out[name].dtype))
    for name, factor in factors.items():
        out[name] = (out[name] * factor).astype(out[name].dtype)
    return out
```

```python
from contextlib import ExitStack

import numpy as np

import concourse.bass as bass
from concourse import mybir

F32 = mybir.dt.float32
F32R = mybir.dt.float32r
ALU = mybir.AluOpType
ACT = mybir.ActivationFunctionType
AX = mybir.AxisListType

D = 1024
KT = D // 128
LAT, CTX = 1024, 256
T = LAT + CTX
DEPTH = 2
EPS = 1e-6
GRID_W = 64
HEADS0, HD0 = 4, 64
VD0 = 2 * HD0
HEADS1, NOPE, ROPE, VD1 = 16, 64, 32, 64
QK1 = NOPE + ROPE
Q_RANK, KV_RANK = 384, 256
HIDDEN = 2816
HT = HIDDEN // 128
WINDOWS = (2, 4, 8, 16)
PAD = 16
LAM_INIT = 0.8 - 0.6
BANK = 512
CHUNKS = ((0, 512), (512, 512), (1024, 256))
RANGES = ((0, LAT, 0), (LAT, T, 1))
TT = T // 128

VEC = {}


def _vec_columns():
    at = 0
    for name, n in (("cond", 2 * KT), ("mod_b", DEPTH * 6 * KT), ("mix_g", DEPTH * KT), ("ffn_g", DEPTH * KT),
                    ("pool_scale", 4), ("q_g0", 1), ("k_g0", 1), ("subln_g", 1), ("qlat_g", 3), ("kvlat_g", 2),
                    ("q_g1", 1), ("k_g1", 1), ("lam", 4)):
        VEC[name] = (at, at + n)
        at += n
    return at


NVEC = _vec_columns()


class Piece:

    def __init__(self, stream, slots, iters):
        self.slots, self.iters, self.n0, self.uses0 = slots, iters, stream.n, list(stream.uses)
        stream.n += len(slots) * iters
        for s in slots:
            stream.uses[s] += iters

    def number(self, i, j):
        return i * len(self.slots) + (self.n0 + j)

    def filled(self, i, j):
        s = self.slots[j]
        return i * (16 * self.slots.count(s)) + 16 * (self.uses0[s] + self.slots[:j].count(s) + 1)


class Stream:

    def __init__(self):
        self.n, self.uses = 0, [0, 0, 0, 0]


RING = 3


class Env:

    def __init__(self, nc, dram):
        self.nc, self.dram = nc, dram
        self.live, self.clearing = [], []

    def sbuf(self, ctx):
        return lambda name, shape, dt: ctx.enter_context(self.nc.sbuf_tensor(name, shape, dt))

    def phase(self, ctx):
        for h in self.clearing:
            self.nc.release_semaphore(h)
        self.clearing, self.live = self.live, []

        def sem(name):
            self.live.append(self.nc.alloc_semaphore(name=name))
            return self.live[-1]

        return self.sbuf(ctx), sem

    def clear_old(self, sp):
        for h in self.clearing:
            sp.sem_clear(h)


def each(eng, n):
    return eng.Fori(0, n)


def load_block(e, sp, p, i, j, src):
    sp.wait_ge(e.split_done, p.number(i, j) + 1)
    s = p.slots[j]
    sp.dma_start(e.raw[:, s, 0:src.shape[1]], src).then_inc(e.raw_full[s], 16)


def settle_pool(e):
    e.nc.gpsimd.tensor_tensor(e.spare[:, 0:1], e.ident[:, 0:1], e.ident[:, 0:1], ALU.mult)


def settle_pe(e, col):
    e.nc.tensor.matmul(e.ps[:, col:col + 1], e.ident[:], e.ident[:, 0:1], start=True, stop=True)


def split_block(e, pool, p, i, j, n):
    nc, s, num = e.nc, p.slots[j], p.number(i, j)
    pool.wait_ge(e.raw_full[s], p.filled(i, j))
    pool.wait_ge(e.w_used, num + 1)
    settle_pool(e)
    nc.gpsimd.tensor_scalar(e.whi[:, s, 0:n], e.raw[:, s, 0:n], 1.0, None, ALU.mult).then_inc(e.split_hi, 1)
    pool.wait_ge(e.split_hi, num + 1)
    nc.gpsimd.tensor_tensor(e.wlo[:, s, 0:n], e.raw[:, s, 0:n], e.whi[:, s, 0:n].bitcast(F32),
                            ALU.subtract).then_inc(e.split_done, 1)


def block_ready(e, pe, p, i, j):
    pe.wait_ge(e.split_done, p.number(i, j) + 1 + RING)


def block_used(e, eng, p, i, j):
    eng.wait_ge(e.w_used, p.number(i, j) + 1 + RING)


def free_at_start(eng, counts):
    for s, n in counts:
        eng.sem_inc(s, n)


def products(nc, out, pairs):
    n = 3 * len(pairs)
    at = 0
    for sh, sl, mh, ml in pairs:
        for a, b in ((sh, mh), (sh, ml), (sl, mh)):
            last = nc.tensor.matmul(out, a, b, start=at == 0, stop=at == n - 1)
            at += 1
    return last


def weight_pairs(e, s, m, acts, kt=KT):
    w = lambda buf, k: buf[:, s, k * m:(k + 1) * m]
    return [(w(e.whi, k), w(e.wlo, k), *acts(k)) for k in range(kt)]


def modulation(e, mod_w):
    nc = e.nc
    with ExitStack() as ctx:
        sb, sem = e.phase(ctx)
        silu_c = sb("silu_c", [128, KT, 2], F32)
        rows = sb("mod_rows", [2, 3, 512], F32)
        full = [sem(f"mod_full{s}") for s in range(4)]
        used, acc_done, acc_free = sem("mod_used"), sem("mod_acc_done"), sem("mod_acc_free")
        turned, turned_free, silu_done, gains = sem("mod_turned"), sem("mod_turned_free"), sem("silu_done"), sem("mod_gains")
        lam_p, lam_s, lam_e, lam_d = sem("lam_prod"), sem("lam_sum"), sem("lam_exp"), sem("lam_diff")
        prod = sb("lam_products", [128, 2], F32)
        lexp = sb("lam_exps", [128, 2], F32)
        ldif = sb("lam_difference", [128, 1], F32)
        iters = DEPTH * 12 // 3
        with nc.Block() as block:
            @block.sync
            def _(sp):
                e.clear_old(sp)
                sp.dma_start(e.vec[:], e.dram["vec"]).then_inc(e.consts, 16)
                sp.dma_start(e.ident[:], e.dram["ident"]).then_inc(e.consts, 16)
                sp.dma_start(e.sel[:], e.dram["sel"]).then_inc(e.consts, 16)
                with each(sp, iters) as i:
                    for j in range(12):
                        if j % 4 < 3:
                            sp.wait_ge(used, i * 9 + j // 4 * 3 + j % 4 + 1)
                        else:
                            sp.wait_ge(acc_done, i * 3 + j // 4 + 1)
                        sp.dma_start(e.raw[:, j % 4, :],
                                     mod_w[bass.ds(i * 12 + j, 1), :, :].rearrange("o p f -> p (o f)"))\
                          .then_inc(full[j % 4], 16)

            @block.scalar
            def _(act):
                act.wait_ge(e.consts, 48)
                a, b = VEC["cond"]
                nc.scalar.activation(silu_c[:, :, :], e.vec[:, a:b].rearrange("p (k c) -> p k c", c=2),
                                     ACT.Silu).then_inc(silu_done, 1)
                act.wait_ge(lam_s, 1)
                nc.scalar.activation(lexp[:], e.ps[:, 7 * BANK:7 * BANK + 2], ACT.Exp).then_inc(lam_e, 1)
                with each(act, iters) as i:
                    for j in range(3):
                        act.wait_ge(acc_done, i * 3 + j + 2)
                        if j == 0:
                            act.wait_ge(turned, i + 1)
                        nc.scalar.activation(rows[:, j, :], e.ps[0:2, j * BANK:(j + 1) * BANK],
                                             ACT.Copy).then_inc(acc_free, 1)

            @block.tensor
            def _(pe):
                pe.sem_inc(used, 3)
                pe.sem_inc(acc_done, 1)
                pe.sem_inc(turned, 1)
                pe.wait_ge(lam_p, 1)
                nc.tensor.matmul(e.ps[:, 7 * BANK:7 * BANK + 2], e.sel[0:64, 2:130], prod[0:64, :],
                                 start=True, stop=True).then_inc(lam_s, 1)
                pe.wait_ge(silu_done, 1)
                with each(pe, iters) as i:
                    for j in range(12):
                        pe.wait_ge(full[j % 4], i * 48 + 16 * (j // 4 + 1))
                        if j % 4 == 0:
                            pe.wait_ge(acc_free, i * 3 + j // 4 + 1)
                        for kk in range(2):
                            k = (j % 4) * 2 + kk
                            last = nc.tensor.matmul(e.ps[0:2, (j // 4) * BANK:(j // 4 + 1) * BANK],
                                                    silu_c[:, k, :], e.raw[:, j % 4, kk * 512:(kk + 1) * 512],
                                                    start=k == 0, stop=k == KT - 1)
                        last.then_inc(used if j % 4 < 3 else acc_done, 1)
                    pe.wait_ge(turned_free, i + 1)
                    pe.wait_ge(acc_free, i * 3 + 3 + 3)
                    settle_pe(e, 6 * BANK)
                    for j in range(3):
                        for q in range(4):
                            last = nc.tensor.transpose(e.ps[:, 6 * BANK + (j * 4 + q) * 2:6 * BANK + (j * 4 + q) * 2 + 2],
                                                       rows[:, j, q * 128:(q + 1) * 128], e.ident[0:2, 0:2])
                    last.then_inc(turned, 1)

            @block.vector
            def _(dve):
                dve.sem_inc(turned_free, 1)
                dve.sem_inc(acc_free, 3)
                dve.wait_ge(e.consts, 48)
                a, _b = VEC["lam"]
                nc.vector.memset(e.eps[:], EPS).then_inc(gains, 1)
                nc.vector.tensor_tensor(prod[:], e.vec[:, a:a + 2], e.vec[:, a + 2:a + 4], ALU.mult).then_inc(lam_p, 1)
                dve.wait_ge(lam_e, 1)
                nc.vector.tensor_tensor(ldif[:], lexp[:, 1:2], lexp[:, 0:1], ALU.subtract).then_inc(lam_d, 1)
                dve.wait_ge(lam_d, 1)
                nc.vector.tensor_scalar(e.neg_lam[:], ldif[:], -LAM_INIT, None, ALU.add).then_inc(gains, 1)
                a, b = VEC["subln_g"]
                nc.vector.tensor_scalar(e.subln[:], e.vec[:, a:b], 1.0 - LAM_INIT, None, ALU.mult).then_inc(gains, 1)
                a, b = VEC["q_g0"]
                nc.vector.tensor_scalar(e.qg0[:], e.vec[:, a:b], HD0 ** -0.5, None, ALU.mult).then_inc(gains, 1)
                a, b = VEC["q_g1"]
                nc.vector.tensor_scalar(e.qg1[:], e.vec[:, a:b], QK1 ** -0.5, None, ALU.mult).then_inc(gains, 1)
                a, _b = VEC["mod_b"]
                with each(dve, iters) as i:
                    dve.wait_ge(turned, i + 2)
                    nc.vector.tensor_tensor(
                        e.mod[:, bass.ds(i * 12, 12), :],
                        e.ps[:, 6 * BANK:6 * BANK + 24].rearrange("p (n c) -> p n c", c=2),
                        e.vec[:, bass.ds(i * 12 + a, 12)].rearrange("p (n o) -> p n o", o=1).broadcast_to([128, 12, 2]),
                        ALU.add).then_inc(turned_free, 1)
                dve.wait_ge(turned_free, iters + 1)
                for n, (layer, part, g) in enumerate(((0, 1, "mix_g"), (0, 4, "ffn_g"), (1, 1, "mix_g"), (1, 4, "ffn_g"))):
                    a = VEC[g][0] + layer * KT
                    m = layer * 48 + part * 8
                    nc.vector.scalar_tensor_tensor(
                        e.gain[:, n, :, :], e.mod[:, m:m + 8, :], 1.0,
                        e.vec[:, a:a + 8].rearrange("p (n o) -> p n o", o=1).broadcast_to([128, 8, 2]),
                        ALU.add, ALU.mult).then_inc(gains, 1)
                dve.wait_ge(gains, 9)


def norm(e, name, src, groups, width, gain, shift, hi, lo, ranges, load=None):
    nc = e.nc
    n_tok = ranges[-1][1]
    tt = n_tok // 128
    G = len(groups)
    order = [(g, k) for g, ks in enumerate(groups) for k in ks]
    nt = len(order)
    with ExitStack() as ctx:
        sb, sem = e.phase(ctx)
        sq = sb(f"{name}_sq", [128, 2, n_tok], F32)
        acc = sb(f"{name}_acc", [128, 2, n_tok], F32)
        rms = sb(f"{name}_rms", [128, G * tt], F32)
        rstd = sb(f"{name}_rstd", [128, G * tt], F32)
        tmp = sb(f"{name}_tmp", [128, 2, n_tok], F32)
        s = {x: sem(f"{name}_{x}") for x in ("in", "sq", "acc", "sum", "rms", "rstd", "bc", "tmp", "hi", "lo")}
        with nc.Block() as block:
            @block.sync
            def _(sp):
                e.clear_old(sp)
                for k in range(nt if load else 0):
                    sp.dma_start(src(k), load(k)).then_inc(s["in"], 16)

            @block.scalar
            def _(act):
                for n, (g, k) in enumerate(order):
                    if load and n == 0:
                        act.wait_ge(s["in"], 16 * nt)
                    if n >= 2:
                        act.wait_ge(s["acc"], n - 1)
                    nc.scalar.activation(sq[:, n % 2, :], src(k), ACT.Square).then_inc(s["sq"], 1)
                act.wait_ge(s["sum"], 1)
                nc.scalar.activation(rms[:], e.ps[:, 7 * BANK:7 * BANK + G * tt], ACT.Sqrt,
                                     bias=e.eps[:, 0:1], scale=1.0 / width).then_inc(s["rms"], 1)
                for n, (g, k) in enumerate(order):
                    act.wait_ge(s["tmp"], n + 1)
                    for at, (a, b, c) in enumerate(ranges):
                        if shift:
                            ins = nc.scalar.activation(hi(k)[:, a:b], tmp[:, n % 2, a:b], ACT.Identity, bias=shift(k, c))
                        else:
                            ins = nc.scalar.activation(hi(k)[:, a:b], tmp[:, n % 2, a:b], ACT.Copy)
                    ins.then_inc(s["hi"], 1)

            @block.tensor
            def _(pe):
                at = 0
                for g, ks in enumerate(groups):
                    at += len(ks)
                    pe.wait_ge(s["acc"], at)
                    for t in range(tt):
                        last = nc.tensor.matmul(e.ps[:, 7 * BANK + g * tt + t:7 * BANK + g * tt + t + 1],
                                                acc[:, g % 2, t * 128:(t + 1) * 128], e.sel[:, 2:3], start=True, stop=True)
                    last.then_inc(s["sum"] if g == G - 1 else s["bc"], 1)
                pe.wait_ge(s["rstd"], 1)
                done = 0
                for g, ks in enumerate(groups):
                    if g >= 2:
                        pe.wait_ge(s["lo"], done - len(groups[g - 1]))
                    for t in range(tt):
                        last = nc.tensor.transpose(e.ps[:, (g % 2) * 3 * BANK + t * 128:(g % 2) * 3 * BANK + t * 128 + 128],
                                                   rstd[:, g * tt + t:g * tt + t + 1].broadcast_to([128, 128]), e.ident[:])
                    last.then_inc(s["bc"], 1)
                    done += len(ks)

            @block.vector
            def _(dve):
                n = 0
                for g, ks in enumerate(groups):
                    if g >= 2:
                        dve.wait_ge(s["bc"], g - 1)
                    for x, k in enumerate(ks):
                        dve.wait_ge(s["sq"], n + 1)
                        if x == 0:
                            ins = nc.vector.tensor_copy(acc[:, g % 2, :], sq[:, n % 2, :])
                        else:
                            dve.wait_ge(s["acc"], n)
                            ins = nc.vector.tensor_tensor(acc[:, g % 2, :], acc[:, g % 2, :], sq[:, n % 2, :], ALU.add)
                        ins.then_inc(s["acc"], 1)
                        n += 1
                dve.wait_ge(s["rms"], 1)
                nc.vector.reciprocal(rstd[:], rms[:]).then_inc(s["rstd"], 1)

                def scaled(n):
                    g, k = order[n]
                    dve.wait_ge(s["bc"], G - 1 + g + 1)
                    if n >= 2:
                        dve.wait_ge(s["lo"], n - 1)
                    for a, b, c in ranges:
                        ins = nc.vector.scalar_tensor_tensor(tmp[:, n % 2, a:b], src(k)[:, a:b], gain(k, c),
                                                             e.ps[:, (g % 2) * 3 * BANK + a:(g % 2) * 3 * BANK + b],
                                                             ALU.mult, ALU.mult)
                    ins.then_inc(s["tmp"], 1)

                scaled(0)
                for n, (g, k) in enumerate(order):
                    if n + 1 < nt:
                        scaled(n + 1)
                    dve.wait_ge(s["hi"], n + 1)
                    for a, b, c in ranges:
                        if shift:
                            ins = nc.vector.scalar_tensor_tensor(lo(k)[:, a:b], tmp[:, n % 2, a:b], shift(k, c),
                                                                 hi(k)[:, a:b].bitcast(F32), ALU.add, ALU.subtract)
                        else:
                            ins = nc.vector.tensor_tensor(lo(k)[:, a:b], tmp[:, n % 2, a:b],
                                                          hi(k)[:, a:b].bitcast(F32), ALU.subtract)
                    ins.then_inc(s["lo"], 1)
                dve.wait_ge(s["lo"], nt)


def project0(e, stream, ahi, alo):
    nc = e.nc
    S = e.scratch
    p = Piece(stream, [0, 1, 2, 3], HEADS0)
    with ExitStack() as ctx:
        sb, sem = e.phase(ctx)
        e.rings(ctx)
        cos, sin = sb("cos0", [128, LAT], F32), sb("sin0", [128, LAT], F32)
        sq = sb("p0_sq", [128, T], F32)
        xg = sb("p0_xg", [128, 2, T], F32)
        xs = sb("p0_xs", [128, 2, LAT], F32)
        rot = sb("p0_rot", [128, 2, T], F32)
        qh = sb("p0_hi", [128, 1, T], F32R)
        ql = sb("p0_lo", [128, 1, T], F32R)
        vt = sb("p0_vt", [128, T], F32)
        vs = sb("p0_vs", [128, TT, 2, VD0], F32R)
        rms = sb("p0_rms", [128, 2 * TT], F32)
        rstd = sb("p0_rstd", [128, 2 * TT], F32)
        wide = sb("p0_wide", [128, 2 * TT * HD0], F32)
        names = ("tab", "chunk", "out", "sum", "xs0", "xs1", "mul", "rot", "rms", "rec", "rstd", "bc", "nrm", "hi", "lo", "st", "turn",
                 "vhi", "vlo", "stv", "stu")
        s = {x: sem("p0_" + x) for x in names}
        ST, TR = 6 * BANK, 7 * BANK
        with nc.Block() as block:
            @block.sync
            def _(sp):
                e.clear_old(sp)
                free_at_start(sp, [(s["out"], 3), (s["sum"], 1), (s["rot"], 2), (s["lo"], 2), (s["rms"], 1), (s["rstd"], 1),
                                   (s["bc"], 1), (s["nrm"], 1), (s["st"], 1), (s["turn"], 1), (s["vlo"], 1),
                                   (s["stv"], 1), (s["stu"], 1)])
                sp.dma_start(cos[:], e.dram["cos0"]).then_inc(s["tab"], 16)
                sp.dma_start(sin[:], e.dram["sin0"]).then_inc(s["tab"], 16)
                with each(sp, HEADS0) as i:
                    for j in range(4):
                        load_block(e, sp, p, i, j, e.dram["w_in"][bass.ds(i * 4 + j, 1), :, :].rearrange("o p f -> p (o f)"))

            @block.gpsimd
            def _(pool):
                def rotate(i, j):
                    pool.wait_ge(s["out"], i * 12 + 3 * j + 3 + 3)
                    pool.wait_ge(s["lo"], i * 2 + j + 1)
                    nc.gpsimd.tensor_tensor(rot[:, j, 0:LAT], xg[:, j, 0:LAT], cos[:], ALU.mult).then_inc(s["mul"], 1)
                    nc.gpsimd.tensor_scalar(rot[:, j, LAT:T], xg[:, j, LAT:T], 1.0, None, ALU.mult).then_inc(s["mul"], 1)
                    pool.wait_ge(s[f"xs{j}"], i * 64 + 64)
                    nc.gpsimd.tensor_tensor(xs[:, j, :], xs[:, j, :], sin[:], ALU.mult).then_inc(s["mul"], 1)
                    pool.wait_ge(s["mul"], i * 6 + 3 * j + 3)
                    nc.gpsimd.tensor_tensor(rot[:, j, 0:LAT], rot[:, j, 0:LAT], xs[:, j, :], ALU.add).then_inc(s["rot"], 1)

                pool.wait_ge(s["tab"], 32)
                with each(pool, HEADS0) as i:
                    for j in range(3):
                        split_block(e, pool, p, i, j, 1024)
                    rotate(i, 0)
                    split_block(e, pool, p, i, 3, 1024)
                    rotate(i, 1)

            @block.scalar
            def _(act):
                def chunk_ready(i, j, c):
                    if c < 2:
                        act.wait_ge(s["chunk"], i * 8 + 2 * j + c + 1)
                    else:
                        block_used(e, act, p, i, j)

                def evict_qk(i, j):
                    g = e.qg0[:, 0:1] if j == 0 else e.vec[:, VEC["k_g0"][0]:VEC["k_g0"][1]]
                    act.wait_ge(s["sum"], i * 2 + j + 1)
                    act.wait_ge(s["rot"], i * 2 + j + 1)
                    for c, (a, w) in enumerate(CHUNKS):
                        chunk_ready(i, j, c)
                        nc.scalar.activation(sq[:, a:a + w], e.ps[:, a:a + w], ACT.Square)
                        nc.scalar.activation(xg[:, j, a:a + w], e.ps[:, a:a + w], ACT.Copy, scale=g).then_inc(s["out"], 1)
                    act.wait_ge(s["out"], i * 12 + 3 * j + 3 + 3)
                    for a, b in ((0, 32), (32, 0), (64, 96), (96, 64)):
                        act.dma_start(xs[a:a + 32, j, :], xg[b:b + 32, j, 0:LAT]).then_inc(s[f"xs{j}"], 16)

                def root(i, j):
                    act.wait_ge(s["sum"], i * 2 + j + 2)
                    act.wait_ge(s["rstd"], i * 2 + j + 1)
                    nc.scalar.activation(rms[:], e.ps[:, ST:ST + 2 * TT], ACT.Sqrt, bias=e.eps[:, 0:1],
                                         scale=1.0 / HD0).then_inc(s["rms"], 1)

                def plain(i, j):
                    for c, (a, w) in enumerate(CHUNKS):
                        chunk_ready(i, j, c)
                        nc.scalar.activation(vt[:, a:a + w], e.ps[:, a:a + w], ACT.Copy).then_inc(s["out"], 1)

                def high(i, j):
                    act.wait_ge(s["nrm"], i * 2 + j + 2)
                    act.wait_ge(s["st"], i * 128 + 64 * j + 1)
                    nc.scalar.activation(qh[:, 0, :], rot[:, j, :], ACT.Copy).then_inc(s["hi"], 1)

                def store(i, j):
                    act.wait_ge(s["lo"], i * 2 + j + 3)
                    dst = S["q0"] if j == 0 else S["k0"]
                    for m in range(2):
                        for x, buf in enumerate((qh, ql)):
                            act.dma_start(dst[bass.ds(i * 4 + (2 * m + x), 1), :, :].rearrange("o p t -> p (o t)"),
                                          buf[64 * m:64 * m + 64, 0, :].bitcast(F32)).then_inc(s["st"], 16)

                with each(act, HEADS0) as i:
                    evict_qk(i, 0)
                    evict_qk(i, 1)
                    root(i, 0)
                    act.wait_ge(s["stu"], i * 16 + 1)
                    plain(i, 2)
                    root(i, 1)
                    high(i, 0)
                    act.wait_ge(s["stv"], i * 16 + 1)
                    for c, (a, w) in enumerate(CHUNKS):
                        act.wait_ge(s["turn"], i * 3 + c + 2)
                        nc.scalar.activation(vs[:, 4 * c:4 * c + w // 128, 0, :],
                                             e.ps[:, TR:TR + w].rearrange("p (t v) -> p t v", v=128),
                                             ACT.Copy).then_inc(s["vhi"], 1)
                    store(i, 0)
                    act.wait_ge(s["vlo"], i * 3 + 3 + 1)
                    act.dma_start(S["v0"][bass.ds(i, 1), :, :].rearrange("o p f -> p (o f)"),
                                  vs[:].rearrange("p t x v -> p (t x v)").bitcast(F32)).then_inc(s["stv"], 16)
                    plain(i, 3)
                    act.wait_ge(s["out"], i * 12 + 12 + 3)
                    act.dma_start(S["u0"][bass.ds(i, 1), :, :].rearrange("o p t -> p (o t)"), vt[:]).then_inc(s["stu"], 16)
                    high(i, 1)
                    store(i, 1)
                act.wait_ge(s["st"], HEADS0 * 128 + 1)
                act.wait_ge(s["stv"], HEADS0 * 16 + 1)
                act.wait_ge(s["stu"], HEADS0 * 16 + 1)

            @block.tensor
            def _(pe):
                def project(i, j):
                    block_ready(e, pe, p, i, j)
                    for c, (a, w) in enumerate(CHUNKS):
                        pe.wait_ge(s["out"], i * 12 + 3 * j + c + 1)
                        last = products(nc, e.ps[:, a:a + w],
                                        weight_pairs(e, j, 128, lambda k: (ahi[:, k, a:a + w], alo[:, k, a:a + w])))
                        last.then_inc(s["chunk"] if c < 2 else e.w_used, 1)

                def sums(i, j):
                    pe.wait_ge(s["out"], i * 12 + 3 * j + 3 + 3)
                    pe.wait_ge(s["rms"], i * 2 + j + 1)
                    for t in range(TT):
                        last = nc.tensor.matmul(e.ps[:, ST + 2 * t:ST + 2 * t + 2], sq[:, t * 128:(t + 1) * 128],
                                                e.sel[:, 0:2], start=True, stop=True)
                    last.then_inc(s["sum"], 1)

                def spread(i, j):
                    pe.wait_ge(s["rstd"], i * 2 + j + 2)
                    pe.wait_ge(s["nrm"], i * 2 + j + 1)
                    for t in range(TT):
                        last = nc.tensor.transpose(
                            e.ps[:, 3 * BANK + t * 128:3 * BANK + (t + 1) * 128],
                            wide[:, t * 128:(t + 1) * 128],
                            e.ident[:])
                    last.then_inc(s["bc"], 1)

                with each(pe, HEADS0) as i:
                    project(i, 0)
                    project(i, 1)
                    sums(i, 0)
                    project(i, 2)
                    spread(i, 0)
                    sums(i, 1)
                    for c, (a, w) in enumerate(CHUNKS):
                        pe.wait_ge(s["out"], i * 12 + 6 + c + 1 + 3)
                        pe.wait_ge(s["vlo"], i * 3 + c + 1)
                        for t in range(w // 128):
                            last = nc.tensor.transpose(e.ps[:, TR + t * 128:TR + (t + 1) * 128],
                                                       vt[:, a + t * 128:a + (t + 1) * 128], e.ident[:])
                        last.then_inc(s["turn"], 1)
                    project(i, 3)
                    spread(i, 1)

            @block.vector
            def _(dve):
                def recip(i, j):
                    dve.wait_ge(s["rms"], i * 2 + j + 2)
                    nc.vector.reciprocal(rstd[:], rms[:]).then_inc(s["rec"], 1)
                    dve.wait_ge(s["rec"], i * 2 + j + 1)
                    dve.wait_ge(s["bc"], i * 2 + j + 1)
                    nc.vector.tensor_copy(wide[:].rearrange("p (m d) -> p m d", d=HD0),
                                          rstd[:].rearrange("p (m o) -> p m o", o=1).broadcast_to([128, 2 * TT, HD0]))\
                      .then_inc(s["rstd"], 1)

                def normed(i, j):
                    dve.wait_ge(s["bc"], i * 2 + j + 2)
                    dve.wait_ge(s["rot"], i * 2 + j + 3)
                    nc.vector.tensor_tensor(rot[:, j, :], rot[:, j, :], e.ps[:, 3 * BANK:3 * BANK + T],
                                            ALU.mult).then_inc(s["nrm"], 1)

                def low(i, j):
                    dve.wait_ge(s["hi"], i * 2 + j + 1)
                    nc.vector.tensor_tensor(ql[:, 0, :], rot[:, j, :], qh[:, 0, :].bitcast(F32),
                                            ALU.subtract).then_inc(s["lo"], 1)

                with each(dve, HEADS0) as i:
                    recip(i, 0)
                    normed(i, 0)
                    recip(i, 1)
                    low(i, 0)
                    for c, (a, w) in enumerate(CHUNKS):
                        dve.wait_ge(s["vhi"], i * 3 + c + 1)
                        nc.vector.tensor_tensor(vs[:, 4 * c:4 * c + w // 128, 1, :],
                                                e.ps[:, TR:TR + w].rearrange("p (t v) -> p t v", v=128),
                                                vs[:, 4 * c:4 * c + w // 128, 0, :].bitcast(F32),
                                                ALU.subtract).then_inc(s["vlo"], 1)
                    normed(i, 1)
                    low(i, 1)


def alternate(first, second):
    out, n = [], max(len(first), len(second))
    for x in range(n):
        for steps in (first, second):
            out += steps[x * len(steps) // n:(x + 1) * len(steps) // n]
    return out


SLOTS0 = [(0, [-9, -8]), (1, [-7, -6, -5]), (2, [-4, -3]), (3, [-2, -1]), (4, []), (5, [0, 1, 2]), (6, [3, 4]),
          (7, [5, 6, 7]), (8, [8, 9]), (9, [10, 11, 12])]
TAIL0 = [(None, list(range(13, 22)))]
KEYS0 = [(u, k) for u, n in ((0, 10), (1, 10), (2, 2)) for k in range(n)]

SLOTS1 = [(0, [-12, -11]), (1, [-10, -9, -8]), (2, [-7, -6]), (3, [-5, -4, -3]), (4, [-2, -1]), (5, [0, 1, 2]),
          (6, [3, 4]), (7, [5, 6, 7])]
TAIL1 = [(None, list(range(8, 20)))]


def attention0(e, ot):
    nc, S = e.nc, e.scratch
    NQ, NK = 10, 22
    with ExitStack() as ctx:
        sb, sem = e.phase(ctx)
        qs = sb("a0_q", [128, 2, 2, T], F32R)
        ks = sb("a0_k", [128, 2, 2, 2, T], F32R)
        vs = sb("a0_v", [128, 2, TT, 2, VD0], F32R)
        pd = sb("a0_pd", [128, 8, T], F32)
        pc = sb("a0_pc", [128, 2, CTX], F32)
        p1 = sb("a0_p1", [128, 2, T], F32)
        pth = sb("a0_pth", [128, 2, BANK], F32R)
        ptl = sb("a0_ptl", [128, 2, BANK], F32R)
        nb = sb("a0_negmax", [128, 4], F32)
        rs = sb("a0_sum", [128, 4], F32)
        rr = sb("a0_recip", [128, 4], F32)
        s = {x: sem("a0_" + x) for x in ("qk0", "qk1", "v0", "v1", "scores", "max", "exp", "rec", "scaled", "mul", "comb",
                                         "turn", "hi", "lo", "pv", "out")}
        TB, OB = 6 * BANK, 7 * BANK

        def probs(q, a, b):
            return pd[:, q, a:b] if q < 8 else pc[:, q - 8, a - LAT:b - LAT]

        def span(q):
            return (0, T) if q < 8 else (LAT, T)

        def unit(k):
            u, kk = KEYS0[k % NK]
            first = {0: 0, 1: 4, 2: 8}[u]
            return u, kk, list(range(first, first + (4 if u < 2 else 2)))

        with nc.Block() as block:
            @block.sync
            def _(sp):
                e.clear_old(sp)
                free_at_start(sp, [(s["exp"], 2), (s["comb"], 2), (s["turn"], 1), (s["pv"], 2), (s["lo"], 1), (s["out"], 1)])
                for h in range(HEADS0):
                    par = h % 2
                    if h >= 2:
                        sp.wait_ge(s["scores"], 2 * NQ * (h - 1))
                    for m in range(2):
                        sp.dma_start(qs[:, par, m, :].bitcast(F32), S["q0"][4 * h + 2 * m:4 * h + 2 * m + 2, :, :]
                                     .rearrange("x d t -> (x d) t")).then_inc(s[f"qk{par}"], 16)
                        for x in range(2):
                            for half in range(2):
                                sp.dma_start(ks[64 * half:64 * half + 64, par, m, x, :].bitcast(F32),
                                             S["k0"][4 * h + 2 * m + x, :, :]).then_inc(s[f"qk{par}"], 16)
                    if h >= 2:
                        sp.wait_ge(s["pv"], NK * (h - 1) + 2)
                    sp.dma_start(vs[:, par, :, :, :].rearrange("p t x v -> p (t x v)").bitcast(F32),
                                 S["v0"][h, :, :]).then_inc(s[f"v{par}"], 16)

            def walk(step):
                for h in range(HEADS0):
                    for n, (q, keys) in enumerate(SLOTS0):
                        step(h, q, [NK * h + k for k in keys if NK * h + k >= 0])
                for q, keys in TAIL0:
                    step(HEADS0 - 1, None, [NK * (HEADS0 - 1) + k for k in keys])

            @block.tensor
            def _(pe):
                def score(h, q, m, c):
                    a, w = CHUNKS[c]
                    def run():
                        par, at = h % 2, 2 * (NQ * h + q) + m
                        if q == 0 and m == 0 and c == 0:
                            pe.wait_ge(s[f"qk{par}"], 160 * (h // 2 + 1))
                        pe.wait_ge(s["exp"], at + 1)
                        o = e.ps[:, m * 3 * BANK + a:m * 3 * BANK + a + w]
                        st = qs[:, par, m, q * 128:(q + 1) * 128]
                        nc.tensor.matmul(o, st, ks[:, par, m, 0, a:a + w], start=True, stop=False)
                        last = nc.tensor.matmul(o, st, ks[:, par, m, 1, a:a + w], start=False, stop=True)
                        if c == 2:
                            last.then_inc(s["scores"], 1)
                    return run

                def turn(k):
                    def run():
                        u, kk, qts = unit(k)
                        key = kk if u < 2 else kk + 8
                        pe.wait_ge(s["comb"], NQ * (k // NK) + qts[-1] + 1 + 2)
                        pe.wait_ge(s["lo"], k + 1)
                        for x, q in enumerate(qts):
                            last = nc.tensor.transpose(e.ps[:, TB + x * 128:TB + (x + 1) * 128],
                                                       probs(q, key * 128, (key + 1) * 128), e.ident[:])
                        last.then_inc(s["turn"], 1)
                    return run

                def value(k):
                    def run():
                        u, kk, qts = unit(k)
                        h, n = k // NK, 128 * len(qts)
                        key = kk if u < 2 else kk + 8
                        final = kk == (9 if u < 2 else 1)
                        if kk == 0:
                            if u == 0:
                                pe.wait_ge(s[f"v{h % 2}"], 16 * (h // 2 + 1))
                            pe.wait_ge(s["out"], 3 * h + u + 1)
                        pe.wait_ge(s["lo"], k + 2)
                        o = e.ps[:, OB:OB + n]
                        vh, vl = vs[:, h % 2, key, 0, :], vs[:, h % 2, key, 1, :]
                        ph, pl = pth[:, k % 2, 0:n], ptl[:, k % 2, 0:n]
                        nc.tensor.matmul(o, vh, ph, start=kk == 0, stop=False)
                        nc.tensor.matmul(o, vh, pl, start=False, stop=False)
                        nc.tensor.matmul(o, vl, ph, start=False, stop=final).then_inc(s["pv"], 1)
                    return run

                done = [0]

                def step(h, q, keys):
                    first = [] if q is None else [score(h, q, m, c) for m in range(2) for c in range(3) if q < 8 or c == 2]
                    second = []
                    for k in keys:
                        second.append(turn(k))
                        if k >= 1:
                            second.append(value(k - 1))
                    for run in alternate(first, second):
                        run()

                walk(step)
                value(NK * HEADS0 - 1)()

            @block.vector
            def _(dve):
                def step(h, q, keys):
                    for k in keys:
                        u, kk, qts = unit(k)
                        n = 128 * len(qts)
                        dve.wait_ge(s["hi"], k + 1)
                        nc.vector.tensor_tensor(ptl[:, k % 2, 0:n], e.ps[:, TB:TB + n], pth[:, k % 2, 0:n].bitcast(F32),
                                                ALU.subtract).then_inc(s["lo"], 1)
                    if q is None:
                        return
                    at = NQ * h + q
                    a, b = span(q)
                    for m in range(2):
                        dve.wait_ge(s["scores"], 2 * at + m + 1)
                        nc.vector.tensor_reduce(nb[:, (2 * at + m) % 4:(2 * at + m) % 4 + 1],
                                                e.ps[:, m * 3 * BANK + a:m * 3 * BANK + b], AX.X, ALU.max,
                                                negate=True).then_inc(s["max"], 1)
                    dve.wait_ge(s["exp"], 2 * at + 2 + 2)
                    dve.wait_ge(s["comb"], at + 1)
                    x = 2 * (at % 2)
                    nc.vector.reciprocal(rr[:, x:x + 2], rs[:, x:x + 2]).then_inc(s["rec"], 1)

                walk(step)

            @block.scalar
            def _(act):
                def step(h, q, keys):
                    for k in keys:
                        u, kk, qts = unit(k)
                        n = 128 * len(qts)
                        act.wait_ge(s["turn"], k + 2)
                        act.wait_ge(s["pv"], k + 1)
                        nc.scalar.activation(pth[:, k % 2, 0:n], e.ps[:, TB:TB + n], ACT.Copy).then_inc(s["hi"], 1)
                        if kk == 0 and k:
                            copy_out(k - 1)
                    if q is None:
                        return
                    at = NQ * h + q
                    a, b = span(q)
                    if q in (0, 4, 8) and h:
                        act.wait_ge(s["turn"], NK * (h - 1) + {0: 10, 4: 20, 8: 22}[q] + 1)
                    for m in range(2):
                        act.wait_ge(s["max"], 2 * at + m + 1)
                        if m == 1:
                            act.wait_ge(s["comb"], at + 1)
                        dst = probs(q, a, b) if m == 0 else p1[:, at % 2, a:b]
                        x = (2 * at + m) % 4
                        nc.scalar.activation(dst, e.ps[:, m * 3 * BANK + a:m * 3 * BANK + b], ACT.Exp,
                                             bias=nb[:, x:x + 1], accum_out=rs[:, x:x + 1]).then_inc(s["exp"], 1)
                    act.wait_ge(s["rec"], at + 1)
                    x = 2 * (at % 2)
                    nc.scalar.activation(probs(q, a, b), probs(q, a, b), ACT.Copy, scale=rr[:, x:x + 1]).then_inc(s["scaled"], 1)

                def copy_out(k):
                    u, kk, qts = unit(k)
                    n, h = 128 * len(qts), k // NK
                    act.wait_ge(s["pv"], k + 1 + 2)
                    nc.scalar.activation(ot[:, h, qts[0] * 128:qts[0] * 128 + n], e.ps[:, OB:OB + n],
                                         ACT.Copy).then_inc(s["out"], 1)

                walk(step)
                copy_out(NK * HEADS0 - 1)
                act.wait_ge(s["out"], 3 * HEADS0 + 1)

            @block.gpsimd
            def _(pool):
                for h in range(HEADS0):
                    for q in range(NQ):
                        at = NQ * h + q
                        a, b = span(q)
                        x = 2 * (at % 2)
                        pool.wait_ge(s["rec"], at + 1)
                        nc.gpsimd.tensor_scalar(p1[:, at % 2, a:b], p1[:, at % 2, a:b], rr[:, x + 1:x + 2],
                                                e.neg_lam[:, 0:1], ALU.mult, ALU.mult).then_inc(s["mul"], 1)
                        pool.wait_ge(s["mul"], at + 1)
                        pool.wait_ge(s["scaled"], at + 1)
                        nc.gpsimd.tensor_tensor(probs(q, a, b), probs(q, a, b), p1[:, at % 2, a:b],
                                                ALU.add).then_inc(s["comb"], 1)


def pool_mixer(e, ahi, alo):
    nc, S = e.nc, e.scratch
    segs = ((PAD, 0, LAT), (3 * PAD + LAT, LAT, CTX))
    W = LAT + CTX + 4 * PAD
    G = len(WINDOWS)
    with ExitStack() as ctx:
        sb, sem = e.phase(ctx)
        u = sb("pm_u", [128, G, W], F32)
        edge = sb("pm_edge", [128, G, 2 * PAD], F32)
        wa, wb = sb("pm_wa", [128, W], F32), sb("pm_wb", [128, W], F32)
        d = sb("pm_d", [128, 2, T], F32)
        pw = sb("pm_w", [128, G, 128], F32)
        s = {x: sem("pm_" + x) for x in ("zero", "in", "sum", "d", "y", "hi", "lo")}
        with nc.Block() as block:
            @block.sync
            def _(sp):
                e.clear_old(sp)
                sp.dma_start(edge[:], e.dram["pool_edge"]).then_inc(s["in"], 16)
                sp.dma_start(pw[:], e.dram["pool_w"]).then_inc(s["in"], 16)
                sp.wait_ge(s["zero"], 1)
                for g in range(G):
                    for at, a, n in segs:
                        sp.dma_start(u[:, g, at:at + n], S["u0"][g, :, a:a + n]).then_inc(s["in"], 16)

            @block.gpsimd
            def _(pool):
                nc.gpsimd.memset(u[:], 0.0).then_inc(s["zero"], 1)

            def low(dve, g):
                for c, (a, w) in enumerate(CHUNKS):
                    dve.wait_ge(s["hi"], 3 * g + c + 1)
                    x = VEC["pool_scale"][0] + g
                    nc.vector.scalar_tensor_tensor(alo[:, g, a:a + w], e.ps[:, (g % 2) * 3 * BANK + a:(g % 2) * 3 * BANK + a + w],
                                                   e.vec[:, x:x + 1], ahi[:, g, a:a + w].bitcast(F32),
                                                   ALU.mult, ALU.subtract).then_inc(s["lo"], 1)

            @block.vector
            def _(dve):
                dve.wait_ge(s["in"], 16 * (2 + 2 * G))
                sums = 0
                for g, w in enumerate(WINDOWS):
                    src, m = u[:, g, :], 1
                    a, b = 0, W
                    if g:
                        dve.wait_ge(s["d"], 2 * g)
                    while m < w:
                        dst = (wa, wb)[m.bit_length() % 2]
                        l, r = (1, 0) if m == 1 else (m // 2, m // 2)
                        a, b = a + l, b - r
                        nc.vector.tensor_tensor(dst[:, a:b], src[:, a - l:b - l], src[:, a + r:b + r],
                                                ALU.add).then_inc(s["sum"], 1)
                        sums += 1
                        dve.wait_ge(s["sum"], sums)
                        src, m = dst, 2 * m
                    if g >= 2:
                        dve.wait_ge(s["y"], 3 * (g - 1))
                    for at, t, n in segs:
                        for x, y in ((at, 0), (at + n - PAD, PAD)):
                            nc.vector.tensor_tensor(src[:, x:x + PAD], src[:, x:x + PAD], edge[:, g, y:y + PAD],
                                                    ALU.mult).then_inc(s["sum"], 1)
                            sums += 1
                    dve.wait_ge(s["sum"], sums)
                    for at, t, n in segs:
                        nc.vector.scalar_tensor_tensor(d[:, g % 2, t:t + n], src[:, at:at + n], 1.0 / w, u[:, g, at:at + n],
                                                       ALU.mult, ALU.subtract).then_inc(s["d"], 1)
                    if g:
                        low(dve, g - 1)
                low(dve, G - 1)
                dve.wait_ge(s["lo"], 3 * G)

            @block.tensor
            def _(pe):
                for g in range(G):
                    pe.wait_ge(s["d"], 2 * g + 2)
                    for c, (a, w) in enumerate(CHUNKS):
                        if g >= 2:
                            pe.wait_ge(s["lo"], 3 * (g - 2) + c + 1)
                        nc.tensor.matmul(e.ps[:, (g % 2) * 3 * BANK + a:(g % 2) * 3 * BANK + a + w], pw[:, g, :],
                                         d[:, g % 2, a:a + w], start=True, stop=True).then_inc(s["y"], 1)

            @block.scalar
            def _(act):
                for g in range(G):
                    x = VEC["pool_scale"][0] + g
                    for c, (a, w) in enumerate(CHUNKS):
                        act.wait_ge(s["y"], 3 * g + c + 1)
                        nc.scalar.activation(ahi[:, g, a:a + w], e.ps[:, (g % 2) * 3 * BANK + a:(g % 2) * 3 * BANK + a + w],
                                             ACT.Copy, scale=e.vec[:, x:x + 1]).then_inc(s["hi"], 1)


def mix_out(e, name, stream, h, acts, n_tok, w_dram, layer, load_h=None):
    nc = e.nc
    chunks = [c for c in CHUNKS if c[0] < n_tok]
    n = len(chunks)
    p = Piece(stream, [0, 1, 2, 3], KT // 4)
    with ExitStack() as ctx:
        sb, sem = e.phase(ctx)
        e.rings(ctx)
        s = {x: sem(f"{name}_{x}") for x in ("h", "chunk", "out")}
        with nc.Block() as block:
            @block.sync
            def _(sp):
                e.clear_old(sp)
                free_at_start(sp, [(s["out"], n)])
                if load_h:
                    load_h(sp, s["h"])
                with each(sp, p.iters) as i:
                    for j in range(4):
                        load_block(e, sp, p, i, j, w_dram[bass.ds(i * 4 + j, 1), :, :].rearrange("o p f -> p (o f)"))

            @block.gpsimd
            def _(pool):
                with each(pool, p.iters) as i:
                    for j in range(4):
                        split_block(e, pool, p, i, j, 1024)

            @block.tensor
            def _(pe):
                with each(pe, p.iters) as i:
                    for j in range(4):
                        block_ready(e, pe, p, i, j)
                        for c, (a, w) in enumerate(chunks):
                            pe.wait_ge(s["out"], i * 4 * n + j * n + c + 1)
                            last = products(nc, e.ps[:, a:a + w], weight_pairs(e, j, 128, lambda k: acts(k, a, w)))
                            last.then_inc(s["chunk"] if c < n - 1 else e.w_used, 1)

            @block.vector
            def _(dve):
                if load_h:
                    dve.wait_ge(s["h"], 16 * KT)
                with each(dve, p.iters) as i:
                    for j in range(4):
                        for c, (a, w) in enumerate(chunks):
                            if c < n - 1:
                                dve.wait_ge(s["chunk"], i * 4 * (n - 1) + j * (n - 1) + c + 1)
                            else:
                                block_used(e, dve, p, i, j)
                            m = layer * 48 + 2 * 8 + j
                            nc.vector.scalar_tensor_tensor(
                                h[:, bass.ds(i * 4 + j, 1), a:a + w].rearrange("p o t -> p (o t)"), e.ps[:, a:a + w],
                                e.mod[:, bass.ds(i * 4 + m, 1), int(a >= LAT)],
                                h[:, bass.ds(i * 4 + j, 1), a:a + w].rearrange("p o t -> p (o t)"),
                                ALU.mult, ALU.add).then_inc(s["out"], 1)
                dve.wait_ge(s["out"], KT * n + n)


def ffn(e, name, stream, h, ahi, alo, n_tok, w_dram, layer):
    nc = e.nc
    chunks = [c for c in CHUNKS if c[0] < n_tok]
    n = len(chunks)
    pairs = HT // 2
    first = Piece(stream, [0, 1, 2, 0], 1)
    mid = Piece(stream, [1, 2, 0, 1, 2, 0], pairs - 1)
    end = Piece(stream, [1, 2], 1)
    with ExitStack() as ctx:
        sb, sem = e.phase(ctx)
        e.rings(ctx, 3)
        sg = sb(f"{name}_silu", [128, n_tok], F32)
        hm = sb(f"{name}_hidden", [128, n_tok], F32)
        hh = sb(f"{name}_hhi", [128, 2, n_tok], F32R)
        hl = sb(f"{name}_hlo", [128, 2, n_tok], F32R)
        s = {x: sem(f"{name}_{x}") for x in ("gate", "silu", "up", "prod", "hi", "lo", "down", "out")}
        NB = KT * n

        with nc.Block() as block:
            @block.sync
            def _(sp):
                e.clear_old(sp)
                free_at_start(sp, [(s["silu"], n), (s["prod"], n), (s["out"], 2), (s["down"], 1)])

                def load(p, i, j, at):
                    load_block(e, sp, p, i, j, w_dram[bass.ds(at, 1), :, :].rearrange("o p f -> p (o f)"))

                for j in range(4):
                    load(first, 0, j, j)
                with each(sp, mid.iters) as i:
                    for j in range(6):
                        load(mid, i, j, i * 6 + 4 + j)
                for j in range(2):
                    load(end, 0, j, 3 * HT - 2 + j)

            @block.gpsimd
            def _(pool):
                for j in range(4):
                    split_block(e, pool, first, 0, j, 1024)
                with each(pool, mid.iters) as i:
                    for j in range(6):
                        split_block(e, pool, mid, i, j, 1024)
                for j in range(2):
                    split_block(e, pool, end, 0, j, 1024)

            @block.tensor
            def _(pe):
                def column(p, i, j, at, bank, done, read):
                    block_ready(e, pe, p, i, j)
                    for c, (a, w) in enumerate(chunks):
                        pe.wait_ge(read, at * n + c + 1)
                        last = products(nc, e.ps[:, bank + a:bank + a + w],
                                        weight_pairs(e, p.slots[j], 128, lambda k: (ahi[:, k, a:a + w], alo[:, k, a:a + w])))
                        last.then_inc(done if c < n - 1 else e.w_used, 1)

                def down(p, i, j, pair):
                    block_ready(e, pe, p, i, j + 1)
                    pe.wait_ge(s["lo"], pair * 2 * n + 2 * n)
                    sl = p.slots[j], p.slots[j + 1]
                    for m in range(KT):
                        for c, (a, w) in enumerate(chunks):
                            x = m * n + c
                            pe.wait_ge(s["out"], pair * NB + x + 1)
                            pairs_ = [(e.whi[:, sl[t], m * 128:(m + 1) * 128], e.wlo[:, sl[t], m * 128:(m + 1) * 128],
                                       hh[:, t, a:a + w], hl[:, t, a:a + w]) for t in range(2)]
                            last = products(nc, e.ps[:, (6 + x % 2) * BANK:(6 + x % 2) * BANK + w], pairs_)
                            last.then_inc(s["down"], 1)
                    pe.wait_ge(s["down"], pair * NB + NB + 1)
                    pe.sem_inc(e.w_used, 2)

                column(first, 0, 0, 0, 0, s["gate"], s["silu"])
                column(first, 0, 1, 0, 3 * BANK, s["up"], s["prod"])
                column(first, 0, 2, 1, 0, s["gate"], s["silu"])
                column(first, 0, 3, 1, 3 * BANK, s["up"], s["prod"])
                with each(pe, mid.iters) as i:
                    column(mid, i, 0, i * 2 + 2, 0, s["gate"], s["silu"])
                    down(mid, i, 1, i)
                    column(mid, i, 3, i * 2 + 2, 3 * BANK, s["up"], s["prod"])
                    column(mid, i, 4, i * 2 + 3, 0, s["gate"], s["silu"])
                    column(mid, i, 5, i * 2 + 3, 3 * BANK, s["up"], s["prod"])
                down(end, 0, 0, pairs - 1)

            def done(eng, p, i, j, at, c, which):
                if c < n - 1:
                    eng.wait_ge(s[which], at * (n - 1) + c + 1)
                else:
                    block_used(e, eng, p, i, j)

            @block.scalar
            def _(act):
                def tile(p, i, jg, at, t):
                    for c, (a, w) in enumerate(chunks):
                        done(act, p, i, jg, at, c, "gate")
                        act.wait_ge(s["prod"], at * n + c + 1)
                        nc.scalar.activation(sg[:, a:a + w], e.ps[:, a:a + w], ACT.Silu).then_inc(s["silu"], 1)
                    for c, (a, w) in enumerate(chunks):
                        act.wait_ge(s["prod"], at * n + c + 1 + n)
                        if c == 0:
                            act.wait_ge(s["down"], (at - t) * (NB // 2) + 1)
                        nc.scalar.activation(hh[:, t, a:a + w], hm[:, a:a + w], ACT.Copy).then_inc(s["hi"], 1)

                tile(first, 0, 0, 0, 0)
                tile(first, 0, 2, 1, 1)
                with each(act, mid.iters) as i:
                    tile(mid, i, 0, i * 2 + 2, 0)
                    tile(mid, i, 4, i * 2 + 3, 1)

            @block.vector
            def _(dve):
                def tile(p, i, ju, at, t):
                    for c, (a, w) in enumerate(chunks):
                        done(dve, p, i, ju, at, c, "up")
                        dve.wait_ge(s["silu"], at * n + c + 1 + n)
                        if (p is mid or at) and c == 0:
                            dve.wait_ge(s["lo"], at * n)
                        nc.vector.tensor_tensor(hm[:, a:a + w], sg[:, a:a + w], e.ps[:, 3 * BANK + a:3 * BANK + a + w],
                                                ALU.mult).then_inc(s["prod"], 1)
                    for c, (a, w) in enumerate(chunks):
                        dve.wait_ge(s["hi"], at * n + c + 1)
                        nc.vector.tensor_tensor(hl[:, t, a:a + w], hm[:, a:a + w], hh[:, t, a:a + w].bitcast(F32),
                                                ALU.subtract).then_inc(s["lo"], 1)

                def add(pair):
                    dve.wait_ge(s["out"], pair * NB + 2)
                    for m in range(KT):
                        for c, (a, w) in enumerate(chunks):
                            x = m * n + c
                            dve.wait_ge(s["down"], pair * NB + x + 2)
                            g = layer * 48 + 5 * 8 + m
                            nc.vector.scalar_tensor_tensor(h[:, m, a:a + w], e.ps[:, (6 + x % 2) * BANK:(6 + x % 2) * BANK + w],
                                                           e.mod[:, g, int(a >= LAT):int(a >= LAT) + 1], h[:, m, a:a + w],
                                                           ALU.mult, ALU.add).then_inc(s["out"], 1)

                tile(first, 0, 1, 0, 0)
                tile(first, 0, 3, 1, 1)
                with each(dve, mid.iters) as i:
                    add(i)
                    tile(mid, i, 3, i * 2 + 2, 0)
                    tile(mid, i, 5, i * 2 + 3, 1)
                add(pairs - 1)
                dve.wait_ge(s["out"], pairs * NB + 2)


def latents1(e, stream, ahi, alo, cq, ck, kx, ksq, cos, sin):
    nc = e.nc
    p = Piece(stream, [0, 1, 2, 0, 1, 2], 1)
    R = slice(NOPE, QK1)
    with ExitStack() as ctx:
        sb, sem = e.phase(ctx)
        e.rings(ctx, 3)
        xs = sb("l1_swapped", [128, LAT], F32)
        s = {x: sem("l1_" + x) for x in ("tab", "chunk", "out", "xs", "mul")}
        jobs = [(j, c) for j in range(6) for c in range(2 if j < 3 else 3)]
        with nc.Block() as block:
            @block.sync
            def _(sp):
                e.clear_old(sp)
                sp.dma_start(cos[R, :], e.dram["cos1"]).then_inc(s["tab"], 16)
                sp.dma_start(sin[R, :], e.dram["sin1"]).then_inc(s["tab"], 16)
                for j in range(6):
                    load_block(e, sp, p, 0, j, e.dram["w_down1"][j, :, :])
                sp.wait_ge(s["out"], len(jobs))
                for a, b in ((64, 80), (80, 64)):
                    sp.dma_start(xs[a:a + 16, :], kx[b:b + 16, 0:LAT]).then_inc(s["xs"], 16)

            @block.gpsimd
            def _(pool):
                for j in range(6):
                    split_block(e, pool, p, 0, j, 1024)
                pool.wait_ge(s["tab"], 32)
                pool.wait_ge(s["xs"], 32)
                nc.gpsimd.tensor_tensor(kx[R, 0:LAT], kx[R, 0:LAT], cos[R, :], ALU.mult).then_inc(s["mul"], 1)
                nc.gpsimd.tensor_tensor(xs[R, :], xs[R, :], sin[R, :], ALU.mult).then_inc(s["mul"], 1)
                pool.wait_ge(s["mul"], 2)
                nc.gpsimd.tensor_tensor(kx[R, 0:LAT], kx[R, 0:LAT], xs[R, :], ALU.add).then_inc(s["mul"], 1)
                pool.wait_ge(s["mul"], 3)

            @block.tensor
            def _(pe):
                for n, (j, c) in enumerate(jobs):
                    a, w = CHUNKS[c]
                    if c == 0:
                        block_ready(e, pe, p, 0, j)
                    if n >= 6:
                        pe.wait_ge(s["out"], n - 5)
                    last = products(nc, e.ps[:, (n % 6) * BANK:(n % 6) * BANK + w],
                                    weight_pairs(e, p.slots[j], 128, lambda k: (ahi[:, k, a:a + w], alo[:, k, a:a + w])))
                    last.then_inc(s["chunk"] if c < (1 if j < 3 else 2) else e.w_used, 1)

            @block.scalar
            def _(act):
                chunks = 0
                a0, _b0 = VEC["k_g1"]
                for n, (j, c) in enumerate(jobs):
                    a, w = CHUNKS[c]
                    if c < (1 if j < 3 else 2):
                        chunks += 1
                        act.wait_ge(s["chunk"], chunks)
                    else:
                        block_used(e, act, p, 0, j)
                    o = e.ps[:, (n % 6) * BANK:(n % 6) * BANK + w]
                    if j < 3:
                        ins = nc.scalar.activation(cq[:, j, a:a + w], o, ACT.Copy)
                    elif j < 5:
                        ins = nc.scalar.activation(ck[:, j - 3, a:a + w], o, ACT.Copy)
                    else:
                        nc.scalar.activation(ksq[R, a:a + w], o[R, :], ACT.Square)
                        ins = nc.scalar.activation(kx[R, a:a + w], o[R, :], ACT.Copy, scale=e.vec[R, a0:a0 + 1])
                    ins.then_inc(s["out"], 1)
                act.wait_ge(s["out"], len(jobs))


def heads1(e, stream, cqh, cql, ckh, ckl, kx, ksq, cos, sin):
    nc, S = e.nc, e.scratch
    p = Piece(stream, [0, 1, 2, 3], HEADS1 // 2)
    KQ, KK = Q_RANK // 128, KV_RANK // 128
    R = slice(NOPE, QK1)
    QT = LAT // 128
    with ExitStack() as ctx:
        sb, sem = e.phase(ctx)
        e.rings(ctx, 4, KQ * 128)
        qsq = sb("h1_qsq", [128, LAT], F32)
        xg = sb("h1_xg", [128, LAT], F32)
        xs = sb("h1_xs", [128, LAT], F32)
        kn = sb("h1_kn", [128, T], F32)
        vt = sb("h1_vt", [64, T], F32)
        vs = sb("h1_vs", [128, TT, 2, VD1], F32R)
        qh, ql = sb("h1_qh", [128, LAT], F32R), sb("h1_ql", [128, LAT], F32R)
        kh, kl = sb("h1_kh", [128, T], F32R), sb("h1_kl", [128, T], F32R)
        rms, rstd = sb("h1_rms", [128, TT], F32), sb("h1_rstd", [128, TT], F32)
        s = {x: sem("h1_" + x) for x in ("chunk", "out", "sum", "xs", "mul", "rot", "rms", "rstd", "bc", "nrm", "hi", "lo",
                                         "turn", "vhi", "vlo", "stq", "stk", "stv")}
        ST, TR, RB = 6 * BANK, 7 * BANK, 3 * BANK
        VCH = ((0, 8), (8, 2))
        with nc.Block() as block:
            @block.sync
            def _(sp):
                e.clear_old(sp)
                free_at_start(sp, [(s["out"], 3), (s["sum"], 2), (s["rot"], 1), (s["rms"], 1), (s["rstd"], 1), (s["bc"], 1),
                                   (s["nrm"], 1), (s["lo"], 2), (s["turn"], 2), (s["vlo"], 1), (s["stq"], 1), (s["stk"], 1),
                                   (s["stv"], 1)])
                with each(sp, p.iters) as i:
                    for j in range(4):
                        src = (e.dram["w_uq"], e.dram["w_ukv"])[j % 2]
                        load_block(e, sp, p, i, j, src[bass.ds(i * 2 + j // 2, 1), :, :].rearrange("o p f -> p (o f)"))

            @block.gpsimd
            def _(pool):
                def rotate(i, x):
                    h = i * 2 + x
                    pool.wait_ge(e.split_done, p.number(i, 2 * x + 1) + 1 + RING)
                    pool.wait_ge(s["xs"], h * 32 + 32)
                    nc.gpsimd.tensor_tensor(xg[R, :], xg[R, :], cos[R, :], ALU.mult).then_inc(s["mul"], 1)
                    pool.wait_ge(s["mul"], h * 2 + 1)
                    nc.gpsimd.tensor_tensor(xs[R, :], xs[R, :], sin[R, :], ALU.mult).then_inc(s["mul"], 1)
                    pool.wait_ge(s["mul"], h * 2 + 2)
                    nc.gpsimd.tensor_tensor(xg[R, :], xg[R, :], xs[R, :], ALU.add).then_inc(s["rot"], 1)
                    pool.wait_ge(s["rot"], h + 2)

                with each(pool, p.iters) as i:
                    split_block(e, pool, p, i, 0, KQ * 128)
                    split_block(e, pool, p, i, 1, KK * 128)
                    rotate(i, 0)
                    split_block(e, pool, p, i, 2, KQ * 128)
                    split_block(e, pool, p, i, 3, KK * 128)
                    rotate(i, 1)

            @block.tensor
            def _(pe):
                def head(i, x):
                    h = i * 2 + x
                    block_ready(e, pe, p, i, 2 * x)
                    for c in range(2):
                        a, w = CHUNKS[c]
                        pe.wait_ge(s["out"], h * 5 + c + 1)
                        last = products(nc, e.ps[:, a:a + w],
                                        weight_pairs(e, 2 * x, 128, lambda k: (cqh[:, k, a:a + w], cql[:, k, a:a + w]), KQ))
                        last.then_inc(s["chunk"] if c < 1 else e.w_used, 1)
                    block_ready(e, pe, p, i, 2 * x + 1)
                    for c, (a, w) in enumerate(CHUNKS):
                        pe.wait_ge(s["out"], h * 5 + 3 + (c + 1 if c < 2 else 0))
                        last = products(nc, e.ps[:, a:a + w],
                                        weight_pairs(e, 2 * x + 1, 128, lambda k: (ckh[:, k, a:a + w], ckl[:, k, a:a + w]), KK))
                        last.then_inc(s["chunk"] if c < 2 else e.w_used, 1)
                    sums(h, 0)
                    for c, (t0, n) in enumerate(VCH):
                        pe.wait_ge(s["out"], h * 5 + 5 + 3)
                        pe.wait_ge(s["vlo"], h * 2 + c + 1)
                        settle_pe(e, TR)
                        for t in range(n):
                            last = nc.tensor.transpose(e.ps[:, TR + t * 64:TR + (t + 1) * 64],
                                                       vt[:, (t0 + t) * 128:(t0 + t + 1) * 128], e.ident[0:64, 0:64])
                        last.then_inc(s["turn"], 1)
                        if c == 0:
                            spread(h, 0)
                            sums(h, 1)
                    spread(h, 1)

                def sums(h, j):
                    src, tt = ((qsq, QT), (ksq, TT))[j]
                    pe.wait_ge(s["out"], h * 5 + (2, 5)[j] + 3)
                    pe.wait_ge(s["rms"], h * 2 + j + 1)
                    for t in range(tt):
                        last = nc.tensor.matmul(e.ps[:, ST + t:ST + t + 1], src[0:QK1, t * 128:(t + 1) * 128],
                                                e.sel[0:QK1, 2:3], start=True, stop=True)
                    last.then_inc(s["sum"], 1)

                def spread(h, j):
                    pe.wait_ge(s["rstd"], h * 2 + j + 2)
                    pe.wait_ge(s["nrm"], h * 2 + j + 1)
                    for t in range((QT, TT)[j]):
                        last = nc.tensor.transpose(e.ps[:, RB + t * 128:RB + (t + 1) * 128],
                                                   rstd[:, t:t + 1].broadcast_to([128, 128]), e.ident[:])
                    last.then_inc(s["bc"], 1)

                with each(pe, p.iters) as i:
                    head(i, 0)
                    head(i, 1)

            @block.scalar
            def _(act):
                kg = VEC["k_g1"][0]

                def head(i, x):
                    h = i * 2 + x
                    act.wait_ge(s["sum"], h * 2 + 1)
                    act.wait_ge(s["lo"], h * 2 + 1)
                    for c in range(2):
                        a, w = CHUNKS[c]
                        if c < 1:
                            act.wait_ge(s["chunk"], h * 3 + 1)
                        else:
                            block_used(e, act, p, i, 2 * x)
                        nc.scalar.activation(qsq[0:QK1, a:a + w], e.ps[0:QK1, a:a + w], ACT.Square)
                        nc.scalar.activation(xg[0:QK1, a:a + w], e.ps[0:QK1, a:a + w], ACT.Copy,
                                             scale=e.qg1[0:QK1, :]).then_inc(s["out"], 1)
                    act.wait_ge(s["out"], h * 5 + 2 + 3)
                    for a, b in ((64, 80), (80, 64)):
                        act.dma_start(xs[a:a + 16, :], xg[b:b + 16, :]).then_inc(s["xs"], 16)
                    act.wait_ge(s["sum"], h * 2 + 2)
                    act.wait_ge(s["nrm"], h * 2 + 1)
                    act.wait_ge(s["turn"], h * 2 + 2)
                    for c, (a, w) in enumerate(CHUNKS):
                        if c < 2:
                            act.wait_ge(s["chunk"], h * 3 + 2 + c)
                        else:
                            block_used(e, act, p, i, 2 * x + 1)
                        nc.scalar.activation(ksq[0:NOPE, a:a + w], e.ps[0:NOPE, a:a + w], ACT.Square)
                        nc.scalar.activation(kx[0:NOPE, a:a + w], e.ps[0:NOPE, a:a + w], ACT.Copy,
                                             scale=e.vec[0:NOPE, kg:kg + 1])
                        nc.scalar.activation(vt[:, a:a + w], e.ps[64:128, a:a + w], ACT.Copy).then_inc(s["out"], 1)
                    root(h, 0)
                    act.wait_ge(s["stv"], h * 16 + 1)
                    vhigh(h, 0)
                    root(h, 1)
                    high(h, 0)
                    vhigh(h, 1)
                    store(h, 0)
                    high(h, 1)
                    act.wait_ge(s["vlo"], h * 2 + 2 + 1)
                    act.dma_start(S["v1"][bass.ds(h, 1), :, :].rearrange("o p f -> p (o f)"),
                                  vs[:].rearrange("p t x v -> p (t x v)").bitcast(F32)).then_inc(s["stv"], 16)
                    store(h, 1)

                def root(h, j):
                    tt = (QT, TT)[j]
                    act.wait_ge(s["sum"], h * 2 + j + 3)
                    act.wait_ge(s["rstd"], h * 2 + j + 1)
                    nc.scalar.activation(rms[:, 0:tt], e.ps[:, ST:ST + tt], ACT.Sqrt, bias=e.eps[:, 0:1],
                                         scale=1.0 / QK1).then_inc(s["rms"], 1)

                def high(h, j):
                    act.wait_ge(s["nrm"], h * 2 + j + 2)
                    act.wait_ge(s["stq" if j == 0 else "stk"], h * 32 + 1)
                    dst, src = ((qh, xg), (kh, kn))[j]
                    nc.scalar.activation(dst[0:QK1, :], src[0:QK1, :], ACT.Copy).then_inc(s["hi"], 1)

                def vhigh(h, c):
                    t0, n = VCH[c]
                    act.wait_ge(s["turn"], h * 2 + c + 3)
                    nc.scalar.activation(vs[:, t0:t0 + n, 0, :], e.ps[:, TR:TR + n * 64].rearrange("p (t v) -> p t v", v=64),
                                         ACT.Copy).then_inc(s["vhi"], 1)

                def store(h, j):
                    act.wait_ge(s["lo"], h * 2 + j + 3)
                    st, dst, bufs = ((s["stq"], S["q1"], (qh, ql)), (s["stk"], S["k1"], (kh, kl)))[j]
                    for x, buf in enumerate(bufs):
                        act.dma_start(dst[bass.ds(h * 2 + x, 1), :, :].rearrange("o p t -> p (o t)"),
                                      buf[0:QK1, :].bitcast(F32)).then_inc(st, 16)

                with each(act, p.iters) as i:
                    head(i, 0)
                    head(i, 1)
                act.wait_ge(s["stq"], HEADS1 * 32 + 1)
                act.wait_ge(s["stk"], HEADS1 * 32 + 1)
                act.wait_ge(s["stv"], HEADS1 * 16 + 1)

            @block.vector
            def _(dve):
                def recip(h, j):
                    tt = (QT, TT)[j]
                    dve.wait_ge(s["rms"], h * 2 + j + 2)
                    dve.wait_ge(s["bc"], h * 2 + j + 1)
                    nc.vector.reciprocal(rstd[:, 0:tt], rms[:, 0:tt]).then_inc(s["rstd"], 1)

                def normed(h, j):
                    dve.wait_ge(s["bc"], h * 2 + j + 2)
                    if j == 0:
                        dve.wait_ge(s["rot"], h + 2)
                    dst, src, n = ((xg, xg, LAT), (kn, kx, T))[j]
                    nc.vector.tensor_tensor(dst[0:QK1, :], src[0:QK1, :], e.ps[0:QK1, RB:RB + n],
                                            ALU.mult).then_inc(s["nrm"], 1)

                def low(h, j):
                    dve.wait_ge(s["hi"], h * 2 + j + 1)
                    dst, src, hi = ((ql, xg, qh), (kl, kn, kh))[j]
                    nc.vector.tensor_tensor(dst[0:QK1, :], src[0:QK1, :], hi[0:QK1, :].bitcast(F32),
                                            ALU.subtract).then_inc(s["lo"], 1)

                def vlow(h, c):
                    t0, n = VCH[c]
                    dve.wait_ge(s["vhi"], h * 2 + c + 1)
                    nc.vector.tensor_tensor(vs[:, t0:t0 + n, 1, :], e.ps[:, TR:TR + n * 64].rearrange("p (t v) -> p t v", v=64),
                                            vs[:, t0:t0 + n, 0, :].bitcast(F32), ALU.subtract).then_inc(s["vlo"], 1)

                with each(dve, p.iters) as i:
                    for x in range(2):
                        h = i * 2 + x
                        recip(h, 0)
                        vlow(h, 0)
                        normed(h, 0)
                        recip(h, 1)
                        low(h, 0)
                        vlow(h, 1)
                        normed(h, 1)
                        low(h, 1)


def attention1(e, oh, ol):
    nc, S = e.nc, e.scratch
    with ExitStack() as ctx:
        sb, sem = e.phase(ctx)
        qs = sb("a1_q", [128, 2, 2, LAT], F32R)
        ks = sb("a1_k", [128, 2, 2, T], F32R)
        vs = sb("a1_v", [128, 2, TT, 2 * VD1], F32R)
        pd = sb("a1_pd", [128, 8, T], F32)
        pth, ptl = sb("a1_pth", [128, 2, BANK], F32R), sb("a1_ptl", [128, 2, BANK], F32R)
        part = sb("a1_part", [64, BANK], F32)
        whole = sb("a1_whole", [128, BANK], F32)
        nb, rs, rr = sb("a1_negmax", [128, 8], F32), sb("a1_sum", [128, 8], F32), sb("a1_recip", [128, 8], F32)
        s = {x: sem("a1_" + x) for x in ("qk0", "qk1", "v0", "v1", "scores", "max", "exp", "rec", "comb", "turn", "hi", "lo",
                                         "pv", "part", "whole", "ohi", "out")}
        TB, OB = 6 * BANK, 7 * BANK
        NQ, NK, PAIRS = 8, 20, HEADS1 // 2 - 1

        def walk(eng, step):
            def head(h, par, tiles):
                for q, keys in SLOTS1:
                    step(h, par, tiles, q, [k for k in keys if k >= 0 or tiles[1] is not None])
            head(0, 0, (0, None))
            with each(eng, PAIRS) as i:
                head(i * 2 + 1, 1, (i, i))
                head(i * 2 + 2, 0, (i + 1, i))
            last = HEADS1 // 2 - 1
            head(HEADS1 - 1, 1, (last, last))
            for q, keys in TAIL1:
                step(HEADS1 - 1, 1, (last, last), q, keys)

        with nc.Block() as block:
            @block.sync
            def _(sp):
                e.clear_old(sp)
                free_at_start(sp, [(s["exp"], 2), (s["comb"], 1), (s["turn"], 1), (s["pv"], 2), (s["lo"], 1), (s["part"], 1),
                                   (s["whole"], 1), (s["out"], 1)])

                def load(h, par, first):
                    if not first:
                        sp.wait_ge(s["scores"], h * NQ - NQ)
                    for x in range(2):
                        sp.dma_start(qs[0:QK1, par, x, :].bitcast(F32), S["q1"][bass.ds(h * 2 + x, 1), :, :]
                                     .rearrange("o p t -> p (o t)")).then_inc(s[f"qk{par}"], 16)
                        sp.dma_start(ks[0:QK1, par, x, :].bitcast(F32), S["k1"][bass.ds(h * 2 + x, 1), :, :]
                                     .rearrange("o p t -> p (o t)")).then_inc(s[f"qk{par}"], 16)
                    if not first:
                        sp.wait_ge(s["pv"], h * NK - NK + 2)
                    sp.dma_start(vs[:, par, :, :].rearrange("p t v -> p (t v)").bitcast(F32),
                                 S["v1"][bass.ds(h, 1), :, :].rearrange("o p f -> p (o f)")).then_inc(s[f"v{par}"], 16)

                load(0, 0, True)
                load(1, 1, True)
                with each(sp, PAIRS) as i:
                    load(i * 2 + 2, 0, False)
                    load(i * 2 + 3, 1, False)

            @block.tensor
            def _(pe):
                def score(h, par, q, c):
                    a, w = CHUNKS[c]
                    if q == 0 and c == 0:
                        pe.wait_ge(s[f"qk{par}"], (h - par) * 32 + 64)
                    if c == 0:
                        pe.wait_ge(s["exp"], h * NQ + q + 1)
                    o = e.ps[:, (q % 2) * 3 * BANK + a:(q % 2) * 3 * BANK + a + w]
                    qh_, ql_ = (qs[0:QK1, par, x, q * 128:(q + 1) * 128] for x in range(2))
                    kh_, kl_ = (ks[0:QK1, par, x, a:a + w] for x in range(2))
                    last = products(nc, o, [(qh_, ql_, kh_, kl_)])
                    if c == 2:
                        last.then_inc(s["scores"], 1)

                def turn(h, k):
                    unit, kk = k // 10, k % 10
                    if kk == 0:
                        pe.wait_ge(s["comb"], h * NQ + unit * 4 + 4 + 1)
                    pe.wait_ge(s["lo"], h * NK + k + 1)
                    for x in range(4):
                        last = nc.tensor.transpose(e.ps[:, TB + x * 128:TB + (x + 1) * 128],
                                                   pd[:, 4 * (unit % 2) + x, kk * 128:(kk + 1) * 128], e.ident[:])
                    last.then_inc(s["turn"], 1)

                def value(h, par, k):
                    unit, kk = k // 10, k % 10
                    if k < 0:
                        par = 1 - par
                    if kk == 0:
                        if unit % 2 == 0:
                            pe.wait_ge(s[f"v{par}"], (h - par) * 8 + 16)
                        pe.wait_ge(s["part"], h * 2 + unit + 1)
                        pe.wait_ge(s["whole"], h * 2 + unit + 1)
                    pe.wait_ge(s["lo"], h * NK + k + 2)
                    v = vs[:, par, kk, :]
                    nc.tensor.matmul(e.ps[:, OB:OB + BANK], v, pth[:, k % 2, :], start=kk == 0, stop=False)
                    nc.tensor.matmul(e.ps[:, OB:OB + BANK], v, ptl[:, k % 2, :], start=False, stop=kk == 9).then_inc(s["pv"], 1)

                def step(h, par, tiles, q, keys):
                    first = [] if q is None else [(score, h, par, q, c) for c in range(3)]
                    second = []
                    for k in keys:
                        second.append((turn, h, k))
                        if k or tiles[1] is not None:
                            second.append((value, h, par, k - 1))
                    for f, *args in alternate(first, second):
                        f(*args)

                walk(pe, step)
                value(HEADS1 - 1, 1, NK - 1)

            def place(buf, par, tiles, u):
                tok = (u % 2) * BANK
                tile = tiles[1] if u < 0 else tiles[0]
                return buf[64 * par:64 * par + 64, bass.ds(tile, 1), tok:tok + BANK].rearrange("p o t -> p (o t)")

            @block.vector
            def _(dve):
                def step(h, par, tiles, q, keys):
                    for k in keys:
                        dve.wait_ge(s["hi"], h * NK + k + 1)
                        nc.vector.tensor_tensor(ptl[:, k % 2, :], e.ps[:, TB:TB + BANK], pth[:, k % 2, :].bitcast(F32),
                                                ALU.subtract).then_inc(s["lo"], 1)
                        if k % 10 == 0 and (k or tiles[1] is not None):
                            finish(h, par, tiles, k // 10 - 1)
                    if q is None:
                        return
                    dve.wait_ge(s["scores"], h * NQ + q + 1)
                    nc.vector.tensor_reduce(nb[:, q:q + 1], e.ps[:, (q % 2) * 3 * BANK:(q % 2) * 3 * BANK + T], AX.X,
                                            ALU.max, negate=True).then_inc(s["max"], 1)
                    dve.wait_ge(s["exp"], h * NQ + q + 1 + 2)
                    nc.vector.reciprocal(rr[:, q:q + 1], rs[:, q:q + 1]).then_inc(s["rec"], 1)

                def finish(h, par, tiles, u):
                    if u < 0:
                        par = 1 - par
                    n = h * 2 + u
                    r = slice(64 * par, 64 * par + 64)
                    dve.wait_ge(s["part"], n + 2)
                    dve.wait_ge(s["out"], n + 1)
                    nc.vector.tensor_tensor(whole[r, :], e.ps[0:64, OB:OB + BANK], part[:, :], ALU.add).then_inc(s["whole"], 1)
                    dve.wait_ge(s["ohi"], n + 1)
                    o = place(ol, par, tiles, u)
                    nc.vector.tensor_tensor(o, whole[r, :], place(oh, par, tiles, u).bitcast(F32), ALU.subtract).then_inc(s["out"], 1)

                walk(dve, step)
                finish(HEADS1 - 1, 1, (HEADS1 // 2 - 1,) * 2, 1)
                dve.wait_ge(s["out"], 2 * HEADS1 + 1)

            @block.scalar
            def _(act):
                def step(h, par, tiles, q, keys):
                    for k in keys:
                        act.wait_ge(s["turn"], h * NK + k + 2)
                        act.wait_ge(s["pv"], h * NK + k + 1)
                        nc.scalar.activation(pth[:, k % 2, :], e.ps[:, TB:TB + BANK], ACT.Copy).then_inc(s["hi"], 1)
                        if k % 10 == 0 and (k or tiles[1] is not None):
                            finish(h, par, tiles, k // 10 - 1)
                    if q is None:
                        return
                    if q in (0, 4) and tiles[1] is not None:
                        act.wait_ge(s["turn"], h * NK - NK + 10 + (q // 4) * 10 + 1)
                    act.wait_ge(s["max"], h * NQ + q + 1)
                    nc.scalar.activation(pd[:, q, :], e.ps[:, (q % 2) * 3 * BANK:(q % 2) * 3 * BANK + T], ACT.Exp,
                                         bias=nb[:, q:q + 1], accum_out=rs[:, q:q + 1]).then_inc(s["exp"], 1)

                def finish(h, par, tiles, u):
                    if u < 0:
                        par = 1 - par
                    n = h * 2 + u
                    k = (u + 1) * 10
                    act.wait_ge(s["pv"], h * NK + k + 2)
                    act.wait_ge(s["whole"], n + 1)
                    nc.scalar.activation(part[:, :], e.ps[64:128, OB:OB + BANK], ACT.Copy).then_inc(s["part"], 1)
                    act.wait_ge(s["whole"], n + 2)
                    nc.scalar.activation(place(oh, par, tiles, u), whole[64 * par:64 * par + 64, :], ACT.Copy).then_inc(s["ohi"], 1)

                walk(act, step)
                finish(HEADS1 - 1, 1, (HEADS1 // 2 - 1,) * 2, 1)

            @block.gpsimd
            def _(pool):
                with each(pool, HEADS1) as h:
                    for q in range(NQ):
                        pool.wait_ge(s["comb"], h * NQ + q + 1)
                        pool.wait_ge(s["rec"], h * NQ + q + 1)
                        settle_pool(e)
                        nc.gpsimd.tensor_scalar(pd[:, q, :], pd[:, q, :], rr[:, q:q + 1], None,
                                                ALU.mult).then_inc(s["comb"], 1)


def program(nc, dram, out):
    e = Env(nc, dram)
    stream = Stream()
    top = ExitStack()

    with top:
        sb = e.sbuf(top)

        def sem(name):
            return top.enter_context(nc.semaphore(name))

        e.scratch = {n: nc.dram_tensor("scratch_" + n, shape, dt, kind="Internal").ap() for n, shape, dt in (
            ("q0", (HEADS0 * 4, HD0, T), F32), ("k0", (HEADS0 * 4, HD0, T), F32),
            ("v0", (HEADS0, 128, TT * 2 * VD0), F32), ("u0", (HEADS0, 128, T), F32),
            ("q1", (HEADS1 * 2, QK1, LAT), F32), ("k1", (HEADS1 * 2, QK1, T), F32),
            ("v1", (HEADS1, 128, TT * 2 * VD1), F32))}
        e.ps = top.enter_context(nc.psum_tensor("ps", [128, 8 * BANK], F32))
        e.vec, e.ident, e.sel = sb("vec", [128, NVEC], F32), sb("ident", [128, 128], F32), sb("sel", [128, 130], F32)
        e.eps, e.neg_lam, e.subln = sb("eps", [128, 1], F32), sb("neg_lam", [128, 1], F32), sb("subln", [128, 1], F32)
        e.qg0, e.qg1 = sb("qg0", [128, 1], F32), sb("qg1", [128, 1], F32)
        e.spare = sb("spare", [128, 1], F32)
        e.mod = sb("mod", [128, DEPTH * 48, 2], F32)
        e.gain = sb("gain", [128, 4, KT, 2], F32)
        e.consts, stored = sem("consts"), sem("stored")
        e.raw_full = [sem(f"raw_full{i}") for i in range(4)]
        e.split_hi, e.split_done, e.w_used = sem("split_hi"), sem("split_done"), sem("w_used")

        def rings(ctx, slots=4, width=1024, split=True):
            new = e.sbuf(ctx)
            e.raw = new(f"raw{stream.n}", [128, slots, width], F32)
            if split:
                e.whi = new(f"whi{stream.n}", [128, slots, width], F32R)
                e.wlo = new(f"wlo{stream.n}", [128, slots, width], F32R)

        e.rings = rings
        with ExitStack() as c:
            rings(c, split=False)
            modulation(e, dram["mod_w"])
        with nc.Block() as block:
            @block.gpsimd
            def _(pool):
                pool.sem_inc(e.split_done, RING)

            @block.tensor
            def _(pe):
                pe.sem_inc(e.w_used, RING)

        def acts(c, name, n_tok=T, tiles=KT):
            return (e.sbuf(c)(name + "_hi", [128, tiles, n_tok], F32R), e.sbuf(c)(name + "_lo", [128, tiles, n_tok], F32R))

        def adaln(name, h, hi, lo, which, layer, part, n_tok=T, load=None):
            ranges = RANGES if n_tok == T else RANGES[:1]
            norm(e, name, lambda k: h[:, k, 0:n_tok], [list(range(KT))], D,
                 lambda k, c: e.gain[:, which, k, c:c + 1],
                 lambda k, c: e.mod[:, layer * 48 + part * 8 + k, c:c + 1],
                 lambda k: hi[:, k, :], lambda k: lo[:, k, :], ranges, load)

        with ExitStack() as c:
            hi, lo = acts(c, "mix0")
            with ExitStack() as c2:
                x = e.sbuf(c2)("x0", [128, KT, T], F32)
                adaln("norm_mix0", x, hi, lo, 0, 0, 0, load=lambda k: dram["x"][k, :, :])
            project0(e, stream, hi, lo)
        h = sb("residual", [128, KT, T], F32)
        with ExitStack() as c:
            ot = e.sbuf(c)("ot", [128, HEADS0, T], F32)
            attention0(e, ot)
            hi, lo = acts(c, "mixed0")
            norm(e, "norm_sub", lambda k: ot[:, k, :], [[k] for k in range(HEADS0)], VD0,
                 lambda k, c_: e.subln[:, 0:1], None, lambda k: hi[:, 4 + k, :], lambda k: lo[:, 4 + k, :], ((0, T, 0),))
            pool_mixer(e, hi, lo)

            def load_x(sp, loaded):
                for k in range(KT):
                    sp.dma_start(h[:, k, :], dram["x"][k, :, :]).then_inc(loaded, 16)

            mix_out(e, "out0", stream, h, lambda k, a, w: (hi[:, k, a:a + w], lo[:, k, a:a + w]), T, dram["w_out0"], 0,
                    load_x)
        with ExitStack() as c:
            hi, lo = acts(c, "ffn0_in")
            adaln("norm_ffn0", h, hi, lo, 1, 0, 3)
            ffn(e, "ffn0", stream, h, hi, lo, T, dram["w_ffn"][0], 0)

        with ExitStack() as c:
            new = e.sbuf(c)
            kx, ksq = new("kx", [128, T], F32), new("ksq", [128, T], F32)
            cos, sin = new("cos1", [128, LAT], F32), new("sin1", [128, LAT], F32)
            cq, ck = new("cq", [128, Q_RANK // 128, LAT], F32), new("ck", [128, KV_RANK // 128, T], F32)
            with ExitStack() as c2:
                hi, lo = acts(c2, "mix1")
                adaln("norm_mix1", h, hi, lo, 2, 1, 0)
                latents1(e, stream, hi, lo, cq, ck, kx, ksq, cos, sin)
            cqh, cql = acts(c, "cq", LAT, Q_RANK // 128)
            ckh, ckl = acts(c, "ck", T, KV_RANK // 128)
            qg, kg = VEC["qlat_g"][0], VEC["kvlat_g"][0]
            norm(e, "norm_q", lambda k: cq[:, k, :], [[0, 1, 2]], Q_RANK, lambda k, c_: e.vec[:, qg + k:qg + k + 1], None,
                 lambda k: cqh[:, k, :], lambda k: cql[:, k, :], ((0, LAT, 0),))
            norm(e, "norm_kv", lambda k: ck[:, k, :], [[0, 1]], KV_RANK, lambda k, c_: e.vec[:, kg + k:kg + k + 1], None,
                 lambda k: ckh[:, k, :], lambda k: ckl[:, k, :], ((0, T, 0),))
            heads1(e, stream, cqh, cql, ckh, ckl, kx, ksq, cos, sin)
        with ExitStack() as c:
            oh, ol = acts(c, "o1", LAT)
            attention1(e, oh, ol)
            mix_out(e, "out1", stream, h, lambda k, a, w: (oh[:, k, a:a + w], ol[:, k, a:a + w]), LAT, dram["w_out1"], 1)
        with ExitStack() as c:
            hi, lo = acts(c, "ffn1_in", LAT)
            adaln("norm_ffn1", h, hi, lo, 3, 1, 3, LAT)
            ffn(e, "ffn1", stream, h, hi, lo, LAT, dram["w_ffn"][1], 1)
        with nc.Block() as block:
            @block.sync
            def _(sp):
                for k in range(KT):
                    sp.dma_start(out[k, :, :], h[:, k, 0:LAT]).then_inc(stored, 16)
                sp.wait_ge(stored, 16 * KT)


def _rope(rot_dim):
    n = rot_dim // 4
    freqs = (10000.0 ** (-np.arange(n, dtype=np.float32) / n)).astype(np.float32)
    t = np.arange(LAT)
    row, col = (t // GRID_W).astype(np.float32), (t % GRID_W).astype(np.float32)
    ang = np.concatenate([freqs[:, None] * row, freqs[:, None] * col], axis=0)
    cos, sin = np.cos(ang), np.sin(ang)
    return np.concatenate([cos, cos]).astype(np.float32), np.concatenate([-sin, sin]).astype(np.float32)


def _edges():
    out = np.ones((len(WINDOWS), 2 * PAD), np.float32)
    for g, w in enumerate(WINDOWS):
        for t in range(PAD):
            out[g, t] = w / (t + w // 2 - max(t - w // 2, 0))
            left = PAD - t
            out[g, PAD + t] = w / (w // 2 + min(w // 2, left))
    return out


def _columns(w, cols=128):
    k, m = w.shape
    return np.ascontiguousarray(w.reshape(k // 128, 128, m // cols, cols).transpose(2, 1, 0, 3).reshape(m // cols, 128, -1))


def _feature_major(v):
    return v.reshape(-1, 128).T


def _lay_out(i):
    A = {k: np.asarray(v) for k, v in i.items()}
    d = {}
    d["x"] = np.ascontiguousarray(np.concatenate([A["x"][0], A["ctx"][0]]).T.reshape(KT, 128, T))
    d["mod_w"] = np.ascontiguousarray(
        A["mod_w"].reshape(DEPTH, 4, 2, 128, 12, 512).transpose(0, 4, 1, 3, 2, 5).reshape(DEPTH * 48, 128, 1024))
    w = A["ab_w_in"][0]
    cols = [c for h in range(HEADS0) for c in (512 + 128 * h, 1024 + 128 * h, 1536 + 128 * h, 128 * h)]
    d["w_in"] = np.concatenate([_columns(w[:, c:c + 128]) for c in cols])
    d["w_out0"], d["w_out1"] = _columns(A["ab_w_out"][0]), _columns(A["mla_w_out"][0])
    order = [("g", 0), ("u", 0), ("g", 1), ("u", 1)]
    for p in range(1, HT // 2):
        order += [("g", 2 * p), ("d", 2 * p - 2), ("d", 2 * p - 1), ("u", 2 * p), ("g", 2 * p + 1), ("u", 2 * p + 1)]
    order += [("d", HT - 2), ("d", HT - 1)]
    ffn_w = []
    for layer in range(DEPTH):
        parts = {"g": _columns(A["ffn_w_gate"][layer]), "u": _columns(A["ffn_w_up"][layer]),
                 "d": A["ffn_w_down"][layer].reshape(HT, 128, D)}
        ffn_w.append(np.stack([parts[k][m] for k, m in order]))
    d["w_ffn"] = np.stack(ffn_w)
    kv = A["mla_w_dkv"][0]
    d["w_down1"] = np.concatenate([_columns(A["mla_w_dq"][0]), _columns(kv[:, :KV_RANK]),
                                   _columns(np.tile(kv[:, KV_RANK:], (1, 4)))])
    uq = A["mla_w_uq"][0].reshape(Q_RANK, HEADS1, QK1)
    uq = np.concatenate([uq, uq[:, :, :128 - QK1]], axis=2).reshape(Q_RANK, HEADS1 * 128)
    d["w_uq"], d["w_ukv"] = _columns(uq), _columns(A["mla_w_ukv"][0])
    d["pool_w"] = np.ascontiguousarray(A["pool_w"][0].transpose(1, 0, 2))
    d["pool_edge"] = np.ascontiguousarray(np.broadcast_to(_edges(), (128, len(WINDOWS), 2 * PAD)))
    vec = np.zeros((128, NVEC), np.float32)

    def put(name, v):
        a, b = VEC[name]
        vec[:v.shape[0], a:b] = v

    put("cond", np.stack([A["c"][0].reshape(KT, 128), A["c_ctx"].reshape(KT, 128)], axis=1).reshape(2 * KT, 128).T)
    for name, key in (("mod_b", "mod_b"), ("mix_g", "norm_mix_g"), ("ffn_g", "norm_ffn_g"), ("pool_scale", "pool_scale"),
                      ("subln_g", "diff_subln_g"), ("qlat_g", "mla_q_lat_g"), ("kvlat_g", "mla_kv_lat_g")):
        put(name, _feature_major(A[key]))
    for name, key in (("q_g0", "diff_q_norm_g"), ("k_g0", "diff_k_norm_g")):
        put(name, np.tile(A[key][0], 2)[:, None])
    for name, key in (("q_g1", "mla_q_norm_g"), ("k_g1", "mla_k_norm_g")):
        put(name, A[key][0][:, None])
    put("lam", np.stack([A["diff_lam_q1"][0], A["diff_lam_q2"][0], A["diff_lam_k1"][0], A["diff_lam_k2"][0]], axis=1))
    d["vec"] = vec
    d["ident"] = np.eye(128, dtype=np.float32)
    sel = np.ones((128, 130), np.float32)
    sel[64:, 0] = 0
    sel[:64, 1] = 0
    d["sel"] = sel
    c0, s0 = _rope(HD0)
    d["cos0"], d["sin0"] = np.concatenate([c0, c0]), np.concatenate([s0, s0])
    d["cos1"], d["sin1"] = _rope(ROPE)
    return {k: np.ascontiguousarray(v) for k, v in d.items()}


def kernel(**inputs):
    import concourse.bacc as bacc
    from concourse.bass_utils import run_bass_kernel_spmd

    nc = bacc.Bacc("TRN2", target_bir_lowering=False, num_devices=1)
    arrays = _lay_out(inputs)
    dram = {k: nc.dram_tensor("in_" + k, v.shape, mybir.dt.from_np(v.dtype), kind="ExternalInput").ap()
            for k, v in arrays.items()}
    out = nc.dram_tensor("out_0", (KT, 128, LAT), F32, kind="ExternalOutput").ap()
    program(nc, dram, out)
    r = run_bass_kernel_spmd(nc, [{"in_" + k: v for k, v in arrays.items()}], core_ids=[0])
    return np.ascontiguousarray(r.results[0]["out_0"].reshape(1, D, LAT).transpose(0, 2, 1))
```

```python
from contextlib import ExitStack

import numpy as np

import concourse.bass as bass
from concourse import mybir

F32 = mybir.dt.float32
F32R = mybir.dt.float32r
ALU = mybir.AluOpType
ACT = mybir.ActivationFunctionType
AX = mybir.AxisListType

D = 1024
KT = D // 128
LAT, CTX = 1024, 256
T = LAT + CTX
DEPTH = 2
EPS = 1e-6
GRID_W = 64
HEADS0, HD0 = 4, 64
VD0 = 2 * HD0
HEADS1, NOPE, ROPE, VD1 = 16, 64, 32, 64
QK1 = NOPE + ROPE
Q_RANK, KV_RANK = 384, 256
HIDDEN = 2816
HT = HIDDEN // 128
WINDOWS = (2, 4, 8, 16)
PAD = 16
LAM_INIT = 0.8 - 0.6
BANK = 512
CHUNKS = ((0, 512), (512, 512), (1024, 256))
RANGES = ((0, LAT, 0), (LAT, T, 1))
TT = T // 128
QT = LAT // 128

VEC = {}


def _vec_columns():
    at = 0
    for name, n in (("cond", 2 * KT), ("mod_b", DEPTH * 6 * KT), ("mix_g", DEPTH * KT), ("ffn_g", DEPTH * KT),
                    ("pool_scale", 4), ("q_g0", 1), ("k_g0", 1), ("subln_g", 1), ("qlat_g", 3), ("kvlat_g", 2),
                    ("q_g1", 1), ("k_g1", 1), ("lam", 4)):
        VEC[name] = (at, at + n)
        at += n
    return at


NVEC = _vec_columns()


class Piece:

    def __init__(self, stream, slots, iters):
        self.slots, self.iters, self.n0, self.uses0 = slots, iters, stream.n, list(stream.uses)
        stream.n += len(slots) * iters
        for s in slots:
            stream.uses[s] += iters

    def number(self, i, j):
        return i * len(self.slots) + (self.n0 + j)

    def filled(self, i, j):
        s = self.slots[j]
        return i * (16 * self.slots.count(s)) + 16 * (self.uses0[s] + self.slots[:j].count(s) + 1)


class Stream:

    def __init__(self):
        self.n, self.uses = 0, [0, 0, 0, 0]


RING = 3


class Env:

    def __init__(self, nc, dram):
        self.nc, self.dram = nc, dram
        self.live, self.clearing = [], []

    def sbuf(self, ctx):
        return lambda name, shape, dt: ctx.enter_context(self.nc.sbuf_tensor(name, shape, dt))

    def phase(self, ctx):
        for h in self.clearing:
            self.nc.release_semaphore(h)
        self.clearing, self.live = self.live, []

        def sem(name):
            self.live.append(self.nc.alloc_semaphore(name=name))
            return self.live[-1]

        return self.sbuf(ctx), sem

    def clear_old(self, sp):
        for h in self.clearing:
            sp.sem_clear(h)


def each(eng, n):
    return eng.Fori(0, n)


def load_block(e, sp, p, i, j, src):
    sp.wait_ge(e.split_done, p.number(i, j) + 1)
    s = p.slots[j]
    sp.dma_start(e.raw[:, s, 0:src.shape[1]], src).then_inc(e.raw_full[s], 16)


def settle_pool(e):
    e.nc.gpsimd.tensor_tensor(e.spare[:, 0:1], e.ident[:, 0:1], e.ident[:, 0:1], ALU.mult)


def settle_pe(e, col):
    e.nc.tensor.matmul(e.ps[:, col:col + 1], e.ident[:], e.ident[:, 0:1], start=True, stop=True)


def split_block(e, pool, p, i, j, n):
    nc, s, num = e.nc, p.slots[j], p.number(i, j)
    pool.wait_ge(e.raw_full[s], p.filled(i, j))
    pool.wait_ge(e.w_used, num + 1)
    settle_pool(e)
    nc.gpsimd.tensor_scalar(e.whi[:, s, 0:n], e.raw[:, s, 0:n], 1.0, 1.0, ALU.mult, ALU.mult).then_inc(e.split_hi, 1)
    pool.wait_ge(e.split_hi, num + 1)
    nc.gpsimd.tensor_tensor(e.wlo[:, s, 0:n], e.raw[:, s, 0:n], e.whi[:, s, 0:n].bitcast(F32),
                            ALU.subtract).then_inc(e.split_done, 1)


def block_ready(e, pe, p, i, j):
    pe.wait_ge(e.split_done, p.number(i, j) + 1 + RING)


def block_used(e, eng, p, i, j):
    eng.wait_ge(e.w_used, p.number(i, j) + 1 + RING)


def free_at_start(eng, counts):
    for s, n in counts:
        eng.sem_inc(s, n)


def products(nc, out, pairs):
    n = 3 * len(pairs)
    at = 0
    for sh, sl, mh, ml in pairs:
        for a, b in ((sh, mh), (sh, ml), (sl, mh)):
            last = nc.tensor.matmul(out, a, b, start=at == 0, stop=at == n - 1)
            at += 1
    return last


def weight_pairs(e, s, m, acts, kt=KT):
    w = lambda buf, k: buf[:, s, k * m:(k + 1) * m]
    return [(w(e.whi, k), w(e.wlo, k), *acts(k)) for k in range(kt)]


def modulation(e, mod_w):
    nc = e.nc
    with ExitStack() as ctx:
        sb, sem = e.phase(ctx)
        silu_c = sb("silu_c", [128, KT, 2], F32)
        cond = sb("mod_cond", [128, KT, 4], F32R)
        rows = sb("mod_rows", [4, 3, 512], F32)
        whi, wlo = sb("mod_whi", [128, 4, 1024], F32R), sb("mod_wlo", [128, 4, 1024], F32R)
        split_hi, split_lo, summed, cond_done = sem("mod_split_hi"), sem("mod_split_lo"), sem("mod_summed"), sem("mod_cond_done")
        full = [sem(f"mod_full{j}") for j in range(12)]
        used, acc_done, acc_free = sem("mod_used"), sem("mod_acc_done"), sem("mod_acc_free")
        turned, turned_free, silu_done, gains = sem("mod_turned"), sem("mod_turned_free"), sem("silu_done"), sem("mod_gains")
        lam_p, lam_s, lam_e, lam_d = sem("lam_prod"), sem("lam_sum"), sem("lam_exp"), sem("lam_diff")
        prod = sb("lam_products", [128, 2], F32)
        lexp = sb("lam_exps", [128, 2], F32)
        ldif = sb("lam_difference", [128, 1], F32)
        iters = DEPTH * 12 // 3
        with nc.Block() as block:
            @block.sync
            def _(sp):
                e.clear_old(sp)
                sp.dma_start(e.vec[:], e.dram["vec"]).then_inc(e.consts, 16)
                sp.dma_start(e.ident[:], e.dram["ident"]).then_inc(e.consts, 16)
                sp.dma_start(e.sel[:], e.dram["sel"]).then_inc(e.consts, 16)
                with each(sp, iters) as i:
                    for j in range(12):
                        sp.wait_ge(split_lo, i * 12 + j + 1)
                        sp.dma_start(e.raw[:, j, :],
                                     mod_w[bass.ds(i * 12 + j, 1), :, :].rearrange("o p f -> p (o f)"))\
                          .then_inc(full[j], 16)

            @block.scalar
            def _(act):
                act.wait_ge(e.consts, 48)
                a, b = VEC["cond"]
                nc.scalar.activation(silu_c[:, :, :], e.vec[:, a:b].rearrange("p (k c) -> p k c", c=2),
                                     ACT.Silu).then_inc(silu_done, 1)
                act.wait_ge(lam_s, 1)
                nc.scalar.activation(lexp[:], e.ps[:, 7 * BANK:7 * BANK + 2], ACT.Exp).then_inc(lam_e, 1)
                act.wait_ge(silu_done, 1)
                nc.scalar.activation(cond[:, :, 0:2], silu_c[:, :, :], ACT.Copy).then_inc(cond_done, 1)

                def copy_rows(i, j):
                    act.wait_ge(acc_done, i * 3 + j + 2)
                    if j == 0:
                        act.wait_ge(turned, i + 1)
                    nc.scalar.activation(rows[:, j, :], e.ps[0:4, j * BANK:(j + 1) * BANK],
                                         ACT.Copy).then_inc(acc_free, 1)

                with each(act, iters) as i:
                    for j in range(12):
                        act.wait_ge(full[j], i * 16 + 16)
                        if j % 4 < 3:
                            act.wait_ge(used, i * 9 + j // 4 * 3 + j % 4 + 1)
                        else:
                            act.wait_ge(acc_done, i * 3 + j // 4 + 1)
                        nc.scalar.activation(whi[:, j % 4, :], e.raw[:, j, :], ACT.Copy).then_inc(split_hi, 1)
                        if j in (7, 11):
                            copy_rows(i, j // 4 - 1)
                    copy_rows(i, 2)

            @block.tensor
            def _(pe):
                pe.sem_inc(used, 3)
                pe.sem_inc(acc_done, 1)
                pe.sem_inc(turned, 1)
                pe.wait_ge(lam_p, 1)
                nc.tensor.matmul(e.ps[:, 7 * BANK:7 * BANK + 2], e.sel[0:64, 2:130], prod[0:64, :],
                                 start=True, stop=True).then_inc(lam_s, 1)
                pe.wait_ge(cond_done, 2)
                with each(pe, iters) as i:
                    for j in range(12):
                        pe.wait_ge(split_lo, i * 12 + j + 1 + 12)
                        if j % 4 == 0:
                            pe.wait_ge(acc_free, i * 3 + j // 4 + 1)
                        for kk in range(2):
                            k = (j % 4) * 2 + kk
                            bank = slice((j // 4) * BANK, (j // 4 + 1) * BANK)
                            cols = slice(kk * 512, (kk + 1) * 512)
                            parts = ((whi, 4), (wlo, 2)) if k == 0 else ((wlo, 2), (whi, 4))
                            for w, m in parts:
                                last = nc.tensor.matmul(e.ps[0:m, bank], cond[:, k, 0:m], w[:, j % 4, cols],
                                                        start=k == 0 and w is whi, stop=k == KT - 1 and w is whi)
                        last.then_inc(used if j % 4 < 3 else acc_done, 1)
                    pe.wait_ge(turned_free, i + 1)
                    pe.wait_ge(acc_free, i * 3 + 3 + 3)
                    settle_pe(e, 6 * BANK)
                    for j in range(3):
                        for q in range(4):
                            last = nc.tensor.transpose(e.ps[:, 6 * BANK + (j * 4 + q) * 4:6 * BANK + (j * 4 + q) * 4 + 4],
                                                       rows[:, j, q * 128:(q + 1) * 128], e.ident[0:4, 0:4])
                    last.then_inc(turned, 1)

            @block.vector
            def _(dve):
                dve.sem_inc(turned_free, 1)
                dve.sem_inc(acc_free, 3)
                dve.sem_inc(split_lo, 12)
                dve.wait_ge(e.consts, 48)
                a, _b = VEC["lam"]
                nc.vector.memset(e.eps[:], EPS).then_inc(gains, 1)
                nc.vector.tensor_tensor(prod[:], e.vec[:, a:a + 2], e.vec[:, a + 2:a + 4], ALU.mult).then_inc(lam_p, 1)
                dve.wait_ge(lam_e, 1)
                nc.vector.tensor_tensor(ldif[:], lexp[:, 1:2], lexp[:, 0:1], ALU.subtract).then_inc(lam_d, 1)
                dve.wait_ge(lam_d, 1)
                nc.vector.tensor_scalar(e.neg_lam[:], ldif[:], -LAM_INIT, None, ALU.add).then_inc(gains, 1)
                a, b = VEC["subln_g"]
                nc.vector.tensor_scalar(e.subln[:], e.vec[:, a:b], 1.0 - LAM_INIT, None, ALU.mult).then_inc(gains, 1)
                a, b = VEC["q_g0"]
                nc.vector.tensor_scalar(e.qg0[:], e.vec[:, a:b], HD0 ** -0.5, None, ALU.mult).then_inc(gains, 1)
                a, b = VEC["q_g1"]
                nc.vector.tensor_scalar(e.qg1[:], e.vec[:, a:b], QK1 ** -0.5, None, ALU.mult).then_inc(gains, 1)
                a, _b = VEC["mod_b"]
                dve.wait_ge(silu_done, 1)
                dve.wait_ge(cond_done, 1)
                nc.vector.tensor_tensor(cond[:, :, 2:4], silu_c[:, :, :], cond[:, :, 0:2].bitcast(F32),
                                        ALU.subtract).then_inc(cond_done, 1)
                with each(dve, iters) as i:
                    for j in range(12):
                        dve.wait_ge(split_hi, i * 12 + j + 1)
                        nc.vector.tensor_tensor(wlo[:, j % 4, :], e.raw[:, j, :], whi[:, j % 4, :].bitcast(F32),
                                                ALU.subtract).then_inc(split_lo, 1)
                    dve.wait_ge(turned, i + 2)
                    part = e.ps[:, 6 * BANK:6 * BANK + 48].rearrange("p (n c) -> p n c", c=4)
                    nc.vector.tensor_tensor(
                        e.mod[:, bass.ds(i * 12, 12), :], part[:, :, 0:2],
                        e.vec[:, bass.ds(i * 12 + a, 12)].rearrange("p (n o) -> p n o", o=1).broadcast_to([128, 12, 2]),
                        ALU.add).then_inc(summed, 1)
                    dve.wait_ge(summed, i + 1)
                    nc.vector.tensor_tensor(e.mod[:, bass.ds(i * 12, 12), :], e.mod[:, bass.ds(i * 12, 12), :],
                                            part[:, :, 2:4], ALU.add).then_inc(turned_free, 1)
                dve.wait_ge(turned_free, iters + 1)
                for n, (layer, part, g) in enumerate(((0, 1, "mix_g"), (0, 4, "ffn_g"), (1, 1, "mix_g"), (1, 4, "ffn_g"))):
                    a = VEC[g][0] + layer * KT
                    m = layer * 48 + part * 8
                    nc.vector.scalar_tensor_tensor(
                        e.gain[:, n, :, :], e.mod[:, m:m + 8, :], 1.0,
                        e.vec[:, a:a + 8].rearrange("p (n o) -> p n o", o=1).broadcast_to([128, 8, 2]),
                        ALU.add, ALU.mult).then_inc(gains, 1)
                dve.wait_ge(gains, 9)


def norm(e, name, src, groups, width, gain, shift, hi, lo, ranges, load=None, summed=False):
    nc = e.nc
    n_tok = ranges[-1][1]
    tt = n_tok // 128
    G = len(groups)
    order = [(g, k) for g, ks in enumerate(groups) for k in ks]
    nt = len(order)
    with ExitStack() as ctx:
        sb, sem = e.phase(ctx)
        B = 3
        if summed:
            acc = e.squares[:, 0:n_tok].rearrange("p (g t) -> p g t", g=1)
        else:
            sq = sb(f"{name}_sq", [128, B, n_tok], F32)
            acc = sb(f"{name}_acc", [128, min(G, 2), n_tok], F32)
        whole = sb(f"{name}_whole", [128, n_tok], F32)
        rms = sb(f"{name}_rms", [128, G * tt], F32)
        rstd = sb(f"{name}_rstd", [128, G * tt], F32)
        tmp = sb(f"{name}_tmp", [128, B, n_tok], F32)
        s = {x: sem(f"{name}_{x}") for x in ("sq", "acc", "sum", "rms", "rstd", "bc", "tmp", "hi", "whole", "lo0",
                                               "lo1")}
        arrived = [sem(f"{name}_in{k}") for k in range(nt if load else 0)]
        with nc.Block() as block:
            @block.sync
            def _(sp):
                for k in range(nt if load else 0):
                    sp.dma_start(src(k), load(k)).then_inc(arrived[k], 16)
                e.clear_old(sp)

            @block.scalar
            def _(act):
                for n, (g, k) in enumerate([] if summed else order):
                    if load:
                        act.wait_ge(arrived[n], 16)
                    if n >= B:
                        act.wait_ge(s["acc"], n - B + 1)
                    nc.scalar.activation(sq[:, n % B, :], src(k), ACT.Square).then_inc(s["sq"], 1)
                act.wait_ge(s["sum"], G)
                nc.scalar.activation(rms[:], e.ps[:, 7 * BANK:7 * BANK + G * tt], ACT.Sqrt,
                                     bias=e.eps[:, 0:1], scale=1.0 / width).then_inc(s["rms"], 1)
                for n, (g, k) in enumerate(order):
                    act.wait_ge(s["tmp"], n + 1)
                    kinds = [(hi(k), "hi")]
                    if n % 2:
                        if n >= 3:
                            act.wait_ge(s["lo1"], (n - 1) // 2)
                        kinds.append((whole, "whole"))
                    for dst, done in kinds:
                        for a, b, c in ranges:
                            if shift:
                                ins = nc.scalar.activation(dst[:, a:b], tmp[:, n % B, a:b], ACT.Identity, bias=shift(k, c))
                            else:
                                ins = nc.scalar.activation(dst[:, a:b], tmp[:, n % B, a:b], ACT.Copy)
                        ins.then_inc(s[done], 1)

            @block.gpsimd
            def _(pool):
                for n in range(1, nt, 2):
                    k = order[n][1]
                    pool.wait_ge(s["whole"], (n + 1) // 2)
                    nc.gpsimd.tensor_tensor(lo(k), whole[:, 0:n_tok], hi(k).bitcast(F32), ALU.subtract).then_inc(s["lo1"], 1)

            @block.tensor
            def _(pe):
                at = 0
                for g, ks in enumerate(groups):
                    at += len(ks)
                    if not summed:
                        pe.wait_ge(s["acc"], at)
                    for t in range(tt):
                        last = nc.tensor.matmul(e.ps[:, 7 * BANK + g * tt + t:7 * BANK + g * tt + t + 1],
                                                acc[:, g % 2, t * 128:(t + 1) * 128], e.sel[:, 2:3], start=True, stop=True)
                    last.then_inc(s["sum"], 1)
                pe.wait_ge(s["rstd"], 1)
                done = 0
                for g, ks in enumerate(groups):
                    if g >= 2:
                        pe.wait_ge(s["tmp"], done - len(groups[g - 1]))
                    for t in range(tt):
                        last = nc.tensor.transpose(e.ps[:, (g % 2) * 3 * BANK + t * 128:(g % 2) * 3 * BANK + t * 128 + 128],
                                                   rstd[:, g * tt + t:g * tt + t + 1].broadcast_to([128, 128]), e.ident[:])
                    last.then_inc(s["bc"], 1)
                    done += len(ks)

            @block.vector
            def _(dve):
                n = 0
                for g, ks in enumerate([] if summed else groups):
                    if g >= 2:
                        dve.wait_ge(s["sum"], g - 1)
                    for x, k in enumerate(ks):
                        dve.wait_ge(s["sq"], n + 1)
                        if x == 0:
                            ins = nc.vector.tensor_copy(acc[:, g % 2, :], sq[:, n % B, :])
                        else:
                            dve.wait_ge(s["acc"], n)
                            ins = nc.vector.tensor_tensor(acc[:, g % 2, :], acc[:, g % 2, :], sq[:, n % B, :], ALU.add)
                        ins.then_inc(s["acc"], 1)
                        n += 1
                dve.wait_ge(s["rms"], 1)
                nc.vector.reciprocal(rstd[:], rms[:]).then_inc(s["rstd"], 1)

                def scaled(n):
                    g, k = order[n]
                    dve.wait_ge(s["bc"], g + 1)
                    m = n - B
                    if m >= 0:
                        dve.wait_ge(s["whole" if m % 2 else "lo0"], m // 2 + 1)
                    for a, b, c in ranges:
                        ins = nc.vector.scalar_tensor_tensor(tmp[:, n % B, a:b], src(k)[:, a:b], gain(k, c),
                                                             e.ps[:, (g % 2) * 3 * BANK + a:(g % 2) * 3 * BANK + b],
                                                             ALU.mult, ALU.mult)
                    ins.then_inc(s["tmp"], 1)

                scaled(0)
                for n, (g, k) in enumerate(order):
                    if n + 1 < nt:
                        scaled(n + 1)
                    if n % 2:
                        continue
                    dve.wait_ge(s["hi"], n + 1)
                    for a, b, c in ranges:
                        if shift:
                            ins = nc.vector.scalar_tensor_tensor(lo(k)[:, a:b], tmp[:, n % B, a:b], shift(k, c),
                                                                 hi(k)[:, a:b].bitcast(F32), ALU.add, ALU.subtract)
                        else:
                            ins = nc.vector.tensor_tensor(lo(k)[:, a:b], tmp[:, n % B, a:b],
                                                          hi(k)[:, a:b].bitcast(F32), ALU.subtract)
                    ins.then_inc(s["lo0"], 1)
                dve.wait_ge(s["lo0"], (nt + 1) // 2)


def project0(e, stream, ahi, alo):
    nc = e.nc
    S = e.scratch
    p = Piece(stream, [0, 1, 2, 3], HEADS0)
    with ExitStack() as ctx:
        sb, sem = e.phase(ctx)
        e.rings(ctx)
        cos, sin = sb("cos0", [128, LAT], F32), sb("sin0", [128, LAT], F32)
        sq = sb("p0_sq", [128, T], F32)
        xg = sb("p0_xg", [128, 2, T], F32)
        xs = sb("p0_xs", [128, 2, LAT], F32)
        rot = sb("p0_rot", [128, 2, T], F32)
        qh = sb("p0_hi", [128, 1, T], F32R)
        ql = sb("p0_lo", [128, 1, T], F32R)
        vt = sb("p0_vt", [128, T], F32)
        vs = sb("p0_vs", [128, TT, 2, VD0], F32R)
        rms = sb("p0_rms", [128, 2 * TT], F32)
        rstd = sb("p0_rstd", [128, 2 * TT], F32)
        wide = sb("p0_wide", [128, 2 * TT * HD0], F32)
        names = ("tab", "chunk", "out", "sum", "xs0", "xs1", "mul", "rot", "rms", "rec", "rstd", "bc", "nrm", "hi", "lo", "st", "turn",
                 "vhi", "vlo", "stv", "stu")
        s = {x: sem("p0_" + x) for x in names}
        ST, TR = 6 * BANK, 7 * BANK
        with nc.Block() as block:
            @block.sync
            def _(sp):
                free_at_start(sp, [(s["out"], 3), (s["sum"], 1), (s["rot"], 2), (s["lo"], 2), (s["rms"], 1), (s["rstd"], 1),
                                   (s["bc"], 1), (s["nrm"], 1), (s["st"], 1), (s["turn"], 1), (s["vlo"], 1),
                                   (s["stv"], 1), (s["stu"], 1)])
                sp.dma_start(cos[:], e.dram["cos0"]).then_inc(s["tab"], 16)
                sp.dma_start(sin[:], e.dram["sin0"]).then_inc(s["tab"], 16)
                with each(sp, HEADS0) as i:
                    for j in range(4):
                        load_block(e, sp, p, i, j, e.dram["w_in"][bass.ds(i * 4 + j, 1), :, :].rearrange("o p f -> p (o f)"))
                e.clear_old(sp)

            @block.gpsimd
            def _(pool):
                def rotate(i, j):
                    pool.wait_ge(s["out"], i * 12 + 3 * j + 3 + 3)
                    pool.wait_ge(s["lo"], i * 2 + j + 1)
                    nc.gpsimd.tensor_tensor(rot[:, j, 0:LAT], xg[:, j, 0:LAT], cos[:], ALU.mult).then_inc(s["mul"], 1)
                    nc.gpsimd.tensor_scalar(rot[:, j, LAT:T], xg[:, j, LAT:T], 1.0, 1.0, ALU.mult, ALU.mult).then_inc(s["mul"], 1)
                    pool.wait_ge(s[f"xs{j}"], i * 64 + 64)
                    nc.gpsimd.tensor_tensor(xs[:, j, :], xs[:, j, :], sin[:], ALU.mult).then_inc(s["mul"], 1)
                    pool.wait_ge(s["mul"], i * 6 + 3 * j + 3)
                    nc.gpsimd.tensor_tensor(rot[:, j, 0:LAT], rot[:, j, 0:LAT], xs[:, j, :], ALU.add).then_inc(s["rot"], 1)

                pool.wait_ge(s["tab"], 32)
                with each(pool, HEADS0) as i:
                    for j in range(3):
                        split_block(e, pool, p, i, j, 1024)
                    rotate(i, 0)
                    split_block(e, pool, p, i, 3, 1024)
                    rotate(i, 1)

            @block.scalar
            def _(act):
                def chunk_ready(i, j, c):
                    if c < 2:
                        act.wait_ge(s["chunk"], i * 8 + 2 * j + c + 1)
                    else:
                        block_used(e, act, p, i, j)

                def evict_qk(i, j):
                    g = e.qg0[:, 0:1] if j == 0 else e.vec[:, VEC["k_g0"][0]:VEC["k_g0"][1]]
                    act.wait_ge(s["sum"], i * 2 + j + 1)
                    act.wait_ge(s["rot"], i * 2 + j + 1)
                    for c, (a, w) in enumerate(CHUNKS):
                        chunk_ready(i, j, c)
                        nc.scalar.activation(sq[:, a:a + w], e.ps[:, a:a + w], ACT.Square)
                        nc.scalar.activation(xg[:, j, a:a + w], e.ps[:, a:a + w], ACT.Copy, scale=g).then_inc(s["out"], 1)
                    act.wait_ge(s["out"], i * 12 + 3 * j + 3 + 3)
                    for a, b in ((0, 32), (32, 0), (64, 96), (96, 64)):
                        act.dma_start(xs[a:a + 32, j, :], xg[b:b + 32, j, 0:LAT]).then_inc(s[f"xs{j}"], 16)

                def root(i, j):
                    act.wait_ge(s["sum"], i * 2 + j + 2)
                    act.wait_ge(s["rstd"], i * 2 + j + 1)
                    nc.scalar.activation(rms[:], e.ps[:, ST:ST + 2 * TT], ACT.Sqrt, bias=e.eps[:, 0:1],
                                         scale=1.0 / HD0).then_inc(s["rms"], 1)

                def plain(i, j):
                    for c, (a, w) in enumerate(CHUNKS):
                        chunk_ready(i, j, c)
                        nc.scalar.activation(vt[:, a:a + w], e.ps[:, a:a + w], ACT.Copy).then_inc(s["out"], 1)

                def high(i, j):
                    act.wait_ge(s["nrm"], i * 2 + j + 2)
                    act.wait_ge(s["st"], i * 128 + 64 * j + 1)
                    nc.scalar.activation(qh[:, 0, :], rot[:, j, :], ACT.Copy).then_inc(s["hi"], 1)

                def store(i, j):
                    act.wait_ge(s["lo"], i * 2 + j + 3)
                    dst = S["q0"] if j == 0 else S["k0"]
                    for m in range(2):
                        for x, buf in enumerate((qh, ql)):
                            act.dma_start(dst[bass.ds(i * 4 + (2 * m + x), 1), :, :].rearrange("o p t -> p (o t)"),
                                          buf[64 * m:64 * m + 64, 0, :].bitcast(F32)).then_inc(s["st"], 16)

                with each(act, HEADS0) as i:
                    evict_qk(i, 0)
                    evict_qk(i, 1)
                    root(i, 0)
                    act.wait_ge(s["stu"], i * 16 + 1)
                    plain(i, 2)
                    root(i, 1)
                    high(i, 0)
                    act.wait_ge(s["stv"], i * 16 + 1)
                    for c, (a, w) in enumerate(CHUNKS):
                        act.wait_ge(s["turn"], i * 3 + c + 2)
                        nc.scalar.activation(vs[:, 4 * c:4 * c + w // 128, 0, :],
                                             e.ps[:, TR:TR + w].rearrange("p (t v) -> p t v", v=128),
                                             ACT.Copy).then_inc(s["vhi"], 1)
                    store(i, 0)
                    act.wait_ge(s["vlo"], i * 3 + 3 + 1)
                    act.dma_start(S["v0"][bass.ds(i, 1), :, :].rearrange("o p f -> p (o f)"),
                                  vs[:].rearrange("p t x v -> p (t x v)").bitcast(F32)).then_inc(s["stv"], 16)
                    plain(i, 3)
                    act.wait_ge(s["out"], i * 12 + 12 + 3)
                    act.dma_start(S["u0"][bass.ds(i, 1), :, :].rearrange("o p t -> p (o t)"), vt[:]).then_inc(s["stu"], 16)
                    high(i, 1)
                    store(i, 1)
                act.wait_ge(s["st"], HEADS0 * 128 + 1)
                act.wait_ge(s["stv"], HEADS0 * 16 + 1)
                act.wait_ge(s["stu"], HEADS0 * 16 + 1)

            @block.tensor
            def _(pe):
                def project(i, j):
                    block_ready(e, pe, p, i, j)
                    for c, (a, w) in enumerate(CHUNKS):
                        pe.wait_ge(s["out"], i * 12 + 3 * j + c + 1)
                        last = products(nc, e.ps[:, a:a + w],
                                        weight_pairs(e, j, 128, lambda k: (ahi[:, k, a:a + w], alo[:, k, a:a + w])))
                        last.then_inc(s["chunk"] if c < 2 else e.w_used, 1)

                def sums(i, j):
                    pe.wait_ge(s["out"], i * 12 + 3 * j + 3 + 3)
                    pe.wait_ge(s["rms"], i * 2 + j + 1)
                    for t in range(TT):
                        last = nc.tensor.matmul(e.ps[:, ST + 2 * t:ST + 2 * t + 2], sq[:, t * 128:(t + 1) * 128],
                                                e.sel[:, 0:2], start=True, stop=True)
                    last.then_inc(s["sum"], 1)

                def spread(i, j):
                    pe.wait_ge(s["rstd"], i * 2 + j + 2)
                    pe.wait_ge(s["nrm"], i * 2 + j + 1)
                    for t in range(TT):
                        last = nc.tensor.transpose(
                            e.ps[:, 3 * BANK + t * 128:3 * BANK + (t + 1) * 128],
                            wide[:, t * 128:(t + 1) * 128],
                            e.ident[:])
                    last.then_inc(s["bc"], 1)

                with each(pe, HEADS0) as i:
                    project(i, 0)
                    project(i, 1)
                    sums(i, 0)
                    project(i, 2)
                    spread(i, 0)
                    sums(i, 1)
                    for c, (a, w) in enumerate(CHUNKS):
                        pe.wait_ge(s["out"], i * 12 + 6 + c + 1 + 3)
                        pe.wait_ge(s["vlo"], i * 3 + c + 1)
                        for t in range(w // 128):
                            last = nc.tensor.transpose(e.ps[:, TR + t * 128:TR + (t + 1) * 128],
                                                       vt[:, a + t * 128:a + (t + 1) * 128], e.ident[:])
                        last.then_inc(s["turn"], 1)
                    project(i, 3)
                    spread(i, 1)

            @block.vector
            def _(dve):
                def recip(i, j):
                    dve.wait_ge(s["rms"], i * 2 + j + 2)
                    nc.vector.reciprocal(rstd[:], rms[:]).then_inc(s["rec"], 1)
                    dve.wait_ge(s["rec"], i * 2 + j + 1)
                    dve.wait_ge(s["bc"], i * 2 + j + 1)
                    nc.vector.tensor_copy(wide[:].rearrange("p (m d) -> p m d", d=HD0),
                                          rstd[:].rearrange("p (m o) -> p m o", o=1).broadcast_to([128, 2 * TT, HD0]))\
                      .then_inc(s["rstd"], 1)

                def normed(i, j):
                    dve.wait_ge(s["bc"], i * 2 + j + 2)
                    dve.wait_ge(s["rot"], i * 2 + j + 3)
                    nc.vector.tensor_tensor(rot[:, j, :], rot[:, j, :], e.ps[:, 3 * BANK:3 * BANK + T],
                                            ALU.mult).then_inc(s["nrm"], 1)

                def low(i, j):
                    dve.wait_ge(s["hi"], i * 2 + j + 1)
                    nc.vector.tensor_tensor(ql[:, 0, :], rot[:, j, :], qh[:, 0, :].bitcast(F32),
                                            ALU.subtract).then_inc(s["lo"], 1)

                with each(dve, HEADS0) as i:
                    recip(i, 0)
                    normed(i, 0)
                    recip(i, 1)
                    low(i, 0)
                    for c, (a, w) in enumerate(CHUNKS):
                        dve.wait_ge(s["vhi"], i * 3 + c + 1)
                        nc.vector.tensor_tensor(vs[:, 4 * c:4 * c + w // 128, 1, :],
                                                e.ps[:, TR:TR + w].rearrange("p (t v) -> p t v", v=128),
                                                vs[:, 4 * c:4 * c + w // 128, 0, :].bitcast(F32),
                                                ALU.subtract).then_inc(s["vlo"], 1)
                    normed(i, 1)
                    low(i, 1)


SLOTS0 = [(0, [-11, -10]), (1, [-9, -8]), (2, [-7, -6]), (3, [-5, -4]), (4, [-3, -2]), (5, [-1, 0]), (6, [1, 2]),
          (7, [3, 4]), (8, [5, 6, 7]), (9, [8, 9, 10])]
TAIL0 = [(None, list(range(11, 22)))]
KEYS0 = [(u, k) for u, n in ((0, 10), (1, 10), (2, 2)) for k in range(n)]


def attention0(e, ot, residual, x_dram):
    nc, S = e.nc, e.scratch
    NQ, NK = 10, 22
    with ExitStack() as ctx:
        sb, sem = e.phase(ctx)
        qs = sb("a0_q", [128, 2, 2, T], F32R)
        ks = sb("a0_k", [128, 2, 2, 2, T], F32R)
        vs = sb("a0_v", [128, 2, TT, 2, VD0], F32R)
        pd = sb("a0_pd", [128, 8, T], F32)
        pc = sb("a0_pc", [128, 2, CTX], F32)
        p1 = e.squares, sb("a0_p1", [128, T], F32)
        pth = sb("a0_pth", [128, 2, BANK], F32R)
        ptl = sb("a0_ptl", [128, 2, BANK], F32R)
        mx = sb("a0_max", [128, 2, 2, 2], F32)
        nb = sb("a0_negmax", [128, 2, 2], F32)
        rs = sb("a0_sums", [128, 2, 2, 2], F32)
        sm = sb("a0_sum", [128, 2, 2], F32)
        rr = sb("a0_recip", [128, 2, 2], F32)
        s = {x: sem("a0_" + x) for x in ("qk0", "qk1", "v0", "v1", "lat", "ctx", "part", "max", "explat", "expctx", "sm", "rec", "scaled", "mul", "comb",
                                         "turn", "hi", "lo", "pv", "out", "x")}
        CB, TB, OB = 4 * BANK, 5 * BANK, 7 * BANK

        def probs(q, a, b):
            return pd[:, q, a:b] if q < 8 else pc[:, q - 8, a - LAT:b - LAT]

        def span(q):
            return (0, T) if q < 8 else (LAT, T)

        def lat_slots(h, q):
            return 8 * h + min(q, 8)

        def unit(k):
            u, kk = KEYS0[k % NK]
            first = {0: 0, 1: 4, 2: 8}[u]
            return u, kk, list(range(first, first + (4 if u < 2 else 2)))

        with nc.Block() as block:
            @block.sync
            def _(sp):
                free_at_start(sp, [(s["explat"], 2), (s["expctx"], 2), (s["comb"], 2), (s["turn"], 1), (s["pv"], 2),
                                   (s["lo"], 2), (s["out"], 1)])
                for h in range(HEADS0):
                    par = h % 2
                    if h >= 2:
                        sp.wait_ge(s["ctx"], NQ * (h - 1))
                    for m in range(2):
                        sp.dma_start(qs[:, par, m, :].bitcast(F32), S["q0"][4 * h + 2 * m:4 * h + 2 * m + 2, :, :]
                                     .rearrange("x d t -> (x d) t")).then_inc(s[f"qk{par}"], 16)
                        for x in range(2):
                            for half in range(2):
                                sp.dma_start(ks[64 * half:64 * half + 64, par, m, x, :].bitcast(F32),
                                             S["k0"][4 * h + 2 * m + x, :, :]).then_inc(s[f"qk{par}"], 16)
                    if h >= 2:
                        sp.wait_ge(s["pv"], NK * (h - 1) + 2)
                    sp.dma_start(vs[:, par, :, :, :].rearrange("p t x v -> p (t x v)").bitcast(F32),
                                 S["v0"][h, :, :]).then_inc(s[f"v{par}"], 16)
                    if h == 1:
                        for k in range(KT):
                            sp.dma_start(residual[:, k, :], x_dram[k, :, :]).then_inc(s["x"], 16)
                sp.wait_ge(s["x"], 16 * KT)
                e.clear_old(sp)


            def walk(step):
                for h in range(HEADS0):
                    for n, (q, keys) in enumerate(SLOTS0):
                        step(h, q, [NK * h + k for k in keys if NK * h + k >= 0])
                for q, keys in TAIL0:
                    step(HEADS0 - 1, None, [NK * (HEADS0 - 1) + k for k in keys])

            @block.tensor
            def _(pe):
                def context(h, q):
                    par, at = h % 2, NQ * h + q
                    if q == 0:
                        pe.wait_ge(s[f"qk{par}"], 160 * (h // 2 + 1))
                    pe.wait_ge(s["expctx"], 2 * at + 2)
                    for m in range(2):
                        st = qs[:, par, m, q * 128:(q + 1) * 128]
                        for x in range(2):
                            last = nc.tensor.matmul(e.ps[:, CB + m * CTX:CB + (m + 1) * CTX], st, ks[:, par, m, x, LAT:T],
                                                    start=x == 0, stop=x == 1)
                    last.then_inc(s["ctx"], 1)

                def latent(h, q, m):
                    par = h % 2
                    pe.wait_ge(s["explat"], 2 * lat_slots(h, q) + m + 1)
                    st = qs[:, par, m, q * 128:(q + 1) * 128]
                    for a in (0, BANK):
                        for x in range(2):
                            last = nc.tensor.matmul(e.ps[:, m * LAT + a:m * LAT + a + BANK], st, ks[:, par, m, x, a:a + BANK],
                                                    start=x == 0, stop=x == 1)
                    last.then_inc(s["lat"], 1)

                def turn(k):
                    u, kk, qts = unit(k)
                    key = kk if u < 2 else kk + 8
                    pe.wait_ge(s["comb"], NQ * (k // NK) + qts[-1] + 1 + 2)
                    pe.wait_ge(s["lo"], k + 1)
                    for x, q in enumerate(qts):
                        last = nc.tensor.transpose(e.ps[:, TB + k % 2 * BANK + x * 128:TB + k % 2 * BANK + (x + 1) * 128],
                                                   probs(q, key * 128, (key + 1) * 128), e.ident[:])
                    last.then_inc(s["turn"], 1)

                def value(k):
                    u, kk, qts = unit(k)
                    h, n = k // NK, 128 * len(qts)
                    key = kk if u < 2 else kk + 8
                    final = kk == (9 if u < 2 else 1)
                    if kk == 0:
                        if u == 0:
                            pe.wait_ge(s[f"v{h % 2}"], 16 * (h // 2 + 1))
                        pe.wait_ge(s["out"], 3 * h + u + 1)
                    pe.wait_ge(s["lo"], k + 3)
                    o = e.ps[:, OB:OB + n]
                    vh, vl = vs[:, h % 2, key, 0, :], vs[:, h % 2, key, 1, :]
                    ph, pl = pth[:, k % 2, 0:n], ptl[:, k % 2, 0:n]
                    nc.tensor.matmul(o, vh, ph, start=kk == 0, stop=False)
                    nc.tensor.matmul(o, vh, pl, start=False, stop=False)
                    nc.tensor.matmul(o, vl, ph, start=False, stop=final).then_inc(s["pv"], 1)

                def step(h, q, keys):
                    if q is not None:
                        context(h, q)
                        if q < 8:
                            latent(h, q, 0)
                            latent(h, q, 1)
                    for k in keys:
                        turn(k)
                        if k >= 1:
                            value(k - 1)

                walk(step)
                value(NK * HEADS0 - 1)

            @block.vector
            def _(dve):
                def lower(k):
                    u, kk, qts = unit(k)
                    n, tb = 128 * len(qts), TB + k % 2 * BANK
                    dve.wait_ge(s["hi"], k + 1)
                    nc.vector.tensor_tensor(ptl[:, k % 2, 0:n], e.ps[:, tb:tb + n], pth[:, k % 2, 0:n].bitcast(F32),
                                            ALU.subtract).then_inc(s["lo"], 1)

                def recip(h, q):
                    at = NQ * h + q
                    x = at % 2
                    dve.wait_ge(s["expctx"], 2 * at + 2 + 2)
                    dve.wait_ge(s["comb"], at + 1)
                    if q < 8:
                        nc.vector.tensor_reduce(sm[:, x, :], rs[:, x, :, :], AX.X, ALU.add).then_inc(s["sm"], 1)
                        dve.wait_ge(s["sm"], lat_slots(h, q) + 1)
                    total = sm[:, x, :] if q < 8 else rs[:, x, :, 1]
                    nc.vector.reciprocal(rr[:, x, :], total).then_inc(s["rec"], 1)

                def top(h, q, m):
                    x, n = (NQ * h + q) % 2, lat_slots(h, q)
                    dve.wait_ge(s["lat"], 2 * n + m + 1)
                    nc.vector.tensor_reduce(mx[:, x, m, 0:1], e.ps[:, m * LAT:(m + 1) * LAT], AX.X, ALU.max).then_inc(s["part"], 1)
                    dve.wait_ge(s["part"], 3 * n + m + 2)
                    nc.vector.tensor_reduce(nb[:, x, m:m + 1], mx[:, x, m, :], AX.X, ALU.max, negate=True).then_inc(s["max"], 1)

                def step(h, q, keys):
                    if q is None:
                        recip(h, NQ - 1)
                        for k in [keys[0] - 1] + keys:
                            lower(k)
                        return
                    at = NQ * h + q
                    x = at % 2
                    if at:
                        recip(*divmod(at - 1, NQ))
                    dve.wait_ge(s["ctx"], at + 1)
                    if q < 8:
                        nc.vector.tensor_reduce(mx[:, x, :, 1], e.ps[:, CB:CB + 2 * CTX].rearrange("p (m k) -> p m k", m=2), AX.X,
                                                ALU.max).then_inc(s["part"], 1)
                    for m in range(2):
                        if q < 8:
                            top(h, q, m)
                        else:
                            nc.vector.tensor_reduce(nb[:, x, m:m + 1], e.ps[:, CB + m * CTX:CB + (m + 1) * CTX], AX.X, ALU.max,
                                                    negate=True).then_inc(s["max"], 1)
                        if m == 0 and keys and keys[0] >= 1:
                            lower(keys[0] - 1)
                    for k in keys[:-1]:
                        lower(k)

                walk(step)

            @block.scalar
            def _(act):
                def high(k):
                    u, kk, qts = unit(k)
                    n, tb = 128 * len(qts), TB + k % 2 * BANK
                    act.wait_ge(s["turn"], k + 2)
                    act.wait_ge(s["pv"], k + 1)
                    nc.scalar.activation(pth[:, k % 2, 0:n], e.ps[:, tb:tb + n], ACT.Copy).then_inc(s["hi"], 1)
                    if kk == 0 and k:
                        copy_out(k - 1)

                def exps(h, q, m):
                    at = NQ * h + q
                    x = at % 2
                    if m == 0 and q in (0, 4, 8) and h:
                        act.wait_ge(s["turn"], NK * (h - 1) + {0: 10, 4: 20, 8: 22}[q] + 1)
                    if m == 1:
                        act.wait_ge(s["comb"], at + 1)
                    act.wait_ge(s["max"], 2 * at + (m if q < 8 else 1) + 1)
                    for part, a, b, src in ((0, 0, LAT, m * LAT), (1, LAT, T, CB + m * CTX)):
                        if part == 0 and q >= 8:
                            continue
                        dst = probs(q, a, b) if m == 0 else p1[x][:, a:b]
                        nc.scalar.activation(dst, e.ps[:, src:src + b - a], ACT.Exp, bias=nb[:, x, m:m + 1],
                                             accum_out=rs[:, x, m, part:part + 1]).then_inc(
                                                 s[("explat", "expctx")[part]], 1)

                def scale(h, q):
                    at = NQ * h + q
                    a, b = span(q)
                    act.wait_ge(s["rec"], at + 1)
                    nc.scalar.activation(probs(q, a, b), probs(q, a, b), ACT.Copy, scale=rr[:, at % 2, 0:1]).then_inc(s["scaled"], 1)

                def step(h, q, keys):
                    if q is None:
                        scale(h, NQ - 1)
                        for k in keys:
                            high(k)
                        return
                    at = NQ * h + q
                    if at:
                        scale(*divmod(at - 1, NQ))
                    exps(h, q, 0)
                    for k in keys[:1]:
                        high(k)
                    exps(h, q, 1)
                    for k in keys[1:]:
                        high(k)

                def copy_out(k):
                    u, kk, qts = unit(k)
                    n, h = 128 * len(qts), k // NK
                    act.wait_ge(s["pv"], k + 1 + 2)
                    nc.scalar.activation(ot[:, h, qts[0] * 128:qts[0] * 128 + n], e.ps[:, OB:OB + n],
                                         ACT.Copy).then_inc(s["out"], 1)

                walk(step)
                copy_out(NK * HEADS0 - 1)
                act.wait_ge(s["out"], 3 * HEADS0 + 1)

            @block.gpsimd
            def _(pool):
                for h in range(HEADS0):
                    for q in range(NQ):
                        at = NQ * h + q
                        a, b = span(q)
                        pool.wait_ge(s["rec"], at + 1)
                        nc.gpsimd.tensor_scalar(p1[at % 2][:, a:b], p1[at % 2][:, a:b], rr[:, at % 2, 1:2],
                                                e.neg_lam[:, 0:1], ALU.mult, ALU.mult).then_inc(s["mul"], 1)
                        pool.wait_ge(s["mul"], at + 1)
                        pool.wait_ge(s["scaled"], at + 1)
                        nc.gpsimd.tensor_tensor(probs(q, a, b), probs(q, a, b), p1[at % 2][:, a:b],
                                                ALU.add).then_inc(s["comb"], 1)


def pool_mixer(e, ahi, alo):
    nc, S = e.nc, e.scratch
    segs = ((PAD, 0, LAT), (3 * PAD + LAT, LAT, CTX))
    W = LAT + CTX + 4 * PAD
    G = len(WINDOWS)
    with ExitStack() as ctx:
        sb, sem = e.phase(ctx)
        u = sb("pm_u", [128, G, W], F32)
        edge = sb("pm_edge", [128, G, 2 * PAD], F32)
        wa, wb = sb("pm_wa", [128, W], F32), sb("pm_wb", [128, W], F32)
        d = sb("pm_d", [128, 2, T], F32)
        pw = sb("pm_w", [128, G, 128], F32)
        s = {x: sem("pm_" + x) for x in ("zero", "weights", "sum", "d", "y", "hi", "lo")}
        arrived = [sem(f"pm_in{g}") for g in range(G)]
        with nc.Block() as block:
            @block.sync
            def _(sp):
                for g in range(G):
                    for at, a, n in segs:
                        sp.dma_start(u[:, g, at:at + n], S["u0"][g, :, a:a + n]).then_inc(arrived[g], 16)
                    if g == 0:
                        sp.dma_start(edge[:], e.dram["pool_edge"]).then_inc(s["weights"], 16)
                        sp.dma_start(pw[:], e.dram["pool_w"]).then_inc(s["weights"], 16)
                e.clear_old(sp)

            @block.gpsimd
            def _(pool):
                for a, b in ((0, PAD), (PAD + LAT, 3 * PAD + LAT), (W - PAD, W)):
                    nc.gpsimd.memset(u[:, :, a:b], 0.0).then_inc(s["zero"], 1)

            def low(dve, g):
                for c, (a, w) in enumerate(CHUNKS):
                    dve.wait_ge(s["hi"], 3 * g + c + 1)
                    x = VEC["pool_scale"][0] + g
                    nc.vector.scalar_tensor_tensor(alo[:, g, a:a + w], e.ps[:, (g % 2) * 3 * BANK + a:(g % 2) * 3 * BANK + a + w],
                                                   e.vec[:, x:x + 1], ahi[:, g, a:a + w].bitcast(F32),
                                                   ALU.mult, ALU.subtract).then_inc(s["lo"], 1)

            @block.vector
            def _(dve):
                dve.wait_ge(s["zero"], 3)
                sums = 0
                for g, w in enumerate(WINDOWS):
                    src, m = u[:, g, :], 1
                    a, b = 0, W
                    dve.wait_ge(arrived[g], 16 * len(segs))
                    if g:
                        dve.wait_ge(s["d"], 2 * g)
                    while m < w:
                        dst = (wa, wb)[m.bit_length() % 2]
                        l, r = (1, 0) if m == 1 else (m // 2, m // 2)
                        a, b = a + l, b - r
                        nc.vector.tensor_tensor(dst[:, a:b], src[:, a - l:b - l], src[:, a + r:b + r],
                                                ALU.add).then_inc(s["sum"], 1)
                        sums += 1
                        dve.wait_ge(s["sum"], sums)
                        src, m = dst, 2 * m
                    if g >= 2:
                        dve.wait_ge(s["y"], 3 * (g - 1))
                    if g == 0:
                        dve.wait_ge(s["weights"], 32)
                    for at, t, n in segs:
                        for x, y in ((at, 0), (at + n - PAD, PAD)):
                            nc.vector.tensor_tensor(src[:, x:x + PAD], src[:, x:x + PAD], edge[:, g, y:y + PAD],
                                                    ALU.mult).then_inc(s["sum"], 1)
                            sums += 1
                    dve.wait_ge(s["sum"], sums)
                    for at, t, n in segs:
                        nc.vector.scalar_tensor_tensor(d[:, g % 2, t:t + n], src[:, at:at + n], 1.0 / w, u[:, g, at:at + n],
                                                       ALU.mult, ALU.subtract).then_inc(s["d"], 1)
                    if g:
                        low(dve, g - 1)
                low(dve, G - 1)
                dve.wait_ge(s["lo"], 3 * G)

            @block.tensor
            def _(pe):
                for g in range(G):
                    pe.wait_ge(s["d"], 2 * g + 2)
                    for c, (a, w) in enumerate(CHUNKS):
                        if g >= 2:
                            pe.wait_ge(s["lo"], 3 * (g - 2) + c + 1)
                        nc.tensor.matmul(e.ps[:, (g % 2) * 3 * BANK + a:(g % 2) * 3 * BANK + a + w], pw[:, g, :],
                                         d[:, g % 2, a:a + w], start=True, stop=True).then_inc(s["y"], 1)

            @block.scalar
            def _(act):
                for g in range(G):
                    x = VEC["pool_scale"][0] + g
                    for c, (a, w) in enumerate(CHUNKS):
                        act.wait_ge(s["y"], 3 * g + c + 1)
                        nc.scalar.activation(ahi[:, g, a:a + w], e.ps[:, (g % 2) * 3 * BANK + a:(g % 2) * 3 * BANK + a + w],
                                             ACT.Copy, scale=e.vec[:, x:x + 1]).then_inc(s["hi"], 1)


def mix_out(e, name, stream, h, acts, n_tok, w_dram, layer):
    nc = e.nc
    chunks = [c for c in CHUNKS if c[0] < n_tok]
    n = len(chunks)
    p = Piece(stream, [0, 1, 2, 3], KT // 4)
    with ExitStack() as ctx:
        sb, sem = e.phase(ctx)
        e.rings(ctx)
        sq = sb(f"{name}_sq", [128, n_tok], F32)
        s = {x: sem(f"{name}_{x}") for x in ("chunk", "out", "sq", "acc")}
        with nc.Block() as block:
            @block.sync
            def _(sp):
                free_at_start(sp, [(s["out"], n)])
                with each(sp, p.iters) as i:
                    for j in range(4):
                        load_block(e, sp, p, i, j, w_dram[bass.ds(i * 4 + j, 1), :, :].rearrange("o p f -> p (o f)"))
                e.clear_old(sp)

            @block.gpsimd
            def _(pool):
                with each(pool, p.iters) as i:
                    for j in range(4):
                        split_block(e, pool, p, i, j, 1024)

            @block.tensor
            def _(pe):
                with each(pe, p.iters) as i:
                    for j in range(4):
                        block_ready(e, pe, p, i, j)
                        for c, (a, w) in enumerate(chunks):
                            pe.wait_ge(s["out"], i * 4 * n + j * n + c + 1)
                            last = products(nc, e.ps[:, a:a + w], weight_pairs(e, j, 128, lambda k: acts(k, a, w)))
                            last.then_inc(s["chunk"] if c < n - 1 else e.w_used, 1)

            @block.scalar
            def _(act):
                with each(act, p.iters) as i:
                    for j in range(4):
                        act.wait_ge(s["out"], i * 4 * n + j * n + 2 * n)
                        act.wait_ge(s["acc"], i * 4 + j + 1)
                        nc.scalar.activation(sq[:, :], h[:, bass.ds(i * 4 + j, 1), 0:n_tok].rearrange("p o t -> p (o t)"),
                                             ACT.Square).then_inc(s["sq"], 1)

            @block.vector
            def _(dve):
                total = e.squares[:, 0:n_tok]
                nc.vector.memset(total, 0.0).then_inc(s["acc"], 1)
                with each(dve, p.iters) as i:
                    for j in range(4):
                        for c, (a, w) in enumerate(chunks):
                            if c < n - 1:
                                dve.wait_ge(s["chunk"], i * 4 * (n - 1) + j * (n - 1) + c + 1)
                            else:
                                block_used(e, dve, p, i, j)
                            m = layer * 48 + 2 * 8 + j
                            nc.vector.scalar_tensor_tensor(
                                h[:, bass.ds(i * 4 + j, 1), a:a + w].rearrange("p o t -> p (o t)"), e.ps[:, a:a + w],
                                e.mod[:, bass.ds(i * 4 + m, 1), int(a >= LAT)],
                                h[:, bass.ds(i * 4 + j, 1), a:a + w].rearrange("p o t -> p (o t)"),
                                ALU.mult, ALU.add).then_inc(s["out"], 1)
                        dve.wait_ge(s["sq"], i * 4 + j + 1)
                        dve.wait_ge(s["acc"], i * 4 + j + 1)
                        nc.vector.tensor_tensor(total, total, sq[:, :], ALU.add).then_inc(s["acc"], 1)
                dve.wait_ge(s["acc"], KT + 1)


def ffn(e, name, stream, h, ahi, alo, n_tok, w_dram, layer, keep_squares=False):
    nc = e.nc
    chunks = [c for c in CHUNKS if c[0] < n_tok]
    n = len(chunks)
    pairs = HT // 2
    first = Piece(stream, [0, 1, 2, 0], 1)
    mid = Piece(stream, [1, 2, 0, 1, 2, 0], pairs - 1)
    end = Piece(stream, [1, 2], 1)
    with ExitStack() as ctx:
        sb, sem = e.phase(ctx)
        e.rings(ctx, 3)
        sg = sb(f"{name}_silu", [128, n_tok], F32)
        hm = sb(f"{name}_hidden", [128, n_tok], F32)
        hh = sb(f"{name}_hhi", [128, 2, n_tok], F32R)
        hl = sb(f"{name}_hlo", [128, 2, n_tok], F32R)
        s = {x: sem(f"{name}_{x}") for x in ("gate", "silu", "up", "prod", "hi", "lo", "down", "out", "sq", "acc")}
        uses = []
        for m in range(0, KT, 2):
            uses += [[(x, a, w, 0)] for x in (m, m + 1) for a, w in chunks[:2]]
            if n == 3:
                uses.append([(m, LAT, CTX, 0), (m + 1, LAT, CTX, CTX)])
        NB = len(uses)

        with nc.Block() as block:
            @block.sync
            def _(sp):
                free_at_start(sp, [(s["silu"], n), (s["prod"], n), (s["out"], 2), (s["down"], 1)])

                def load(p, i, j, at):
                    load_block(e, sp, p, i, j, w_dram[bass.ds(at, 1), :, :].rearrange("o p f -> p (o f)"))

                for j in range(4):
                    load(first, 0, j, j)
                with each(sp, mid.iters) as i:
                    for j in range(6):
                        load(mid, i, j, i * 6 + 4 + j)
                for j in range(2):
                    load(end, 0, j, 3 * HT - 2 + j)
                e.clear_old(sp)

            @block.gpsimd
            def _(pool):
                for j in range(4):
                    split_block(e, pool, first, 0, j, 1024)
                with each(pool, mid.iters) as i:
                    for j in range(6):
                        split_block(e, pool, mid, i, j, 1024)
                for j in range(2):
                    split_block(e, pool, end, 0, j, 1024)

            @block.tensor
            def _(pe):
                def column(p, i, j, at, bank, done, read):
                    block_ready(e, pe, p, i, j)
                    for c, (a, w) in enumerate(chunks):
                        pe.wait_ge(read, at * n + c + 1)
                        last = products(nc, e.ps[:, bank + a:bank + a + w],
                                        weight_pairs(e, p.slots[j], 128, lambda k: (ahi[:, k, a:a + w], alo[:, k, a:a + w])))
                        last.then_inc(done if c < n - 1 else e.w_used, 1)

                def down(p, i, j, pair):
                    block_ready(e, pe, p, i, j + 1)
                    pe.wait_ge(s["lo"], pair * 2 * n + 2 * n)
                    sl = p.slots[j], p.slots[j + 1]
                    for x, parts in enumerate(uses):
                        pe.wait_ge(s["out"], pair * NB + x + 1)
                        for m, a, w, at in parts:
                            o = (6 + x % 2) * BANK + at
                            last = products(nc, e.ps[:, o:o + w],
                                            [(e.whi[:, t, m * 128:(m + 1) * 128], e.wlo[:, t, m * 128:(m + 1) * 128],
                                              hh[:, y, a:a + w], hl[:, y, a:a + w]) for y, t in enumerate(sl)])
                        last.then_inc(s["down"], 1)
                    pe.wait_ge(s["down"], pair * NB + NB + 1)
                    pe.sem_inc(e.w_used, 2)

                column(first, 0, 0, 0, 0, s["gate"], s["silu"])
                column(first, 0, 1, 0, 3 * BANK, s["up"], s["prod"])
                column(first, 0, 2, 1, 0, s["gate"], s["silu"])
                column(first, 0, 3, 1, 3 * BANK, s["up"], s["prod"])
                with each(pe, mid.iters) as i:
                    column(mid, i, 0, i * 2 + 2, 0, s["gate"], s["silu"])
                    down(mid, i, 1, i)
                    column(mid, i, 3, i * 2 + 2, 3 * BANK, s["up"], s["prod"])
                    column(mid, i, 4, i * 2 + 3, 0, s["gate"], s["silu"])
                    column(mid, i, 5, i * 2 + 3, 3 * BANK, s["up"], s["prod"])
                down(end, 0, 0, pairs - 1)

            def done(eng, p, i, j, at, c, which):
                if c < n - 1:
                    eng.wait_ge(s[which], at * (n - 1) + c + 1)
                else:
                    block_used(e, eng, p, i, j)

            @block.scalar
            def _(act):
                def tile(p, i, jg, at, t):
                    for c, (a, w) in enumerate(chunks):
                        done(act, p, i, jg, at, c, "gate")
                        act.wait_ge(s["prod"], at * n + c + 1)
                        nc.scalar.activation(sg[:, a:a + w], e.ps[:, a:a + w], ACT.Silu).then_inc(s["silu"], 1)
                    for c, (a, w) in enumerate(chunks):
                        act.wait_ge(s["prod"], at * n + c + 1 + n)
                        if c == 0:
                            act.wait_ge(s["down"], (at - t) * (NB // 2) + 1)
                        nc.scalar.activation(hh[:, t, a:a + w], hm[:, a:a + w], ACT.Copy).then_inc(s["hi"], 1)

                tile(first, 0, 0, 0, 0)
                tile(first, 0, 2, 1, 1)
                with each(act, mid.iters) as i:
                    tile(mid, i, 0, i * 2 + 2, 0)
                    tile(mid, i, 4, i * 2 + 3, 1)
                for m in range(KT if keep_squares else 0):
                    use = (m // 2 + 1) * (NB // (KT // 2))
                    act.wait_ge(s["out"], (pairs - 1) * NB + use + 2)
                    if m >= 2:
                        act.wait_ge(s["acc"], m - 1)
                    nc.scalar.activation((sg, hm)[m % 2][:, :], h[:, m, 0:n_tok], ACT.Square).then_inc(s["sq"], 1)

            @block.vector
            def _(dve):
                def tile(p, i, ju, at, t):
                    for c, (a, w) in enumerate(chunks):
                        done(dve, p, i, ju, at, c, "up")
                        dve.wait_ge(s["silu"], at * n + c + 1 + n)
                        if (p is mid or at) and c == 0:
                            dve.wait_ge(s["lo"], at * n)
                        nc.vector.tensor_tensor(hm[:, a:a + w], sg[:, a:a + w], e.ps[:, 3 * BANK + a:3 * BANK + a + w],
                                                ALU.mult).then_inc(s["prod"], 1)
                    for c, (a, w) in enumerate(chunks):
                        dve.wait_ge(s["hi"], at * n + c + 1)
                        nc.vector.tensor_tensor(hl[:, t, a:a + w], hm[:, a:a + w], hh[:, t, a:a + w].bitcast(F32),
                                                ALU.subtract).then_inc(s["lo"], 1)

                def add_squares(m):
                    total, sq = e.squares[:, 0:n_tok], (sg, hm)[m % 2][:, :]
                    dve.wait_ge(s["sq"], m + 1)
                    if m == 0:
                        nc.vector.tensor_copy(total, sq).then_inc(s["acc"], 1)
                    else:
                        dve.wait_ge(s["acc"], m)
                        nc.vector.tensor_tensor(total, total, sq, ALU.add).then_inc(s["acc"], 1)

                def add(pair, squares=False):
                    dve.wait_ge(s["out"], pair * NB + 2)
                    for x, parts in enumerate(uses):
                        m = parts[0][0]
                        if squares and m >= 2 and x % (NB // (KT // 2)) in (1, 3):
                            add_squares(m - m % 2 - 2 + x % (NB // (KT // 2)) // 2)
                        dve.wait_ge(s["down"], pair * NB + x + 2)
                        for m, a, w, at in parts:
                            g, o, c = layer * 48 + 5 * 8 + m, (6 + x % 2) * BANK + at, int(a >= LAT)
                            last = nc.vector.scalar_tensor_tensor(h[:, m, a:a + w], e.ps[:, o:o + w], e.mod[:, g, c:c + 1],
                                                                  h[:, m, a:a + w], ALU.mult, ALU.add)
                        last.then_inc(s["out"], 1)

                tile(first, 0, 1, 0, 0)
                tile(first, 0, 3, 1, 1)
                with each(dve, mid.iters) as i:
                    add(i)
                    tile(mid, i, 3, i * 2 + 2, 0)
                    tile(mid, i, 5, i * 2 + 3, 1)
                add(pairs - 1, keep_squares)
                for m in range(KT - 2, KT if keep_squares else 0):
                    add_squares(m)
                dve.wait_ge(s["out"], pairs * NB + 2)
                if keep_squares:
                    dve.wait_ge(s["acc"], KT)


def latents1(e, stream, ahi, alo, cq, ck, kx, ksq, cos, sin):
    nc = e.nc
    p = Piece(stream, [0, 1, 2, 0, 1, 2], 1)
    R = slice(NOPE, QK1)
    with ExitStack() as ctx:
        sb, sem = e.phase(ctx)
        e.rings(ctx, 3)
        xs = e.squares[:, 0:LAT]
        s = {x: sem("l1_" + x) for x in ("tab", "chunk", "out", "xs", "mul")}
        jobs = [(j, c) for j in range(6) for c in range(2 if j < 3 else 3)]
        with nc.Block() as block:
            @block.sync
            def _(sp):
                sp.dma_start(cos[R, :], e.dram["cos1"]).then_inc(s["tab"], 16)
                sp.dma_start(sin[R, :], e.dram["sin1"]).then_inc(s["tab"], 16)
                for j in range(6):
                    load_block(e, sp, p, 0, j, e.dram["w_down1"][j, :, :])
                sp.wait_ge(s["out"], len(jobs))
                for a, b in ((64, 80), (80, 64)):
                    sp.dma_start(xs[a:a + 16, :], kx[b:b + 16, 0:LAT]).then_inc(s["xs"], 16)
                e.clear_old(sp)

            @block.gpsimd
            def _(pool):
                for j in range(6):
                    split_block(e, pool, p, 0, j, 1024)
                pool.wait_ge(s["tab"], 32)
                pool.wait_ge(s["xs"], 32)
                nc.gpsimd.tensor_tensor(kx[R, 0:LAT], kx[R, 0:LAT], cos[R, :], ALU.mult).then_inc(s["mul"], 1)
                nc.gpsimd.tensor_tensor(xs[R, :], xs[R, :], sin[R, :], ALU.mult).then_inc(s["mul"], 1)
                pool.wait_ge(s["mul"], 2)
                nc.gpsimd.tensor_tensor(kx[R, 0:LAT], kx[R, 0:LAT], xs[R, :], ALU.add).then_inc(s["mul"], 1)
                pool.wait_ge(s["mul"], 3)

            @block.tensor
            def _(pe):
                for n, (j, c) in enumerate(jobs):
                    a, w = CHUNKS[c]
                    if c == 0:
                        block_ready(e, pe, p, 0, j)
                    if n >= 6:
                        pe.wait_ge(s["out"], n - 5)
                    last = products(nc, e.ps[:, (n % 6) * BANK:(n % 6) * BANK + w],
                                    weight_pairs(e, p.slots[j], 128, lambda k: (ahi[:, k, a:a + w], alo[:, k, a:a + w])))
                    last.then_inc(s["chunk"] if c < (1 if j < 3 else 2) else e.w_used, 1)

            @block.scalar
            def _(act):
                chunks = 0
                a0, _b0 = VEC["k_g1"]
                for n, (j, c) in enumerate(jobs):
                    a, w = CHUNKS[c]
                    if c < (1 if j < 3 else 2):
                        chunks += 1
                        act.wait_ge(s["chunk"], chunks)
                    else:
                        block_used(e, act, p, 0, j)
                    o = e.ps[:, (n % 6) * BANK:(n % 6) * BANK + w]
                    if j < 3:
                        ins = nc.scalar.activation(cq[:, j, a:a + w], o, ACT.Copy)
                    elif j < 5:
                        ins = nc.scalar.activation(ck[:, j - 3, a:a + w], o, ACT.Copy)
                    else:
                        nc.scalar.activation(ksq[R, a:a + w], o[R, :], ACT.Square)
                        ins = nc.scalar.activation(kx[R, a:a + w], o[R, :], ACT.Copy, scale=e.vec[R, a0:a0 + 1])
                    ins.then_inc(s["out"], 1)
                act.wait_ge(s["out"], len(jobs))


def heads1(e, stream, cqh, cql, ckh, ckl, kx, ksq, cos, sin, cq, ck):
    nc, S = e.nc, e.scratch
    first = Piece(stream, [0, 1], 1)
    mid = Piece(stream, [2, 3, 0, 1], HEADS1 // 2 - 1)
    end = Piece(stream, [2, 3], 1)
    KQ, KK = Q_RANK // 128, KV_RANK // 128
    R = slice(NOPE, QK1)
    QT = LAT // 128
    with ExitStack() as ctx:
        sb, sem = e.phase(ctx)
        e.rings(ctx, 4, KQ * 128)
        qsqs = sb("h1_qsq", [128, LAT], F32), cq[:, 0, :]
        xgs = sb("h1_xg", [128, LAT], F32), cq[:, 1, :]
        xss = sb("h1_xs", [128, LAT], F32), cq[:, 2, :]
        vts = sb("h1_vt0", [64, T], F32), sb("h1_vt1", [64, T], F32)
        kxs, ksqs = (kx, ck[:, 0, :]), (ksq, ck[:, 1, :])
        kn = sb("h1_kn", [128, T], F32)
        vs = sb("h1_vs", [128, TT, 3, VD1], F32R)
        qh, ql = sb("h1_qh", [128, LAT], F32R), sb("h1_ql", [128, LAT], F32R)
        kh, kl = sb("h1_kh", [128, T], F32R), sb("h1_kl", [128, T], F32R)
        rms, rstd = sb("h1_rms", [128, 2, 16], F32), sb("h1_rstd", [128, 2, 16], F32)
        s = {x: sem("h1_" + x) for x in ("chunk", "out", "sum", "xs0", "xs1", "mul", "rot", "rms", "rstd", "bc", "nrm", "hi", "lo",
                                         "turn", "vhi", "vlo", "stq", "stk", "stv", "ones")}
        ST, TR, RB = 6 * BANK, 7 * BANK, 3 * BANK
        VCH = ((0, 8), (8, 2))
        with nc.Block() as block:
            @block.sync
            def _(sp):
                free_at_start(sp, [(s["out"], 3), (s["sum"], 2), (s["rot"], 1), (s["rms"], 2), (s["rstd"], 2), (s["bc"], 2),
                                   (s["nrm"], 1), (s["lo"], 2), (s["turn"], 2), (s["vlo"], 1), (s["stq"], 1), (s["stk"], 1),
                                   (s["stv"], 1)])

                def load(p, i, j, h):
                    for x in range(2):
                        src = (e.dram["w_uq"], e.dram["w_ukv"])[x]
                        load_block(e, sp, p, i, j + x, src[bass.ds(h, 1), :, :].rearrange("o p f -> p (o f)"))
                load(first, 0, 0, 0)
                with each(sp, mid.iters) as i:
                    load(mid, i, 0, i * 2 + 1)
                    load(mid, i, 2, i * 2 + 2)
                load(end, 0, 0, HEADS1 - 1)
                e.clear_old(sp)


            def parity(p, j):
                return 0 if p is end or j == 0 else 1

            def walk(eng, head):
                head(first, 0, 0, 0, None)
                with each(eng, mid.iters) as i:
                    head(mid, i, 0, i * 2 + 1, i * 2)
                    head(mid, i, 2, i * 2 + 2, i * 2 + 1)
                head(end, 0, 0, HEADS1 - 1, HEADS1 - 2)

            @block.gpsimd
            def _(pool):
                def rotate(h, x, p, i, j):
                    xg, xs = xgs[x], xss[x]
                    pool.wait_ge(e.split_done, p.number(i, j + 1) + 1 + RING)
                    pool.wait_ge(s[f"xs{x}"], (h - x) * 16 + 32)
                    nc.gpsimd.tensor_tensor(xg[R, :], xg[R, :], cos[R, :], ALU.mult).then_inc(s["mul"], 1)
                    pool.wait_ge(s["mul"], h * 2 + 1)
                    nc.gpsimd.tensor_tensor(xs[R, :], xs[R, :], sin[R, :], ALU.mult).then_inc(s["mul"], 1)
                    pool.wait_ge(s["mul"], h * 2 + 2)
                    nc.gpsimd.tensor_tensor(xg[R, :], xg[R, :], xs[R, :], ALU.add).then_inc(s["rot"], 1)
                    pool.wait_ge(s["rot"], h + 2)

                def head(p, i, j, m, h):
                    split_block(e, pool, p, i, j, KQ * 128)
                    split_block(e, pool, p, i, j + 1, KK * 128)
                    if h is not None:
                        rotate(h, parity(p, j), p, i, j)

                walk(pool, head)
                rotate(HEADS1 - 1, 1, end, 0, 0)

            @block.tensor
            def _(pe):
                def project_q(p, i, j, m):
                    block_ready(e, pe, p, i, j)
                    for c in range(2):
                        a, w = CHUNKS[c]
                        pe.wait_ge(s["out"], m * 5 + c + 1)
                        last = products(nc, e.ps[:, a:a + w],
                                        weight_pairs(e, p.slots[j], 128, lambda k: (cqh[:, k, a:a + w], cql[:, k, a:a + w]), KQ))
                        last.then_inc(s["chunk"] if c < 1 else e.w_used, 1)

                def project_kv(p, i, j, m):
                    block_ready(e, pe, p, i, j)
                    for c, (a, w) in enumerate(CHUNKS):
                        pe.wait_ge(s["out"], m * 5 + 3 + (c + 1 if c < 2 else 0))
                        last = products(nc, e.ps[:, a:a + w],
                                        weight_pairs(e, p.slots[j], 128, lambda k: (ckh[:, k, a:a + w], ckl[:, k, a:a + w]), KK))
                        last.then_inc(s["chunk"] if c < 2 else e.w_used, 1)

                def sums(h, x, j):
                    src, tt = ((qsqs[x], QT), (ksqs[x], TT))[j]
                    pe.wait_ge(s["out"], h * 5 + (2, 5)[j] + 3)
                    if j == 0:
                        pe.wait_ge(s["rms"], h * 2 + 2)
                    for t in range(tt):
                        last = nc.tensor.matmul(e.ps[:, ST + j * 16 + t:ST + j * 16 + t + 1], src[0:QK1, t * 128:(t + 1) * 128],
                                                e.sel[0:QK1, 2:3], start=True, stop=True)
                    last.then_inc(s["sum"], 1)

                def turn(h, x, c):
                    t0, n = VCH[c]
                    pe.wait_ge(s["out"], h * 5 + 5 + 3)
                    pe.wait_ge(s["vlo"], h * 2 + c + 1)
                    settle_pe(e, TR)
                    for t in range(n):
                        last = nc.tensor.transpose(e.ps[:, TR + t * 64:TR + (t + 1) * 64],
                                                   vts[x][:, (t0 + t) * 128:(t0 + t + 1) * 128], e.ident[0:64, 0:64])
                    last.then_inc(s["turn"], 1)

                def spread(h, j):
                    pe.wait_ge(s["rstd"], h * 2 + j + 3)
                    pe.wait_ge(s["nrm"], h * 2 + j + 1)
                    for t in range((QT, TT)[j]):
                        last = nc.tensor.transpose(e.ps[:, RB + t * 128:RB + (t + 1) * 128],
                                                   rstd[:, j, t:t + 1].broadcast_to([128, 128]), e.ident[:])
                    last.then_inc(s["bc"], 1)

                def start(h, x):
                    sums(h, x, 0)
                    sums(h, x, 1)
                    turn(h, x, 0)

                def finish(h, x):
                    spread(h, 0)
                    turn(h, x, 1)
                    spread(h, 1)

                def head(p, i, j, m, h):
                    x = parity(p, j)
                    project_q(p, i, j, m)
                    if h is not None:
                        start(h, x)
                    project_kv(p, i, j + 1, m)
                    if h is not None:
                        finish(h, x)

                walk(pe, head)
                start(HEADS1 - 1, 1)
                finish(HEADS1 - 1, 1)

            @block.scalar
            def _(act):
                kg = VEC["k_g1"][0]

                def copy_q(p, i, j, m, x):
                    if m is not None:
                        act.wait_ge(s["sum"], m * 2 - 1)
                        act.wait_ge(s["lo"], m * 2 - 1)
                    for c in range(2):
                        a, w = CHUNKS[c]
                        if c < 1:
                            act.wait_ge(s["chunk"], (0 if m is None else m) * 3 + 1)
                        else:
                            block_used(e, act, p, i, j)
                        nc.scalar.activation(qsqs[x][0:QK1, a:a + w], e.ps[0:QK1, a:a + w], ACT.Square)
                        nc.scalar.activation(xgs[x][0:QK1, a:a + w], e.ps[0:QK1, a:a + w], ACT.Copy,
                                             scale=e.qg1[0:QK1, :]).then_inc(s["out"], 1)
                    act.wait_ge(s["out"], (0 if m is None else m) * 5 + 2 + 3)
                    if m is not None:
                        act.wait_ge(s["rot"], m)
                    for a, b in ((64, 80), (80, 64)):
                        act.dma_start(xss[x][a:a + 16, :], xgs[x][b:b + 16, :]).then_inc(s[f"xs{x}"], 16)

                def copy_kv(p, i, j, m, x):
                    if m is not None:
                        act.wait_ge(s["sum"], m * 2)
                        act.wait_ge(s["nrm"], m * 2 - 1)
                        act.wait_ge(s["turn"], m * 2)
                    for c, (a, w) in enumerate(CHUNKS):
                        if c < 2:
                            act.wait_ge(s["chunk"], (0 if m is None else m) * 3 + 2 + c)
                        else:
                            block_used(e, act, p, i, j)
                        nc.scalar.activation(ksqs[x][0:NOPE, a:a + w], e.ps[0:NOPE, a:a + w], ACT.Square)
                        nc.scalar.activation(kxs[x][0:NOPE, a:a + w], e.ps[0:NOPE, a:a + w], ACT.Copy,
                                             scale=e.vec[0:NOPE, kg:kg + 1])
                        nc.scalar.activation(vts[x][:, a:a + w], e.ps[64:128, a:a + w], ACT.Copy).then_inc(s["out"], 1)

                def root(h, j):
                    tt = (QT, TT)[j]
                    act.wait_ge(s["sum"], h * 2 + 4)
                    act.wait_ge(s["rstd"], h * 2 + j + 1)
                    nc.scalar.activation(rms[:, j, 0:tt], e.ps[:, ST + j * 16:ST + j * 16 + tt], ACT.Sqrt, bias=e.eps[:, 0:1],
                                         scale=1.0 / QK1).then_inc(s["rms"], 1)

                def high(h, x, j):
                    act.wait_ge(s["nrm"], h * 2 + j + 2)
                    act.wait_ge(s["stq" if j == 0 else "stk"], h * 32 + 1)
                    dst, src = ((qh, xgs[x]), (kh, kn))[j]
                    nc.scalar.activation(dst[0:QK1, :], src[0:QK1, :], ACT.Copy).then_inc(s["hi"], 1)

                def vhigh(h, c):
                    t0, n = VCH[c]
                    act.wait_ge(s["turn"], h * 2 + c + 3)
                    nc.scalar.activation(vs[:, t0:t0 + n, 0, :], e.ps[:, TR:TR + n * 64].rearrange("p (t v) -> p t v", v=64),
                                         ACT.Copy).then_inc(s["vhi"], 1)

                def store(h, j):
                    act.wait_ge(s["lo"], h * 2 + j + 3)
                    st, dst, bufs = ((s["stq"], S["q1"], (qh, ql)), (s["stk"], S["k1"], (kh, kl)))[j]
                    for x, buf in enumerate(bufs):
                        act.dma_start(dst[bass.ds(h * 2 + x, 1), :, :].rearrange("o p t -> p (o t)"),
                                      buf[0:QK1, :].bitcast(F32)).then_inc(st, 16)

                def start(h, x):
                    root(h, 0)
                    root(h, 1)
                    act.wait_ge(s["stv"], h * 16 + 1)
                    vhigh(h, 0)

                def finish(h, x):
                    high(h, x, 0)
                    vhigh(h, 1)
                    high(h, x, 1)
                    store(h, 0)
                    act.wait_ge(s["vlo"], h * 2 + 2 + 1)
                    act.dma_start(S["v1"][bass.ds(h, 1), :, :].rearrange("o p f -> p (o f)"),
                                  vs[:].rearrange("p t x v -> p (t x v)").bitcast(F32)).then_inc(s["stv"], 16)
                    store(h, 1)

                def head(p, i, j, m, h):
                    x = parity(p, j) if h is not None else 1
                    copy_q(p, i, j, None if h is None else m, 1 - x)
                    if h is not None:
                        start(h, x)
                    copy_kv(p, i, j + 1, None if h is None else m, 1 - x)
                    if h is not None:
                        finish(h, x)

                act.wait_ge(s["ones"], TT + 2)
                walk(act, head)
                start(HEADS1 - 1, 1)
                finish(HEADS1 - 1, 1)
                act.wait_ge(s["stq"], HEADS1 * 32 + 1)
                act.wait_ge(s["stk"], HEADS1 * 32 + 1)
                act.wait_ge(s["stv"], HEADS1 * 16 + 1)

            @block.vector
            def _(dve):
                def recip(h, j):
                    tt = (QT, TT)[j]
                    dve.wait_ge(s["rms"], h * 2 + j + 3)
                    dve.wait_ge(s["bc"], h * 2 + j + 1)
                    nc.vector.reciprocal(rstd[:, j, 0:tt], rms[:, j, 0:tt]).then_inc(s["rstd"], 1)

                def normed(h, x, j):
                    dve.wait_ge(s["bc"], h * 2 + j + 3)
                    if j == 0:
                        dve.wait_ge(s["rot"], h + 2)
                    else:
                        dve.wait_ge(s["lo"], h * 2 + 2)
                    dst, src, n = ((xgs[x], xgs[x], LAT), (kn, kxs[x], T))[j]
                    nc.vector.tensor_tensor(dst[0:QK1, :], src[0:QK1, :], e.ps[0:QK1, RB:RB + n],
                                            ALU.mult).then_inc(s["nrm"], 1)

                def low(h, x, j):
                    dve.wait_ge(s["hi"], h * 2 + j + 1)
                    dst, src, hi = ((ql, xgs[x], qh), (kl, kn, kh))[j]
                    nc.vector.tensor_tensor(dst[0:QK1, :], src[0:QK1, :], hi[0:QK1, :].bitcast(F32),
                                            ALU.subtract).then_inc(s["lo"], 1)

                def vlow(h, c):
                    t0, n = VCH[c]
                    dve.wait_ge(s["vhi"], h * 2 + c + 1)
                    nc.vector.tensor_tensor(vs[:, t0:t0 + n, 2, :], e.ps[:, TR:TR + n * 64].rearrange("p (t v) -> p t v", v=64),
                                            vs[:, t0:t0 + n, 0, :].bitcast(F32), ALU.subtract).then_inc(s["vlo"], 1)

                def finish(h, x):
                    recip(h, 0)
                    recip(h, 1)
                    vlow(h, 0)
                    normed(h, x, 0)
                    normed(h, x, 1)
                    low(h, x, 0)
                    vlow(h, 1)
                    low(h, x, 1)

                for t in range(TT):
                    nc.vector.tensor_copy(vs[:, t, 1, :], e.sel[:, 2:2 + VD1]).then_inc(s["ones"], 1)
                nc.vector.tensor_copy(kxs[1][R, :], kx[R, :]).then_inc(s["ones"], 1)
                nc.vector.tensor_copy(ksqs[1][R, :], ksq[R, :]).then_inc(s["ones"], 1)
                with each(dve, HEADS1 // 2) as i:
                    finish(i * 2, 0)
                    finish(i * 2 + 1, 1)


def attention1(e, oh, ol):
    nc, S = e.nc, e.scratch
    with ExitStack() as ctx:
        sb, sem = e.phase(ctx)
        qs = sb("a1_q", [128, 2, 2, LAT], F32R)
        ks = sb("a1_k", [128, 2, 2, T], F32R)
        vs = sb("a1_v", [128, 2, TT, 3 * VD1], F32R)
        p = sb("a1_p", [128, 2, LAT], F32)
        ph, pl = sb("a1_ph", [128, 2, LAT], F32R), sb("a1_pl", [128, 2, LAT], F32R)
        raw, rec, whole = sb("a1_raw", [128, LAT], F32), sb("a1_recip", [64, LAT], F32), sb("a1_whole", [128, LAT], F32)
        top, neg = sb("a1_top", [128, QT, 3], F32), sb("a1_negmax", [128, QT], F32R)
        ident = sb("a1_ident", [128, 128], F32R)
        s = {x: sem("a1_" + x) for x in ("qk0", "qk1", "v0", "v1", "rows", "aux", "auxr", "neg", "st", "exp", "pl",
                                         "pv", "raw", "rec", "whole", "ohi", "out")}
        OB, XB = 4 * BANK, 6 * BANK
        KS, MAXES = TT, 20
        AUX = MAXES + 2
        UNITS = {1: range(0, 3), 2: range(3, 6), 3: range(6, 9), 4: range(9, 12), 5: range(12, 15), 6: range(15, 18),
                 7: range(18, 20), 8: range(20, 22)}

        def unit(u):
            return (u // 2, u % 2) if u < 16 else (2 * (u - 16), 2)

        def walk(eng, step):
            def head(h, par, tiles, more=True):
                for kk in range(KS):
                    step(h, par, tiles, kk, more)
            head(0, 0, (0, None))
            with each(eng, HEADS1 // 2 - 1) as i:
                head(i * 2 + 1, 1, (i, i))
                head(i * 2 + 2, 0, (i + 1, i))
            head(HEADS1 - 1, 1, (HEADS1 // 2 - 1,) * 2, False)

        with nc.Block() as block:
            @block.sync
            def _(sp):
                free_at_start(sp, [(s["auxr"], 2), (s["exp"], 8), (s["pv"], 2), (s["raw"], 1),
                                   (s["whole"], 1), (s["ohi"], 1), (s["out"], 1), (s["neg"], 1)])

                def load(h, par, first):
                    if not first:
                        sp.wait_ge(s["st"], h * 2 * KS - 2 * KS)
                    for x in range(2):
                        sp.dma_start(qs[0:QK1, par, x, :].bitcast(F32), S["q1"][bass.ds(h * 2 + x, 1), :, :]
                                     .rearrange("o p t -> p (o t)")).then_inc(s[f"qk{par}"], 16)
                        sp.dma_start(ks[0:QK1, par, x, :].bitcast(F32), S["k1"][bass.ds(h * 2 + x, 1), :, :]
                                     .rearrange("o p t -> p (o t)")).then_inc(s[f"qk{par}"], 16)
                    if not first:
                        sp.wait_ge(s["pv"], h * KS - KS + 2)
                    sp.dma_start(vs[:, par, :, :].rearrange("p t v -> p (t v)").bitcast(F32),
                                 S["v1"][bass.ds(h, 1), :, :].rearrange("o p f -> p (o f)")).then_inc(s[f"v{par}"], 16)

                load(0, 0, True)
                load(1, 1, True)
                with each(sp, HEADS1 // 2 - 1) as i:
                    load(i * 2 + 2, 0, False)
                    load(i * 2 + 3, 1, False)
                e.clear_old(sp)

            @block.tensor
            def _(pe):
                def aux(g, par, u):
                    bank = XB + (u % 2) * BANK
                    if u == 0:
                        pe.wait_ge(s[f"qk{par}"], (g - par) * 32 + 64)
                    if u == MAXES:
                        pe.wait_ge(s["neg"], g + 2)
                    pe.wait_ge(s["auxr"], g * AUX + u + 1)
                    if u >= MAXES:
                        for x in range(4):
                            q = (u - MAXES) * 4 + x
                            last = nc.tensor.matmul(e.ps[:, bank + x * 128:bank + (x + 1) * 128],
                                                    neg[:, q:q + 1].broadcast_to([128, 128]), ident[:], start=True, stop=True)
                    elif u < 16:
                        q, c = unit(u)
                        last = nc.tensor.matmul(e.ps[:, bank:bank + BANK], qs[0:QK1, par, 0, q * 128:(q + 1) * 128],
                                                ks[0:QK1, par, 0, c * BANK:(c + 1) * BANK], start=True, stop=True)
                    else:
                        for x in range(2):
                            q = unit(u)[0] + x
                            last = nc.tensor.matmul(e.ps[:, bank + x * CTX:bank + (x + 1) * CTX],
                                                    qs[0:QK1, par, 0, q * 128:(q + 1) * 128],
                                                    ks[0:QK1, par, 0, LAT:T], start=True, stop=True)
                    last.then_inc(s["aux"], 1)

                def scores(h, par, kk, x):
                    k, a = h * KS + kk, x * BANK
                    if kk == 0 and x == 0:
                        pe.wait_ge(s["auxr"], h * AUX + AUX + 2)
                    kh_, kl_ = (ks[0:QK1 + 1, par, x, kk * 128:(kk + 1) * 128] for x in range(2))
                    qh_, ql_ = (qs[0:QK1 + 1, par, y, a:a + BANK] for y in range(2))
                    pe.wait_ge(s["exp"], k * 4 + 2 * x + 2)
                    o = (kk % 2) * 2 * BANK + a
                    products(nc, e.ps[:, o:o + BANK], [(kh_, kl_, qh_, ql_)]).then_inc(s["st"], 1)

                def value(h, par, kk, x):
                    k, a = h * KS + kk, x * BANK
                    if kk == 0 and x == 0:
                        pe.wait_ge(s[f"v{par}"], (h - par) * 8 + 16)
                        pe.wait_ge(s["raw"], h + 1)
                    vone, vl = vs[:, par, kk, 0:2 * VD1], vs[:, par, kk, 2 * VD1:3 * VD1]
                    pe.wait_ge(s["pl"], k * 2 + x + 1)
                    h_, l_ = ph[:, kk % 2, a:a + BANK], pl[:, kk % 2, a:a + BANK]
                    o = OB + a
                    nc.tensor.matmul(e.ps[:, o:o + BANK], vone, h_, start=kk == 0, stop=False)
                    nc.tensor.matmul(e.ps[0:VD1, o:o + BANK], vl, h_, start=False, stop=False)
                    last = nc.tensor.matmul(e.ps[:, o:o + BANK], vone, l_, start=False, stop=kk == KS - 1)
                    if x == 1:
                        last.then_inc(s["pv"], 1)

                def step(h, par, tiles, kk, more):
                    units = list(UNITS.get(kk, ())) if more else []
                    for x in range(2):
                        if kk < KS - 1:
                            scores(h, par, kk + 1, x)
                        elif more:
                            scores(h + 1, 1 - par, 0, x)
                        for u in units[x:x + 1]:
                            aux(h + 1, 1 - par, u)
                    value(h, par, kk, 0)
                    for u in units[2:]:
                        aux(h + 1, 1 - par, u)
                    value(h, par, kk, 1)

                pe.wait_ge(s["rows"], 8)
                for u in range(AUX):
                    aux(0, 0, u)
                for x in range(2):
                    scores(0, 0, 0, x)
                walk(pe, step)

            def place(buf, par, tile):
                return buf[64 * par:64 * par + 64, bass.ds(tile, 1), 0:LAT].rearrange("p o t -> p (o t)")

            @block.vector
            def _(dve):
                def read_aux(g, par, u):
                    bank = XB + (u % 2) * BANK
                    dve.wait_ge(s["aux"], g * AUX + u + 1)
                    if u >= MAXES:
                        x = u - MAXES
                        nc.vector.tensor_copy(qs[QK1:QK1 + 1, par, 0, x * BANK:(x + 1) * BANK],
                                              e.ps[QK1:QK1 + 1, bank:bank + BANK]).then_inc(s["auxr"], 1)
                        return
                    q, c = unit(u)
                    if u < 16:
                        nc.vector.tensor_reduce(top[:, q:q + 1, c], e.ps[:, bank:bank + BANK], AX.X, ALU.max).then_inc(s["auxr"], 1)
                    else:
                        nc.vector.tensor_reduce(top[:, q:q + 2, c], e.ps[:, bank:bank + BANK].rearrange("p (q k) -> p q k", k=CTX),
                                                AX.X, ALU.max).then_inc(s["auxr"], 1)
                    if u == MAXES - 1:
                        dve.wait_ge(s["auxr"], g * AUX + MAXES + 2)
                        nc.vector.tensor_reduce(neg[:, :], top[:, :, :], AX.X, ALU.max, negate=True).then_inc(s["neg"], 1)

                def step(h, par, tiles, kk, more):
                    if tiles[1] is not None and kk < QT:
                        recip(h - 1, kk)
                    if tiles[1] is not None and kk == QT:
                        divide(h - 1, 1 - par)
                    if more:
                        for u in UNITS.get(kk, ()):
                            if u == 0:
                                dve.wait_ge(s["neg"], h + 2)
                            read_aux(h + 1, 1 - par, u)
                    if kk == QT + 1 and tiles[1] is not None:
                        low(h - 1, 1 - par, tiles[1])

                def recip(g, x):
                    if x == 0:
                        dve.wait_ge(s["raw"], g + 2)
                        dve.wait_ge(s["whole"], g + 1)
                    nc.vector.reciprocal(rec[:, x * 128:(x + 1) * 128], raw[64:128, x * 128:(x + 1) * 128]).then_inc(s["rec"], 1)

                def divide(g, par):
                    dve.wait_ge(s["rec"], g * QT + QT)
                    dve.wait_ge(s["out"], g + 1)
                    nc.vector.tensor_tensor(whole[64 * par:64 * par + 64, :], raw[0:64, :], rec[:, :],
                                            ALU.mult).then_inc(s["whole"], 1)

                def low(g, par, tile):
                    dve.wait_ge(s["ohi"], g + 2)
                    nc.vector.tensor_tensor(place(ol, par, tile), whole[64 * par:64 * par + 64, :],
                                            place(oh, par, tile).bitcast(F32), ALU.subtract).then_inc(s["out"], 1)

                zeros = p[:].rearrange("p x t -> p (x t)")[QK1:QK1 + 1, :]
                nc.vector.memset(zeros, 0.0).then_inc(s["rows"], 1)
                nc.vector.tensor_copy(ident[:], e.ident[:]).then_inc(s["rows"], 1)
                dve.wait_ge(s["rows"], 2)
                for par in range(2):
                    nc.vector.tensor_scalar(ks[QK1:QK1 + 1, par, 0, :], zeros[:, 0:T], 1.0, None, ALU.add).then_inc(s["rows"], 1)
                    nc.vector.tensor_copy(ks[QK1:QK1 + 1, par, 1, :], zeros[:, 0:T]).then_inc(s["rows"], 1)
                    nc.vector.tensor_copy(qs[QK1:QK1 + 1, par, 1, :], zeros[:, 0:LAT]).then_inc(s["rows"], 1)
                for u in range(AUX):
                    read_aux(0, 0, u)
                walk(dve, step)
                for x in range(QT):
                    recip(HEADS1 - 1, x)
                divide(HEADS1 - 1, 1)
                low(HEADS1 - 1, 1, HEADS1 // 2 - 1)
                dve.wait_ge(s["out"], HEADS1 + 1)

            @block.scalar
            def _(act):
                def step(h, par, tiles, kk, more):
                    k = h * KS + kk
                    for x in range(2):
                        act.wait_ge(s["st"], k * 2 + x + 1)
                        if x == 0:
                            act.wait_ge(s["pv"], k + 1)
                        c = slice(x * BANK, (x + 1) * BANK)
                        b = e.ps[:, (kk % 2) * 2 * BANK + x * BANK:(kk % 2) * 2 * BANK + (x + 1) * BANK]
                        nc.scalar.activation(ph[:, kk % 2, c], b, ACT.Exp).then_inc(s["exp"], 1)
                        nc.scalar.activation(p[:, kk % 2, c], b, ACT.Exp).then_inc(s["exp"], 1)
                    if kk == 0 and tiles[1] is not None:
                        copy_out(h - 1)
                    if kk == QT and tiles[1] is not None:
                        high(h - 1, 1 - par, tiles[1])

                def copy_out(g):
                    act.wait_ge(s["pv"], g * KS + KS + 2)
                    act.wait_ge(s["whole"], g + 1)
                    nc.scalar.activation(raw[:, :], e.ps[:, OB:OB + LAT], ACT.Copy).then_inc(s["raw"], 1)

                def high(g, par, tile):
                    act.wait_ge(s["whole"], g + 2)
                    nc.scalar.activation(place(oh, par, tile), whole[64 * par:64 * par + 64, :], ACT.Copy).then_inc(s["ohi"], 1)

                walk(act, step)
                copy_out(HEADS1 - 1)
                high(HEADS1 - 1, 1, HEADS1 // 2 - 1)

            @block.gpsimd
            def _(pool):
                def step(h, par, tiles, kk, more):
                    k = h * KS + kk
                    for x in range(2):
                        pool.wait_ge(s["exp"], k * 4 + 2 * x + 2 + 8)
                        c = slice(x * BANK, (x + 1) * BANK)
                        nc.gpsimd.tensor_tensor(pl[:, kk % 2, c], p[:, kk % 2, c], ph[:, kk % 2, c].bitcast(F32),
                                                ALU.subtract).then_inc(s["pl"], 1)

                walk(pool, step)


def program(nc, dram, out):
    e = Env(nc, dram)
    stream = Stream()
    top = ExitStack()

    with top:
        sb = e.sbuf(top)

        def sem(name):
            return top.enter_context(nc.semaphore(name))

        e.scratch = {n: nc.dram_tensor("scratch_" + n, shape, dt, kind="Internal").ap() for n, shape, dt in (
            ("q0", (HEADS0 * 4, HD0, T), F32), ("k0", (HEADS0 * 4, HD0, T), F32),
            ("v0", (HEADS0, 128, TT * 2 * VD0), F32), ("u0", (HEADS0, 128, T), F32),
            ("q1", (HEADS1 * 2, QK1, LAT), F32), ("k1", (HEADS1 * 2, QK1, T), F32),
            ("v1", (HEADS1, 128, TT * 3 * VD1), F32))}
        e.ps = top.enter_context(nc.psum_tensor("ps", [128, 8 * BANK], F32))
        e.vec, e.ident, e.sel = sb("vec", [128, NVEC], F32), sb("ident", [128, 128], F32), sb("sel", [128, 130], F32)
        e.eps, e.neg_lam, e.subln = sb("eps", [128, 1], F32), sb("neg_lam", [128, 1], F32), sb("subln", [128, 1], F32)
        e.qg0, e.qg1 = sb("qg0", [128, 1], F32), sb("qg1", [128, 1], F32)
        e.spare = sb("spare", [128, 1], F32)
        e.mod = sb("mod", [128, DEPTH * 48, 2], F32)
        e.squares = sb("squares", [128, T], F32)
        e.gain = sb("gain", [128, 4, KT, 2], F32)
        e.consts, stored = sem("consts"), sem("stored")
        e.raw_full = [sem(f"raw_full{i}") for i in range(4)]
        e.split_hi, e.split_done, e.w_used = sem("split_hi"), sem("split_done"), sem("w_used")

        def rings(ctx, slots=4, width=1024, split=True):
            new = e.sbuf(ctx)
            e.raw = new(f"raw{stream.n}", [128, slots, width], F32)
            if split:
                e.whi = new(f"whi{stream.n}", [128, slots, width], F32R)
                e.wlo = new(f"wlo{stream.n}", [128, slots, width], F32R)

        e.rings = rings
        with ExitStack() as c:
            rings(c, 12, split=False)
            modulation(e, dram["mod_w"])
        with nc.Block() as block:
            @block.gpsimd
            def _(pool):
                pool.sem_inc(e.split_done, RING)

            @block.tensor
            def _(pe):
                pe.sem_inc(e.w_used, RING)

        def acts(c, name, n_tok=T, tiles=KT):
            return (e.sbuf(c)(name + "_hi", [128, tiles, n_tok], F32R), e.sbuf(c)(name + "_lo", [128, tiles, n_tok], F32R))

        def adaln(name, h, hi, lo, which, layer, part, n_tok=T, load=None):
            ranges = RANGES if n_tok == T else RANGES[:1]
            norm(e, name, lambda k: h[:, k, 0:n_tok], [list(range(KT))], D,
                 lambda k, c: e.gain[:, which, k, c:c + 1],
                 lambda k, c: e.mod[:, layer * 48 + part * 8 + k, c:c + 1],
                 lambda k: hi[:, k, :], lambda k: lo[:, k, :], ranges, load, summed=load is None)

        with ExitStack() as c:
            hi, lo = acts(c, "mix0")
            with ExitStack() as c2:
                x = e.sbuf(c2)("x0", [128, KT, T], F32)
                adaln("norm_mix0", x, hi, lo, 0, 0, 0, load=lambda k: dram["x"][k, :, :])
            project0(e, stream, hi, lo)
        h = sb("residual", [128, KT, T], F32)
        with ExitStack() as c:
            ot = e.sbuf(c)("ot", [128, HEADS0, T], F32)
            attention0(e, ot, h, dram["x"])
            hi, lo = acts(c, "mixed0")
            norm(e, "norm_sub", lambda k: ot[:, k, :], [[k] for k in range(HEADS0)], VD0,
                 lambda k, c_: e.subln[:, 0:1], None, lambda k: hi[:, 4 + k, :], lambda k: lo[:, 4 + k, :], ((0, T, 0),))
            pool_mixer(e, hi, lo)

            mix_out(e, "out0", stream, h, lambda k, a, w: (hi[:, k, a:a + w], lo[:, k, a:a + w]), T, dram["w_out0"], 0)
        with ExitStack() as c:
            hi, lo = acts(c, "ffn0_in")
            adaln("norm_ffn0", h, hi, lo, 1, 0, 3)
            ffn(e, "ffn0", stream, h, hi, lo, T, dram["w_ffn"][0], 0, keep_squares=True)

        with ExitStack() as c:
            new = e.sbuf(c)
            kx, ksq = new("kx", [128, T], F32), new("ksq", [128, T], F32)
            cos, sin = new("cos1", [128, LAT], F32), new("sin1", [128, LAT], F32)
            cq, ck = new("cq", [128, Q_RANK // 128, LAT], F32), new("ck", [128, KV_RANK // 128, T], F32)
            with ExitStack() as c2:
                hi, lo = acts(c2, "mix1")
                adaln("norm_mix1", h, hi, lo, 2, 1, 0)
                latents1(e, stream, hi, lo, cq, ck, kx, ksq, cos, sin)
            cqh, cql = acts(c, "cq", LAT, Q_RANK // 128)
            ckh, ckl = acts(c, "ck", T, KV_RANK // 128)
            qg, kg = VEC["qlat_g"][0], VEC["kvlat_g"][0]
            norm(e, "norm_q", lambda k: cq[:, k, :], [[0, 1, 2]], Q_RANK, lambda k, c_: e.vec[:, qg + k:qg + k + 1], None,
                 lambda k: cqh[:, k, :], lambda k: cql[:, k, :], ((0, LAT, 0),))
            norm(e, "norm_kv", lambda k: ck[:, k, :], [[0, 1]], KV_RANK, lambda k, c_: e.vec[:, kg + k:kg + k + 1], None,
                 lambda k: ckh[:, k, :], lambda k: ckl[:, k, :], ((0, T, 0),))
            heads1(e, stream, cqh, cql, ckh, ckl, kx, ksq, cos, sin, cq, ck)
        with ExitStack() as c:
            oh, ol = acts(c, "o1", LAT)
            attention1(e, oh, ol)
            mix_out(e, "out1", stream, h, lambda k, a, w: (oh[:, k, a:a + w], ol[:, k, a:a + w]), LAT, dram["w_out1"], 1)
        with ExitStack() as c:
            hi, lo = acts(c, "ffn1_in", LAT)
            adaln("norm_ffn1", h, hi, lo, 3, 1, 3, LAT)
            ffn(e, "ffn1", stream, h, hi, lo, LAT, dram["w_ffn"][1], 1)
        with nc.Block() as block:
            @block.sync
            def _(sp):
                for k in range(KT):
                    sp.dma_start(out[k, :, :], h[:, k, 0:LAT]).then_inc(stored, 16)
                sp.wait_ge(stored, 16 * KT)


def _rope(rot_dim):
    n = rot_dim // 4
    freqs = (10000.0 ** (-np.arange(n, dtype=np.float32) / n)).astype(np.float32)
    t = np.arange(LAT)
    row, col = (t // GRID_W).astype(np.float32), (t % GRID_W).astype(np.float32)
    ang = np.concatenate([freqs[:, None] * row, freqs[:, None] * col], axis=0)
    cos, sin = np.cos(ang), np.sin(ang)
    return np.concatenate([cos, cos]).astype(np.float32), np.concatenate([-sin, sin]).astype(np.float32)


def _edges():
    out = np.ones((len(WINDOWS), 2 * PAD), np.float32)
    for g, w in enumerate(WINDOWS):
        for t in range(PAD):
            out[g, t] = w / (t + w // 2 - max(t - w // 2, 0))
            left = PAD - t
            out[g, PAD + t] = w / (w // 2 + min(w // 2, left))
    return out


def _columns(w, cols=128):
    k, m = w.shape
    return np.ascontiguousarray(w.reshape(k // 128, 128, m // cols, cols).transpose(2, 1, 0, 3).reshape(m // cols, 128, -1))


def _feature_major(v):
    return v.reshape(-1, 128).T


def _lay_out(i):
    A = {k: np.asarray(v) for k, v in i.items()}
    d = {}
    d["x"] = np.ascontiguousarray(np.concatenate([A["x"][0], A["ctx"][0]]).T.reshape(KT, 128, T))
    d["mod_w"] = np.ascontiguousarray(
        A["mod_w"].reshape(DEPTH, 4, 2, 128, 12, 512).transpose(0, 4, 1, 3, 2, 5).reshape(DEPTH * 48, 128, 1024))
    w = A["ab_w_in"][0]
    cols = [c for h in range(HEADS0) for c in (512 + 128 * h, 1024 + 128 * h, 1536 + 128 * h, 128 * h)]
    d["w_in"] = np.concatenate([_columns(w[:, c:c + 128]) for c in cols])
    d["w_out0"], d["w_out1"] = _columns(A["ab_w_out"][0]), _columns(A["mla_w_out"][0])
    order = [("g", 0), ("u", 0), ("g", 1), ("u", 1)]
    for p in range(1, HT // 2):
        order += [("g", 2 * p), ("d", 2 * p - 2), ("d", 2 * p - 1), ("u", 2 * p), ("g", 2 * p + 1), ("u", 2 * p + 1)]
    order += [("d", HT - 2), ("d", HT - 1)]
    ffn_w = []
    for layer in range(DEPTH):
        parts = {"g": _columns(A["ffn_w_gate"][layer]), "u": _columns(A["ffn_w_up"][layer]),
                 "d": A["ffn_w_down"][layer].reshape(HT, 128, D)}
        ffn_w.append(np.stack([parts[k][m] for k, m in order]))
    d["w_ffn"] = np.stack(ffn_w)
    kv = A["mla_w_dkv"][0]
    d["w_down1"] = np.concatenate([_columns(A["mla_w_dq"][0]), _columns(kv[:, :KV_RANK]),
                                   _columns(np.tile(kv[:, KV_RANK:], (1, 4)))])
    uq = A["mla_w_uq"][0].reshape(Q_RANK, HEADS1, QK1)
    uq = np.concatenate([uq, uq[:, :, :128 - QK1]], axis=2).reshape(Q_RANK, HEADS1 * 128)
    d["w_uq"], d["w_ukv"] = _columns(uq), _columns(A["mla_w_ukv"][0])
    d["pool_w"] = np.ascontiguousarray(A["pool_w"][0].transpose(1, 0, 2))
    d["pool_edge"] = np.ascontiguousarray(np.broadcast_to(_edges(), (128, len(WINDOWS), 2 * PAD)))
    vec = np.zeros((128, NVEC), np.float32)

    def put(name, v):
        a, b = VEC[name]
        vec[:v.shape[0], a:b] = v

    put("cond", np.stack([A["c"][0].reshape(KT, 128), A["c_ctx"].reshape(KT, 128)], axis=1).reshape(2 * KT, 128).T)
    for name, key in (("mod_b", "mod_b"), ("mix_g", "norm_mix_g"), ("ffn_g", "norm_ffn_g"), ("pool_scale", "pool_scale"),
                      ("subln_g", "diff_subln_g"), ("qlat_g", "mla_q_lat_g"), ("kvlat_g", "mla_kv_lat_g")):
        put(name, _feature_major(A[key]))
    for name, key in (("q_g0", "diff_q_norm_g"), ("k_g0", "diff_k_norm_g")):
        put(name, np.tile(A[key][0], 2)[:, None])
    for name, key in (("q_g1", "mla_q_norm_g"), ("k_g1", "mla_k_norm_g")):
        put(name, A[key][0][:, None])
    put("lam", np.stack([A["diff_lam_q1"][0], A["diff_lam_q2"][0], A["diff_lam_k1"][0], A["diff_lam_k2"][0]], axis=1))
    d["vec"] = vec
    d["ident"] = np.eye(128, dtype=np.float32)
    sel = np.ones((128, 130), np.float32)
    sel[64:, 0] = 0
    sel[:64, 1] = 0
    d["sel"] = sel
    c0, s0 = _rope(HD0)
    d["cos0"], d["sin0"] = np.concatenate([c0, c0]), np.concatenate([s0, s0])
    d["cos1"], d["sin1"] = _rope(ROPE)
    return {k: np.ascontiguousarray(v) for k, v in d.items()}


def kernel(**inputs):
    import concourse.bacc as bacc
    from concourse.bass_utils import run_bass_kernel_spmd

    nc = bacc.Bacc("TRN2", target_bir_lowering=False, num_devices=1)
    arrays = _lay_out(inputs)
    dram = {k: nc.dram_tensor("in_" + k, v.shape, mybir.dt.from_np(v.dtype), kind="ExternalInput").ap()
            for k, v in arrays.items()}
    out = nc.dram_tensor("out_0", (KT, 128, LAT), F32, kind="ExternalOutput").ap()
    program(nc, dram, out)
    r = run_bass_kernel_spmd(nc, [{"in_" + k: v for k, v in arrays.items()}], core_ids=[0])
    return np.ascontiguousarray(r.results[0]["out_0"].reshape(1, D, LAT).transpose(0, 2, 1))
```
